# Optimizing a Trainium2 kernel written in Bass

```python
import math
import jax, jax.numpy as jnp
from jax import lax
import numpy as np

D_MODEL = 1024
BATCH = 1
SEQ = 512
DEPTH = 2

BLOCK_Q = 128
EPS = 1e-6
SB_HEADS = 8
SB_HEAD_DIM = 64
MLA_HEADS = 8
MLA_Q_LORA = 256
MLA_KV_LORA = 128
MLA_NOPE = 64
MLA_ROPE = 32
MLA_V = 64
ROPE_THETA = 10000.0
DSA_HEADS = 8
DSA_HEAD_DIM = 64
IDX_HEADS = 8
IDX_DIM = 32
TOPK_MAX = 256
REL_BUCKETS = 32
REL_MAX_DIST = 128
N_BRANCH = 3
BRANCH_WIDTH = 512
IN_SIZES = (SB_HEADS * SB_HEAD_DIM, SB_HEADS * SB_HEAD_DIM, SB_HEADS * SB_HEAD_DIM,
            MLA_Q_LORA, MLA_KV_LORA, MLA_ROPE,
            DSA_HEADS * DSA_HEAD_DIM, DSA_HEAD_DIM, DSA_HEAD_DIM,
            IDX_HEADS * IDX_DIM, IDX_DIM, IDX_HEADS,
            BRANCH_WIDTH, BRANCH_WIDTH, BRANCH_WIDTH,
            N_BRANCH * D_MODEL)
D_IN = sum(IN_SIZES)

kernel_name = 'hybrid_sb_mla_dsa_gated_block'

def _split_points(sizes):
    pts, acc = [], 0
    for s in sizes[:-1]:
        acc += s
        pts.append(acc)
    return pts

def rms_norm(x, g):
    xf = x.astype(jnp.float32)
    y = xf * lax.rsqrt(jnp.mean(xf * xf, axis=-1, keepdims=True) + EPS)
    return (y * g.astype(jnp.float32)).astype(x.dtype)

def apply_rope(x, cos, sin):
    xf = x.astype(jnp.float32)
    x1, x2 = xf[..., : MLA_ROPE // 2], xf[..., MLA_ROPE // 2:]
    return jnp.concatenate([x1 * cos - x2 * sin, x2 * cos + x1 * sin], axis=-1).astype(x.dtype)

def t5_bucket(dist):
    n = jnp.maximum(dist, 0)
    exact = REL_BUCKETS // 2
    nf = jnp.maximum(n, 1).astype(jnp.float32)
    large = exact + (jnp.log(nf / exact) / math.log(REL_MAX_DIST / exact)
                     * (REL_BUCKETS - exact)).astype(jnp.int32)
    large = jnp.minimum(large, REL_BUCKETS - 1)
    return jnp.where(n < exact, n, large)

def stick_breaking_attention(q, k, v):
    B, S, H, dh = q.shape
    kf, vf = k.astype(jnp.float32), v.astype(jnp.float32)
    key_idx = jnp.arange(S)

    def block(n):
        start = n * BLOCK_Q
        qb = lax.dynamic_slice_in_dim(q, start, BLOCK_Q, axis=1).astype(jnp.float32)
        z = jnp.einsum('bqhd,bkhd->bhqk', qb, kf) * (dh ** -0.5)
        q_idx = start + jnp.arange(BLOCK_Q)
        mask = key_idx[None, :] < q_idx[:, None]
        log_1m = jnp.where(mask, jax.nn.log_sigmoid(-z), 0.0)
        csum = jnp.cumsum(log_1m, axis=-1)
        log_a = jax.nn.log_sigmoid(z) + csum[..., -1:] - csum
        a = jnp.where(mask, jnp.exp(log_a), 0.0)
        return jnp.einsum('bhqk,bkhd->bqhd', a, vf)

    out = lax.map(block, jnp.arange(S // BLOCK_Q))
    return out.transpose(1, 0, 2, 3, 4).reshape(B, S, H * dh).astype(q.dtype)

def causal_softmax_attention(q, k, v, scale):
    B, S, H, _ = q.shape
    dv = v.shape[-1]
    kf, vf = k.astype(jnp.float32), v.astype(jnp.float32)
    key_idx = jnp.arange(S)

    def block(n):
        start = n * BLOCK_Q
        qb = lax.dynamic_slice_in_dim(q, start, BLOCK_Q, axis=1).astype(jnp.float32)
        logits = jnp.einsum('bqhd,bkhd->bhqk', qb, kf) * scale
        q_idx = start + jnp.arange(BLOCK_Q)
        mask = key_idx[None, :] <= q_idx[:, None]
        p = jax.nn.softmax(jnp.where(mask, logits, -jnp.inf), axis=-1)
        return jnp.einsum('bhqk,bkhd->bqhd', p, vf)

    out = lax.map(block, jnp.arange(S // BLOCK_Q))
    return out.transpose(1, 0, 2, 3, 4).reshape(B, S, H * dv).astype(q.dtype)

_gather_rows = jax.vmap(lambda a, i: a[i])

def dsa_attention(q, k, v, ix_q, ix_k, ix_w, positions, rel_bias):
    B, S, H, dh = q.shape
    topk = min(TOPK_MAX, S // 4)
    ixk = ix_k.astype(jnp.float32)
    key_idx = jnp.arange(S)

    def block(n):
        start = n * BLOCK_Q
        q_idx = start + jnp.arange(BLOCK_Q)
        iq = lax.dynamic_slice_in_dim(ix_q, start, BLOCK_Q, axis=1).astype(jnp.float32)
        iw = lax.dynamic_slice_in_dim(ix_w, start, BLOCK_Q, axis=1).astype(jnp.float32)
        s_idx = jax.nn.relu(jnp.einsum('bqhd,bkd->bqhk', iq, ixk) * (IDX_DIM ** -0.5))
        score = jnp.einsum('bqh,bqhk->bqk', iw * (IDX_HEADS ** -0.5), s_idx)
        score = jnp.where(key_idx[None, None, :] <= q_idx[None, :, None], score, -jnp.inf)
        _, sel = lax.top_k(score, topk)
        valid = sel <= q_idx[None, :, None]
        kg = _gather_rows(k, sel).astype(jnp.float32)
        vg = _gather_rows(v, sel).astype(jnp.float32)
        qb = lax.dynamic_slice_in_dim(q, start, BLOCK_Q, axis=1).astype(jnp.float32)
        logits = jnp.einsum('bqhd,bqkd->bqhk', qb, kg) * (dh ** -0.5)
        pq = lax.dynamic_slice_in_dim(positions, start, BLOCK_Q, axis=1)
        pk = _gather_rows(positions, sel)
        bias = rel_bias.astype(jnp.float32)[t5_bucket(pq[:, :, None] - pk)]
        logits = logits + jnp.moveaxis(bias, -1, 2)
        p = jax.nn.softmax(jnp.where(valid[:, :, None, :], logits, -jnp.inf), axis=-1)
        return jnp.einsum('bqhk,bqkd->bqhd', p, vg)

    out = lax.map(block, jnp.arange(S // BLOCK_Q))
    return out.transpose(1, 0, 2, 3, 4).reshape(B, S, H * dh).astype(q.dtype)

def hybrid_layer(x, positions, cos, sin, norm_g, w_in, q_norm_g, kv_norm_g, w_uq, w_ukv,
                 mla_q_g, mla_k_g, dsa_q_g, dsa_k_g, rel_bias, gate_b, w_branch, w_out):
    B, S, D = x.shape
    h = rms_norm(x, norm_g)
    proj = h @ w_in
    (sa_q, sa_k, sa_v, c_q, c_kv, k_pe, ds_q, ds_k, ds_v, ix_q, ix_k, ix_w,
     z_a, z_b, z_c, g) = jnp.split(proj, _split_points(IN_SIZES), axis=-1)

    y_a = stick_breaking_attention(sa_q.reshape(B, S, SB_HEADS, SB_HEAD_DIM),
                                   sa_k.reshape(B, S, SB_HEADS, SB_HEAD_DIM),
                                   sa_v.reshape(B, S, SB_HEADS, SB_HEAD_DIM))

    q_b = (rms_norm(c_q, q_norm_g) @ w_uq).reshape(B, S, MLA_HEADS, MLA_NOPE + MLA_ROPE)
    kv_b = (rms_norm(c_kv, kv_norm_g) @ w_ukv).reshape(B, S, MLA_HEADS, MLA_NOPE + MLA_V)
    k_nope, v_b = kv_b[..., :MLA_NOPE], kv_b[..., MLA_NOPE:]
    k_b = jnp.concatenate([k_nope, jnp.broadcast_to(k_pe[:, :, None, :], (B, S, MLA_HEADS, MLA_ROPE))], axis=-1)
    q_b = rms_norm(q_b, mla_q_g)
    k_b = rms_norm(k_b, mla_k_g)
    c4, s4 = cos[:, :, None, :], sin[:, :, None, :]
    q_b = jnp.concatenate([q_b[..., :MLA_NOPE], apply_rope(q_b[..., MLA_NOPE:], c4, s4)], axis=-1)
    k_b = jnp.concatenate([k_b[..., :MLA_NOPE], apply_rope(k_b[..., MLA_NOPE:], c4, s4)], axis=-1)
    y_b = causal_softmax_attention(q_b, k_b, v_b, (MLA_NOPE + MLA_ROPE) ** -0.5)

    y_c = dsa_attention(rms_norm(ds_q.reshape(B, S, DSA_HEADS, DSA_HEAD_DIM), dsa_q_g),
                        rms_norm(ds_k, dsa_k_g), ds_v,
                        ix_q.reshape(B, S, IDX_HEADS, IDX_DIM), ix_k, ix_w,
                        positions, rel_bias)

    branches = jnp.stack([y_a * jax.nn.silu(z_a), y_b * jax.nn.silu(z_b), y_c * jax.nn.silu(z_c)], axis=2)
    up = jnp.einsum('bsnc,ncd->bsnd', branches, w_branch)
    gates = jax.nn.sigmoid(g.reshape(B, S, N_BRANCH, D) + gate_b)
    merged = jnp.sum(gates * up, axis=2)
    return x + merged @ w_out

def setup_inputs(seed: int = 0) -> dict:
    key = jax.random.key(seed)
    ks = jax.random.split(key, 17)
    f32 = jnp.float32

    def nrm(k, shape, scale):
        return jax.random.normal(k, shape, f32) * scale

    def gain(k, shape):
        return 1.0 + 0.02 * jax.random.normal(k, shape, f32)

    x = jax.random.normal(ks[0], (BATCH, SEQ, D_MODEL), f32)
    offset = jax.random.randint(ks[1], (BATCH, 1), 0, 1024, dtype=jnp.int32)
    positions = offset + jnp.arange(SEQ, dtype=jnp.int32)[None, :]
    return {
        'x': x,
        'positions': positions,
        'norm_g': gain(ks[2], (DEPTH, D_MODEL)),
        'w_in': nrm(ks[3], (DEPTH, D_MODEL, D_IN), D_MODEL ** -0.5),
        'mla_q_norm_g': gain(ks[4], (DEPTH, MLA_Q_LORA)),
        'mla_kv_norm_g': gain(ks[5], (DEPTH, MLA_KV_LORA)),
        'mla_w_uq': nrm(ks[6], (DEPTH, MLA_Q_LORA, MLA_HEADS * (MLA_NOPE + MLA_ROPE)), MLA_Q_LORA ** -0.5),
        'mla_w_ukv': nrm(ks[7], (DEPTH, MLA_KV_LORA, MLA_HEADS * (MLA_NOPE + MLA_V)), MLA_KV_LORA ** -0.5),
        'mla_q_g': gain(ks[8], (DEPTH, MLA_NOPE + MLA_ROPE)),
        'mla_k_g': gain(ks[9], (DEPTH, MLA_NOPE + MLA_ROPE)),
        'dsa_q_g': gain(ks[10], (DEPTH, DSA_HEAD_DIM)),
        'dsa_k_g': gain(ks[11], (DEPTH, DSA_HEAD_DIM)),
        'rel_bias': nrm(ks[12], (REL_BUCKETS, DSA_HEADS), 0.5),
        'gate_b': nrm(ks[13], (DEPTH, N_BRANCH, D_MODEL), 0.02),
        'w_branch': nrm(ks[14], (DEPTH, N_BRANCH, BRANCH_WIDTH, D_MODEL), BRANCH_WIDTH ** -0.5),
        'w_out': nrm(ks[15], (DEPTH, D_MODEL, D_MODEL), D_MODEL ** -0.5),
    }

def reference(x, positions, norm_g, w_in, mla_q_norm_g, mla_kv_norm_g, mla_w_uq, mla_w_ukv,
              mla_q_g, mla_k_g, dsa_q_g, dsa_k_g, rel_bias, gate_b, w_branch, w_out):
    half = MLA_ROPE // 2
    inv_freq = ROPE_THETA ** (-(jnp.arange(half, dtype=jnp.float32) * 2.0) / MLA_ROPE)
    ang = positions.astype(jnp.float32)[..., None] * inv_freq
    cos, sin = jnp.cos(ang), jnp.sin(ang)
    for l in range(DEPTH):
        x = hybrid_layer(x, positions, cos, sin, norm_g[l], w_in[l], mla_q_norm_g[l], mla_kv_norm_g[l],
                         mla_w_uq[l], mla_w_ukv[l], mla_q_g[l], mla_k_g[l], dsa_q_g[l], dsa_k_g[l],
                         rel_bias, gate_b[l], w_branch[l], w_out[l])
    return x


_drawn_inputs = setup_inputs


def setup_inputs(seed=0):
    import zlib

    import numpy as np

    out = dict(_drawn_inputs(seed))
    spreads = {}
    factors = {'norm_g': 3.956,
     'mla_q_norm_g': 8.0,
     'mla_kv_norm_g': 8.0,
     'mla_q_g': 8.0,
     'mla_k_g': 8.0,
     'dsa_q_g': 8.0,
     'dsa_k_g': 8.0,
     'gate_b': 8.0}
    for name, (base, spread) in spreads.items():
        noise = np.random.default_rng([zlib.crc32(name.encode()), seed]).standard_normal(out[name].shape)
        drawn = base * np.exp(spread * noise) if base else spread * noise
        out[name] = __import__('jax').numpy.asarray(drawn.astype(out[name].dtype))
    for name, factor in factors.items():
        out[name] = (out[name] * factor).astype(out[name].dtype)
    return out
```

```python
from contextlib import ExitStack
import math

import numpy as np
import concourse.bass as bass
from concourse import mybir

ALU = mybir.AluOpType
ACT = mybir.ActivationFunctionType
F32 = mybir.dt.float32
F32R = mybir.dt.float32r
BF16 = mybir.dt.bfloat16
I32 = mybir.dt.int32
AX_X = mybir.AxisListType.X

P = 128
D = 1024
S = 512
DEPTH = 2
KT = D // P
ST = S // P
HEADS = 8
HD = 64
NOPE, ROPE = 64, 32
QK = NOPE + ROPE
Q_LORA, KV_LORA = 256, 128
IDX_DIM = 32
TOPK = min(256, S // 4)
BUCKETS, MAX_DIST = 32, 128
BW = 512
EPS = 1e-6
THETA = 10000.0

SIZES = dict(sa_q=512, sa_k=512, sa_v=512, c_q=Q_LORA, c_kv=KV_LORA, k_pe=ROPE, ds_q=512, ds_k=HD,
             ds_v=HD, ix_q=HEADS * IDX_DIM, ix_k=IDX_DIM, ix_w=HEADS, z=3 * BW, g=3 * D)
COL = {}
_at = 0
for _n, _w in SIZES.items():
    COL[_n] = _at
    _at += _w
D_IN = _at

SLAB = 264
MASKED = -1e30
TAKEN = -3e38
CLIP = 30.0
STICK_SCALE = HD ** -0.5
OFF = [P * (t * (t + 1) // 2) for t in range(ST)]
SOFF = [P * (t * ST - t * (t - 1) // 2) for t in range(ST)]
STRIPS = P * ST * (ST + 1) // 2


def bucket_thresholds():
    exact = BUCKETS // 2
    n = np.arange(1, 4 * MAX_DIST)
    large = exact + (np.log(n / exact) / math.log(MAX_DIST / exact) * (BUCKETS - exact) + 1e-9).astype(int)
    bucket = np.where(n < exact, n, np.minimum(large, BUCKETS - 1))
    least = [-float(2 ** 26)] + [float(n[np.argmax(bucket >= b)]) for b in range(1, BUCKETS)]
    return np.array(least, np.float32)


def constants():
    r = np.arange(P)
    eye = np.eye(P)
    suffix = np.where(r[:, None] >= r[None, :], -1.0 / STICK_SCALE, 0.0)
    all_later = np.full((P, P), -1.0 / STICK_SCALE)
    ones = np.ones((P, P))
    per_head = (r[:, None] // HD == r[None, :] // HD) * 1.0
    first_qk = (r[:, None] < QK) * np.ones((P, P))
    big_eye = eye * -MASKED
    causal = np.where(r[None, :] > r[:, None], -1.0, 0.0)
    mats = np.concatenate([eye, suffix, all_later, ones, per_head, first_qk, big_eye, causal], 1)
    half = ROPE // 2
    inv = (np.float32(THETA) ** (-(np.arange(half, dtype=np.float32) * np.float32(2.0)) / np.float32(ROPE))).astype(np.float32)
    cols = np.zeros((P, 4))
    cols[:, 0] = np.tile(bucket_thresholds(), P // BUCKETS)
    cols[64:, 1] = np.tile(inv, 4)
    cols[64:96, 2] = math.pi / 2
    cols[64:, 3] = 1.0
    cols[96:112, 3] = -1.0
    return np.concatenate([mats, cols], 1).astype(np.float32)


N_MATS = 8


def slab_plan():
    plan = ["small", "ix_q", "sa_q0", "sa_q1", "sa_k0", "sa_k1", "sa_v0", "sa_v1",
            "ckv_dsk", "ds_q0", "ds_q1", "c_q", "uq", "ukv"]
    for n in range(3):
        plan += [f"z{n}_0", f"z{n}_1"]
        for half in range(2):
            plan += [f"g{n}_{2 * half}", f"g{n}_{2 * half + 1}", f"up{n}_{half}"]
    plan += [f"out{c}_{j}" for c in range(2) for j in range(2)]
    return plan


SLABS = slab_plan()
NS = len(SLABS)
SLAB_NO = {n: i for i, n in enumerate(SLABS)}
RAW, RING = 2, 2
N_GAINS = 7


class Signal:

    def __init__(self, sem, name, known):
        self.sem, self.name, self.known = sem, name, known
        self.n, self.events = 0, {}

    def tick(self, *event, by=1):
        self.n += by
        self.events[event] = self.n
        return self.sem, by

    def at(self, *event):
        return self.sem, self.known[self.name][event] if self.name in self.known else 1


def build(nc, x, positions, norm_g, w_in, q_norm_g, kv_norm_g, w_uq, w_ukv, mla_q_g, mla_k_g,
          dsa_q_g, dsa_k_g, rel_bias, gate_b, w_branch, w_out, consts, out, bias_dram, known):
    signals = {}
    ctx = ExitStack()
    with ctx:
        def signal(name):
            signals[name] = Signal(ctx.enter_context(nc.semaphore(name)), name, known)
            return signals[name]

        arena_bytes = 207 * 1024
        arena_base = (nc.sbuf_base + 63) // 64 * 64
        ctx.enter_context(nc.sbuf_tensor("arena", [P, arena_bytes // 4], F32))
        base = arena_base
        cursor = [base]

        def place(name, shape, dt, at=None):
            size = int(np.prod(shape[1:])) * (2 if dt == BF16 else 4)
            size = (size + 31) // 32 * 32
            if at is None:
                at = cursor[0]
                cursor[0] += size
                assert cursor[0] <= base + arena_bytes, (name, cursor[0] - base)
            return nc.alloc_sbuf_tensor_at(name, shape, dt, offset=at), at + size

        def sb(name, shape, dt=F32):
            return place(name, shape, dt)[0]

        mats = sb("mats", [P, N_MATS * P + 4])
        eye, suffix, all_later, ones, per_head, first_qk, big_eye_f, causal_f = (
            mats[:, i * P:(i + 1) * P] for i in range(N_MATS))
        thr, inv_freq, phase, sign = (mats[:, N_MATS * P + i:N_MATS * P + i + 1] for i in range(4))
        big_eye = sb("big_eye", [P, P], BF16)
        causal = sb("causal", [P, P], BF16)
        cos_sin = sb("cos_sin", [P, S])
        k_rope = sb("k_rope", [P, S])
        k_sq = sb("k_sq", [P, S])
        gain = sb("gain", [P, N_GAINS + 3 * KT])
        gains = sb("gains", [P, DEPTH, N_GAINS + 3 * KT])
        stat = sb("stat", [P, 64])
        x_sb = sb("x_sb", [P, ST, D])
        h_hi = sb("h_hi", [P, KT, S], F32R)
        h_lo = sb("h_lo", [P, KT, S], F32R)
        raw = sb("raw", [P, RAW, KT * SLAB])
        w_hi = sb("w_hi", [P, RING, KT * SLAB], F32R)
        w_lo = sb("w_lo", [P, RING, KT * SLAB], F32R)
        y_at = cursor[0]
        y = sb("y", [P, 8, S])
        xn = place("xn", [P, 2, D], F32, y_at)[0]
        x_sq = place("x_sq", [P, D], F32, y_at + 8192)[0]
        u_at = cursor[0]
        ds_q = sb("ds_q", [P, 4, S])
        ds_k = sb("ds_k", [P, S])
        ds_v = sb("ds_v", [P, ST, HD])
        ix_w = sb("ix_w", [P, ST, HEADS])
        score = sb("score", [P, STRIPS])
        chosen = sb("chosen", [P, STRIPS], BF16)
        sa_q_at = cursor[0]
        sa_q = sb("sa_q", [P, 4, S])
        sa_k = sb("sa_k", [P, 4, S])
        sa_v_at = cursor[0]
        sa_v = sb("sa_v", [P, ST, BW])
        q_head, at = place("q_head", [P, 2, S], F32, sa_q_at)
        k_head, at = place("k_head", [P, 2, S], F32, at)
        q_sq, at = place("q_sq", [P, S], F32, at)
        q_rs, at = place("q_rs", [P, S], F32, at)
        k_rs, at = place("k_rs", [P, S], F32, at)
        q_rot, at = place("q_rot", [P, S], F32, at)
        v_b = place("v_b", [P, ST, BW], F32, sa_v_at)[0]
        y_dsa = place("y_dsa", [P, 4, S], F32, sa_v_at)[0]
        lora_at = cursor[0]
        cq_hi = sb("cq_hi", [P, 2, S], F32R)
        cq_lo = sb("cq_lo", [P, 2, S], F32R)
        ckv_hi = sb("ckv_hi", [P, S], F32R)
        ckv_lo = sb("ckv_lo", [P, S], F32R)
        bias = place("bias", [P, 2, STRIPS], F32, lora_at)[0]
        norm_sq = sb("norm_sq", [P, S])
        norm_rs = sb("norm_rs", [P, S])
        norm_out = sb("norm_out", [P, S])
        cq_out = [norm_out, norm_sq]
        tmp_at = cursor[0]
        soft, at = place("soft", [P, 3, S], F32, tmp_at)
        sp, at = place("sp", [P, 2, STRIPS], F32, at)
        gain_row = place("gain_row", [P, D], F32, at)[0]
        stick_a, end = place("stick_a", [P, 2, S], F32, at)
        probs, at = place("probs", [P, 3, S], F32, tmp_at)
        probs_t, at = place("probs_t", [P, 3, S], F32, at)
        ix_q, at = place("ix_q_sb", [P, 2, S], F32, tmp_at)
        ix_k, at = place("ix_k_sb", [P, S], F32, at)
        ix_relu, at = place("ix_relu", [P, 3, S], F32, at)
        cursor[0] = end
        assert cursor[0] <= base + arena_bytes, cursor[0] - base
        br_hi, at = place("br_hi", [P, 4, S], F32R, u_at)
        br_lo, at = place("br_lo", [P, 4, S], F32R, at)
        merged, at = place("merged", [P, KT, S], F32, at)
        assert at <= sa_v_at, (at, sa_v_at)
        gate, at = place("gate", [P, 4, S], F32, sa_v_at + 4 * S * 4)
        z_sig, at = place("z_sig", [P, 2, S], F32, at)
        m_lo, at = place("m_lo", [P, KT, S], F32R, at)
        assert at <= base + arena_bytes, at - base
        m_hi = place("m_hi", [P, KT, S], F32R, y_at)[0]
        pos_i = place("pos_i", [P, S], I32, u_at)[0]
        pos_f = place("pos_f", [P, S], F32, u_at + 2048)[0]
        edge = place("edge", [P, P], F32, u_at + 4096)[0]
        step = place("step", [P, 4, P // 4], F32, u_at + 8192)[0]
        step_f = place("step_w", [P, 32], F32, u_at + 10240)[0]
        prev_f = place("prev_w", [P, 32], F32, u_at + 11264)[0]
        reach = place("reach", [P, 8, S], F32, y_at)[0]
        bias_out = place("bias_out", [P, 2, S], F32, u_at + 12288)[0]
        ang = place("ang", [P, S], F32, u_at + 16384)[0]
        turns = place("turns", [P, S], F32, u_at + 18432)[0]

        bank = [ctx.enter_context(nc.psum_tensor(f"bank{i}", [P, S], F32)) for i in range(8)]
        NORM, Y = 6, 7

        consts_in = signal("consts_in")
        pos_in = signal("pos_in")
        x_in = signal("x_in")
        setup_dve = signal("setup_dve")
        cos_done = signal("cos_done")
        reach_ready = signal("reach_ready")
        bias_mm = signal("bias_mm")
        bias_evac = signal("bias_evac")
        bias_stored = [signal(f"bias_stored{i}") for i in range(2)]
        gains_in = signal("gains_in")
        gain_row_in = signal("gain_row_in")
        raw_in = [signal(f"raw_in{i}") for i in range(RAW)]
        raw_used = signal("raw_used")
        hi_ready = signal("hi_ready")
        x_stat = signal("x_stat")
        dve_stat = signal("dve_stat")
        xn_ready = signal("xn_ready")
        x_turned = signal("x_turned")
        h_hi_done = signal("h_hi_done")
        h_lo_done = signal("h_lo_done")
        dense = signal("dense")
        act_evac = signal("act_evac")
        dve_evac = signal("dve_evac")
        pool_work = signal("pool_work")
        norm_sum = signal("norm_sum")
        ix_mm = signal("ix_mm")
        ix_relu_done = signal("ix_relu_done")
        score_sum = signal("score_sum")
        score_masked = signal("score_masked")
        topk = signal("topk")
        stick_z = signal("stick_z")
        stick_clip = signal("stick_clip")
        stick_exp = signal("stick_exp")
        stick_sp = signal("stick_sp")
        sp_masked = signal("sp_masked")
        stick_sum = signal("stick_sum")
        stick_prob = signal("stick_prob")
        prob_masked = signal("prob_masked")
        pv_done = signal("pv_done")
        y_out = {br: signal(f"y_out_{br}") for br in ("stick", "mla", "dsa")}
        logits = signal("logits")
        row_max = signal("row_max")
        probs_exp = signal("probs_exp")
        row_inv = signal("row_inv")
        probs_normed = signal("probs_normed")
        probs_turned = signal("probs_turned")
        probs_t_ready = {br: signal(f"probs_t_ready_{br}") for br in ("mla", "dsa")}
        bias_in = [signal(f"bias_in{i}") for i in range(2)]
        gate_sig = signal("gate_sig")
        branch = signal("branch")
        up_done = signal("up_done")
        up_gated = signal("up_gated")
        merge = signal("merge")
        merged_hi = signal("merged_hi")
        out_mm = signal("out_mm")
        x_new = signal("x_new")
        stored = signal("stored")

        arrived = ctx.enter_context(nc.semaphore("arrived"))
        cleared = ctx.enter_context(nc.semaphore("cleared"))

        def clear_signals(e):
            e.sem_clear(arrived)
            for s in signals.values():
                e.sem_clear(s.sem)

        def meet(e, n):
            e.drain().then_inc(arrived, 1)
            e.wait_ge(cleared, n)

        dense_tiles = (["ix_k", "k_pe"] + [f"nat{s}" for s in range(ST)] + ["ix_q0", "ix_q1"]
                       + [f"sa_q{j}" for j in range(4)] + [f"sa_k{j}" for j in range(4)]
                       + ["c_kv", "ds_k"] + [f"ds_q{j}" for j in range(4)] + ["c_q0", "c_q1"]
                       + [f"v_b{s}" for s in range(ST)]
                       + [f"{a}{h}" for h in range(HEADS) for a in ("qh", "kh")])
        for n in range(3):
            dense_tiles += [f"z{n}_{m}" for m in range(4)]
            for half in range(2):
                dense_tiles += [f"g{n}_{4 * half + m}" for m in range(4)]
        TILE = {t: i for i, t in enumerate(dense_tiles)}

        def dbank(tile):
            return bank[TILE[tile] % 2]

        def reader(tile):
            if tile.startswith(("sa_q", "sa_k", "v_b")):
                return act_evac, tile
            if tile.startswith("g"):
                return gate_sig, tile
            if tile.startswith("z"):
                return branch, tile + "z"
            return dve_evac, tile

        def hslab(name, kt, a, b, hi=True, width=2 * P):
            t = w_hi if hi else w_lo
            return t[:, SLAB_NO[name] % RING, kt * width + a:kt * width + b]

        def br_split(e, l, n, m):
            yt = (y[:, 4 * n + m, :] if n < 2 else y_dsa[:, m, :])
            e.wait_ge(*branch.at(f"z{n}_{m}y"))
            if n and m == 0:
                e.wait_ge(*up_done.at(8 * n - 1))
            e.copy(br_hi[:, m, :], yt).then_inc(*merged_hi.tick("br", n, m))

        block = ctx.enter_context(nc.Block())

        @block.sync
        def _(sp_eng):
            e = sp_eng
            e.dma_start(mats[:], consts).then_inc(*consts_in.tick("mats", by=16))
            e.dma_start(pos_i[:], positions[0:1, :].to_broadcast([P, S])).then_inc(*pos_in.tick("pos", by=16))
            e.wait_ge(*setup_dve.at("steps_zero"))
            for qq in range(4):
                e.dma_start(step_f[32 * qq:32 * qq + 32, 8 * qq:8 * qq + 8], rel_bias).then_inc(*pos_in.tick("rb", qq, by=16))
                e.dma_start(prev_f[32 * qq + 1:32 * qq + 32, 8 * qq:8 * qq + 8],
                            rel_bias[0:BUCKETS - 1, :]).then_inc(*pos_in.tick("rbp", qq, by=16))
            for s in range(ST):
                e.dma_start(x_sb[:, s, :], x[0, s * P:(s + 1) * P, :]).then_inc(*x_in.tick("x", s, by=16))
            for G in range(S // 16):
                w = P * (G // 8 + 1)
                e.wait_ge(*bias_evac.at(G))
                e.dma_start(bias_dram[:, 16 * G:16 * G + 16, 0:w].rearrange("h q k -> q h k"),
                            bias_out[:, G % 2, 0:w]).then_inc(*bias_stored[G % 2].tick(G, by=16))

            def pieces(name, l):
                slot = raw[:, SLAB_NO[name] % RAW, :]
                wl = w_in[l].rearrange("(c p) n -> p c n", p=P)

                def cols(view, a, col, n):
                    return view[:, :, a:a + n], wl[:, :, col:col + n]

                v8 = slot[:, 0:KT * SLAB].rearrange("p (c n) -> p c n", c=KT)
                v256 = slot[:, 0:KT * 2 * P].rearrange("p (c n) -> p c n", c=KT)
                v512 = slot[:, 0:4 * S].rearrange("p (c n) -> p c n", c=4)
                if name == "small":
                    return ([cols(v8, 32 * i, COL["ix_k"], 32) for i in range(4)]
                            + [cols(v8, 128, COL["ds_v"], HD), cols(v8, 192, COL["k_pe"], 32),
                               cols(v8, 224, COL["k_pe"] + 16, 16), cols(v8, 240, COL["k_pe"], 16),
                               cols(v8, 256, COL["ix_w"], HEADS)])
                if name == "ckv_dsk":
                    return [cols(v256, 0, COL["c_kv"], P), cols(v256, P, COL["ds_k"], HD),
                            cols(v256, P + HD, COL["ds_k"], HD)]
                if name == "uq":
                    v = slot[:, 0:2 * 8 * P].rearrange("p (c h n) -> p c h n", c=2, h=HEADS)
                    src = w_uq[l].rearrange("(c p) (h n) -> p c h n", p=P, h=HEADS)
                    return [r for c in range(2) for r in (
                        (v[:, c, :, 0:QK], src[:, c, :, :]),
                        (v[:, c, :, QK:QK + 16], src[:, c, :, NOPE + 16:QK]),
                        (v[:, c, :, QK + 16:P], src[:, c, :, NOPE:NOPE + 16]))]
                if name == "ukv":
                    return [(slot[:, 0:HEADS * P], w_ukv[l])]
                if name.startswith("sa_v"):
                    j = int(name[-1])
                    return [(v512, wl[:, 4 * j:4 * j + 4, COL["sa_v"]:COL["sa_v"] + BW])]
                if name.startswith("up"):
                    n, half = int(name[2]), int(name[4])
                    return [(v512, w_branch[l, n].rearrange("(c p) n -> p c n", p=P)[:, :, half * S:(half + 1) * S])]
                if name.startswith("out"):
                    c, j = int(name[3]), int(name[5])
                    return [(v512, w_out[l].rearrange("(c p) n -> p c n", p=P)[:, 4 * j:4 * j + 4, c * S:(c + 1) * S])]
                if name[0] in "zg":
                    n, j = int(name[1]), int(name[3])
                    col = COL[name[0]] + n * (BW if name[0] == "z" else D) + 2 * P * j
                elif name in ("ix_q", "c_q"):
                    col = COL[name]
                else:
                    col = COL[name[:-1]] + 2 * P * int(name[-1])
                return [cols(v256, 0, col, 2 * P)]

            for i in range(2):
                e.wait_ge(*bias_stored[i].at(S // 16 - 2 + i))
            e.wait_ge(arrived, 4)
            clear_signals(e)
            e.sem_inc(cleared, 1)
            with e.Fori(0, DEPTH) as l:
                def load(name):
                    if SLAB_NO[name] >= RAW:
                        e.wait_ge(*raw_used.at(SLABS[SLAB_NO[name] - RAW]))
                    for dst, src in pieces(name, l):
                        e.dma_start(dst, src).then_inc(*raw_in[SLAB_NO[name] % RAW].tick(name, by=16))

                e.dma_start(gain_row[:], norm_g[bass.ds(l, 1), :].to_broadcast([P, D])).then_inc(*gain_row_in.tick("row", by=16))
                for name in SLABS[:SLAB_NO["ukv"] + 1]:
                    load(name)
                load("z0_0")
                load("z0_1")
                for h in range(HEADS):
                    if h >= 2:
                        e.wait_ge(*row_max.at("dsa", h - 2, ST - 1))
                    else:
                        e.wait_ge(*dense.at(f"kh{HEADS - 1}"))
                    for t in range(ST):
                        e.dma_start(bias[:, h % 2, OFF[t]:OFF[t] + P * (t + 1)],
                                    bias_dram[h, t * P:(t + 1) * P, 0:P * (t + 1)]
                                    ).then_inc(*bias_in[h % 2].tick(h, by=16))
                for name in SLABS[SLAB_NO["z0_1"] + 1:]:
                    load(name)
                e.wait_ge(arrived, 4)
                clear_signals(e)
                e.sem_inc(cleared, 1)
            for s in range(ST):
                e.dma_start(out[0, s * P:(s + 1) * P, :], x_sb[:, s, :]).then_inc(stored.sem, 16)
            e.wait_ge(stored.sem, 16 * ST)

        def slab_size(name):
            if name == "small":
                return KT * SLAB
            if name == "ukv":
                return HEADS * P
            return KT * 2 * P

        def last_use(name):
            if name == "small":
                return dense, (f"nat{ST - 1}",)
            if name.startswith("sa_v"):
                return dense, ("sa_v", int(name[-1]), ST - 1)
            if name == "ckv_dsk":
                return dense, ("ds_k",)
            if name in ("ix_q", "c_q"):
                return dense, (f"{name}1",)
            if name == "uq":
                return dense, (f"qh{HEADS - 1}",)
            if name == "ukv":
                return dense, (f"kh{HEADS - 1}",)
            if name.startswith("up"):
                return up_done, (8 * int(name[2]) + 4 * int(name[4]) + 3,)
            if name.startswith("out"):
                return out_mm, (int(name[3]), int(name[5]), ST - 1)
            if name[0] in "zg":
                return dense, (f"{name[0]}{name[1]}_{2 * int(name[3]) + 1}",)
            return dense, (f"{name[:-1]}{2 * int(name[-1]) + 1}",)

        def gated(u):
            return (merge, ("sum", u)) if u < KT else (up_gated, (u,))

        def wait_ring_slot(e, l, name):
            s = SLAB_NO[name]
            if s >= RING:
                sig, event = last_use(SLABS[s - RING])
                e.wait_ge(*sig.at(*event))

        def split_hi(e, l, name):
            s = SLAB_NO[name]
            e.wait_ge(*raw_in[s % RAW].at(name))
            wait_ring_slot(e, l, name)
            n = slab_size(name)
            e.copy(w_hi[:, s % RING, 0:n], raw[:, s % RAW, 0:n]).then_inc(*hi_ready.tick(name))

        def split_lo(e, l, name):
            s = SLAB_NO[name]
            e.wait_ge(*hi_ready.at(name))
            n = slab_size(name)
            e.tensor_tensor(w_lo[:, s % RING, 0:n], raw[:, s % RAW, 0:n],
                            w_hi[:, s % RING, 0:n].bitcast(F32), ALU.subtract).then_inc(*raw_used.tick(name))

        @block.tensor
        def _(pe):
            pe.wait_ge(*consts_in.at("mats"))
            for G in range(S // 16):
                w = P * (G // 8 + 1)
                if G >= 2:
                    pe.wait_ge(*bias_evac.at(G - 2))
                for g4 in range(4):
                    g = 4 * G + g4
                    pe.wait_ge(*reach_ready.at(g))
                    mm = pe.matmul(bank[G % 2][32 * g4:32 * g4 + 32, 0:w], step_f[:, 0:32],
                                   reach[:, g % 8, 0:w], start=True, stop=True)
                    mm.then_inc(*bias_mm.tick(g))
            meet(pe, 1)
            with pe.Fori(0, DEPTH) as l:
                def use(name):
                    pe.wait_ge(*raw_used.at(name))

                def tile_bank(tile):
                    i = TILE[tile]
                    if i >= 2:
                        sig, key = reader(dense_tiles[i - 2])
                        pe.wait_ge(*sig.at(key))
                    return bank[i % 2]

                def three(out_ap, terms, start=True, stop=True):
                    n = len(terms)
                    for i, (lh, ll, rh, rl) in enumerate(terms):
                        pe.matmul(out_ap, lh, rh, start=start and i == 0, stop=False)
                        pe.matmul(out_ap, lh, rl, start=False, stop=False)
                        mm = pe.matmul(out_ap, ll, rh, start=False, stop=stop and i == n - 1)
                    return mm

                def project(tile, name, a, m, width=2 * P):
                    b = tile_bank(tile)
                    return three(b[0:m, :], [(hslab(name, k, a, a + m, True, width), hslab(name, k, a, a + m, False, width),
                                              h_hi[:, k, :], h_lo[:, k, :]) for k in range(KT)])

                for s in range(ST):
                    for j in range(2):
                        i = 2 * s + j
                        if j == 0:
                            pe.wait_ge(*xn_ready.at(s))
                        if i >= 2:
                            pe.wait_ge(*h_lo_done.at(i - 2))
                        for k in range(4):
                            mm = pe.transpose(bank[i % 2][:, k * P:(k + 1) * P],
                                              xn[:, s % 2, (4 * j + k) * P:(4 * j + k + 1) * P], eye)
                        mm.then_inc(*x_turned.tick(i))
                pe.wait_ge(*h_lo_done.at(7))
                use("small")
                project("ix_k", "small", 0, P, SLAB).then_inc(*dense.tick("ix_k"))
                project("k_pe", "small", P, P, SLAB).then_inc(*dense.tick("k_pe"))
                for s in range(ST):
                    b = tile_bank(f"nat{s}")
                    q = slice(s * P, (s + 1) * P)
                    mm = three(b[:, 0:136], [(h_hi[:, k, q], h_lo[:, k, q], hslab("small", k, P, SLAB, True, SLAB),
                                              hslab("small", k, P, SLAB, False, SLAB)) for k in range(KT)])
                    mm.then_inc(*dense.tick(f"nat{s}"))
                use("ix_q")
                for j in range(2):
                    project(f"ix_q{j}", "ix_q", j * P, P).then_inc(*dense.tick(f"ix_q{j}"))
                pe.wait_ge(*dve_evac.at("ix_q1"))
                units = [(h, t) for h in range(HEADS) for t in range(1, ST)]
                for u, (h, t) in enumerate(units):
                    if u >= 4:
                        pe.wait_ge(*ix_relu_done.at(u - 4))
                    r = slice(IDX_DIM * (h % 4), IDX_DIM * (h % 4) + IDX_DIM)
                    pe.matmul(bank[2 + u % 4][:, 0:P * (t + 1)], ix_q[r, h // 4, t * P:(t + 1) * P],
                              ix_k[r, 0:P * (t + 1)], start=True, stop=True).then_inc(*ix_mm.tick(u))
                for part in ("sa_q", "sa_k"):
                    for j in range(4):
                        if j % 2 == 0:
                            use(f"{part}{j // 2}")
                        project(f"{part}{j}", f"{part}{j // 2}", (j % 2) * P, P).then_inc(*dense.tick(f"{part}{j}"))
                pe.wait_ge(*ix_relu_done.at(len(units) - 1))
                for j in range(2):
                    use(f"sa_v{j}")
                    for s in range(ST):
                        q = slice(s * P, (s + 1) * P)
                        mm = three(bank[2 + s][:, :],
                                   [(h_hi[:, 4 * j + k, q], h_lo[:, 4 * j + k, q], hslab(f"sa_v{j}", k, 0, S, True, S),
                                     hslab(f"sa_v{j}", k, 0, S, False, S)) for k in range(4)],
                                   start=j == 0, stop=j == 1)
                        mm.then_inc(*dense.tick("sa_v", j, s))
                pe.wait_ge(*act_evac.at("sa_k3"))

                units = [(h, kt) for h in range(HEADS) for kt in reversed(range(ST))]
                fill = ["c_kv", "ds_k", "ds_q0", "ds_q1", "ds_q2", "ds_q3", "c_q0", "c_q1"]
                place_of = {"c_kv": ("ckv_dsk", 0), "ds_k": ("ckv_dsk", P), "c_q0": ("c_q", 0), "c_q1": ("c_q", P)}
                for j in range(4):
                    place_of[f"ds_q{j}"] = (f"ds_q{j // 2}", (j % 2) * P)

                def norm(tile, weights, src, start=True, stop=True, k=P):
                    mm = pe.matmul(bank[NORM][:, :], weights[0:k, :], src[0:k, :], start=start, stop=stop)
                    mm.then_inc(*norm_sum.tick(tile))

                def z_of(u):
                    h, kt = units[u]
                    b, w, r = bank[2 + u % 4], S - kt * P, slice(HD * (h % 2), HD * (h % 2) + HD)
                    if u >= 4:
                        pe.wait_ge(*stick_prob.at(u - 4))
                    elif u < 4:
                        pe.wait_ge(*act_evac.at("sa_v", u))
                    pe.matmul(b[:, 0:w], sa_k[r, h // 2, kt * P:(kt + 1) * P], sa_q[r, h // 2, kt * P:S],
                              start=True, stop=True).then_inc(*stick_z.tick(u))

                def suffix_of(u):
                    h, kt = units[u]
                    b, w = bank[2 + u % 4], S - kt * P
                    pe.wait_ge(*sp_masked.at(u))
                    pe.matmul(b[:, 0:w], suffix, sp[:, h % 2, SOFF[kt]:SOFF[kt] + w], start=False,
                              stop=kt == ST - 1, skip_group_check=True)
                    mm = None
                    for later in range(kt + 1, ST):
                        wl = S - later * P
                        mm = pe.matmul(b[:, (later - kt) * P:w], all_later, sp[:, h % 2, SOFF[later]:SOFF[later] + wl],
                                       start=False, stop=later == ST - 1, skip_group_check=True)
                    return mm

                def pv_of(u):
                    h, kt = units[u]
                    w = S - kt * P
                    pe.wait_ge(*prob_masked.at(u))
                    if kt == ST - 1 and h % 2 == 0 and h:
                        pe.wait_ge(*y_out["stick"].at(h // 2 - 1))
                    pe.matmul(bank[Y][HD * (h % 2):HD * (h % 2) + HD, kt * P:S], sa_v[:, kt, h * HD:(h + 1) * HD],
                              stick_a[:, u % 2, 0:w], start=kt == ST - 1, stop=kt == 0,
                              skip_group_check=True).then_inc(*pv_done.tick("stick", u))

                for i in range(len(units) + 3):
                    if i < len(units):
                        z_of(i)
                    if i % 4 == 1 and i // 4 < len(fill):
                        tile = fill[i // 4]
                        name, a = place_of[tile]
                        if a == 0:
                            use(name)
                        project(tile, name, a, P).then_inc(*dense.tick(tile))
                    if i % 4 == 2 and i // 4 < len(fill):
                        tile = fill[i // 4]
                        pe.wait_ge(*act_evac.at(tile + "sq"))
                        if tile == "c_q0":
                            norm(tile, ones, norm_sq, True, False)
                        elif tile == "c_q1":
                            norm(tile, ones, norm_sq, False, True)
                        else:
                            prev = fill[i // 4 - 1] if i // 4 else None
                            norm(tile, ones if tile == "c_kv" else per_head, norm_sq)
                    if 0 <= i - 2 < len(units):
                        u = i - 2
                        h, kt = units[u]
                        if kt == ST - 1:
                            pe.wait_ge(*sp_masked.at(u))
                            pe.matmul(bank[2 + u % 4][:, 0:P], suffix, sp[:, h % 2, SOFF[kt]:SOFF[kt] + P], start=False,
                                      stop=True, skip_group_check=True).then_inc(*stick_sum.tick(u))
                        else:
                            suffix_of(u).then_inc(*stick_sum.tick(u))
                    if 0 <= i - 3 < len(units):
                        pv_of(i - 3)

                use("uq")
                use("ukv")
                pe.wait_ge(*pool_work.at("c_q1lo"))
                pe.wait_ge(*y_out["stick"].at(3))
                uq = [w[:, SLAB_NO["uq"] % RING, 0:16 * P].rearrange("p (c h n) -> p c h n", c=2, h=HEADS) for w in (w_hi, w_lo)]
                ukv = [w[:, SLAB_NO["ukv"] % RING, 0:HEADS * P].rearrange("p (h n) -> p h n", h=HEADS) for w in (w_hi, w_lo)]
                for s in range(ST):
                    b = tile_bank(f"v_b{s}")
                    q = slice(s * P, (s + 1) * P)
                    three(b[:, :], [(ckv_hi[:, q], ckv_lo[:, q], ukv[0][:, :, NOPE:P], ukv[1][:, :, NOPE:P])]
                          ).then_inc(*dense.tick(f"v_b{s}"))

                def prep_q(h):
                    b = tile_bank(f"qh{h}")
                    three(b[:, :], [(uq[0][:, c, h, :], uq[1][:, c, h, :], cq_hi[:, c, :], cq_lo[:, c, :]) for c in range(2)]
                          ).then_inc(*dense.tick(f"qh{h}"))

                def prep_k(h):
                    b = tile_bank(f"kh{h}")
                    three(b[0:NOPE, :], [(ukv[0][:, h, 0:NOPE], ukv[1][:, h, 0:NOPE], ckv_hi[:, :], ckv_lo[:, :])]
                          ).then_inc(*dense.tick(f"kh{h}"))

                def norm_q(h):
                    pe.wait_ge(*act_evac.at(f"qh{h}sq"))
                    if h == 0:
                        pe.wait_ge(*act_evac.at("c_q1rs"))
                    norm(f"qh{h}", first_qk, q_sq)

                def norm_k(h):
                    pe.wait_ge(*act_evac.at(f"kh{h}sq"))
                    pe.wait_ge(*act_evac.at(f"qh{h}ln"))
                    norm(f"kh{h}", ones, k_sq, k=QK)

                units = [(h, t) for h in range(HEADS) for t in range(ST)]

                def s_of(br, u):
                    h, t = units[u]
                    b, w = bank[2 + u % 2], P * (t + 1)
                    q = slice(t * P, (t + 1) * P)
                    if u >= 2:
                        if br == "mla":
                            pe.wait_ge(*probs_exp.at(br, u - 2))
                        else:
                            pe.wait_ge(*row_max.at(br, *units[u - 2]))
                    elif br == "dsa":
                        pe.wait_ge(*probs_exp.at("mla", len(units) - 2 + u))
                    if br == "mla":
                        if t == 0:
                            pe.wait_ge(*pool_work.at(f"qh{h}rope"))
                            pe.wait_ge(*pool_work.at(f"kh{h}rope"))
                            pe.wait_ge(*dve_evac.at(f"kh{h}"))
                        pe.matmul(b[:, 0:w], q_head[0:QK, h % 2, q], k_head[0:QK, h % 2, 0:w], start=True, stop=True)
                        mm = pe.matmul(b[:, w - P:w], big_eye[:, :], causal[:, :], start=False, stop=True, skip_group_check=True)
                    else:
                        if u == 0:
                            pe.wait_ge(*dve_evac.at("ds_q3"))
                            pe.wait_ge(*topk.at("chosen", ST - 1))
                        r = slice(HD * (h % 2), HD * (h % 2) + HD)
                        pe.matmul(b[:, 0:w], ds_q[r, h // 2, q], ds_k[r, 0:w], start=True, stop=True)
                        m = causal[:, :] if t == 0 else chosen[:, OFF[t]:OFF[t] + w]
                        mm = pe.matmul(b[:, 0:w], big_eye[:, :], m, start=False, stop=True, skip_group_check=True)
                    mm.then_inc(*logits.tick(br, u))

                def t_of(br, u):
                    h, t = units[u]
                    pe.wait_ge(*probs_normed.at(br, u))
                    if u >= 2:
                        pe.wait_ge(*probs_t_ready[br].at(u - 2))
                    elif br == "dsa":
                        pe.wait_ge(*probs_t_ready["mla"].at(len(units) - 2 + u))
                    for k in range(t + 1):
                        mm = pe.transpose(bank[4 + u % 2][:, k * P:(k + 1) * P], probs[:, u % 3, k * P:(k + 1) * P], eye)
                    mm.then_inc(*probs_turned.tick(br, u))

                def av_of(br, u):
                    h, t = units[u]
                    pe.wait_ge(*probs_t_ready[br].at(u))
                    if t == 0 and h % 2 == 0:
                        if h:
                            pe.wait_ge(*y_out[br].at(h // 2 - 1))
                        elif br == "dsa":
                            pe.wait_ge(*y_out["mla"].at(3))
                    if br == "mla" and u == 0:
                        pe.wait_ge(*act_evac.at(f"v_b{ST - 1}"))
                    for k in range(t + 1):
                        v = v_b[:, k, h * HD:(h + 1) * HD] if br == "mla" else ds_v[:, k, :]
                        mm = pe.matmul(bank[Y][HD * (h % 2):HD * (h % 2) + HD, t * P:(t + 1) * P], v,
                                       probs_t[:, u % 3, k * P:(k + 1) * P], start=k == 0, stop=k == t)
                    mm.then_inc(*pv_done.tick(br, u))

                prep_q(0)
                prep_k(0)
                norm_q(0)
                norm_k(0)
                for i in range(len(units) + 3):
                    if i < len(units):
                        s_of("mla", i)
                        h, t = units[i]
                        if h + 1 < HEADS:
                            if t == 0:
                                prep_q(h + 1)
                            if t == 1:
                                prep_k(h + 1)
                                norm_q(h + 1)
                            if t == 2:
                                norm_k(h + 1)
                    if 0 <= i - 2 < len(units):
                        t_of("mla", i - 2)
                    if 0 <= i - 3 < len(units):
                        av_of("mla", i - 3)
                for i in range(len(units) + 3):
                    if i < len(units):
                        s_of("dsa", i)
                    if 0 <= i - 2 < len(units):
                        t_of("dsa", i - 2)
                    if 0 <= i - 3 < len(units):
                        av_of("dsa", i - 3)
                ups = 0
                for n in range(3):
                    for m in range(4):
                        if m % 2 == 0:
                            use(f"z{n}_{m // 2}")
                        project(f"z{n}_{m}", f"z{n}_{m // 2}", (m % 2) * P, P).then_inc(*dense.tick(f"z{n}_{m}"))
                    for half in range(2):
                        for m in range(4):
                            if m % 2 == 0:
                                use(f"g{n}_{2 * half + m // 2}")
                            project(f"g{n}_{4 * half + m}", f"g{n}_{2 * half + m // 2}", (m % 2) * P, P
                                    ).then_inc(*dense.tick(f"g{n}_{4 * half + m}"))
                        use(f"up{n}_{half}")
                        for m in range(4):
                            if n == 0 and half == 0 and m == 0:
                                pe.wait_ge(*y_out["dsa"].at(3))
                                pe.wait_ge(*probs_exp.at("dsa", len(units) - 1))
                            if ups >= 2:
                                sig, event = gated(ups - 2)
                                pe.wait_ge(*sig.at(*event))
                            if half == 0 and m == 0:
                                pe.wait_ge(*branch.at(f"z{n}_3lo"))
                            name = f"up{n}_{half}"
                            three(bank[2 + ups % 2][:, :],
                                  [(hslab(name, k, m * P, (m + 1) * P, True, S), hslab(name, k, m * P, (m + 1) * P, False, S),
                                    br_hi[:, k, :], br_lo[:, k, :]) for k in range(4)]).then_inc(*up_done.tick(ups))
                            ups += 1
                pe.wait_ge(*merge.at("lo", KT - 1))
                for c in range(2):
                    for j in range(2):
                        use(f"out{c}_{j}")
                        for s in range(ST):
                            if j == 0 and c == 1:
                                pe.wait_ge(*x_new.at(0, s))
                            elif j == 0 and s < 2:
                                pe.wait_ge(*up_gated.at(ups - 2 + s))
                            q = slice(s * P, (s + 1) * P)
                            name = f"out{c}_{j}"
                            three(bank[2 + s][:, :],
                                  [(m_hi[:, 4 * j + k, q], m_lo[:, 4 * j + k, q], hslab(name, k, 0, S, True, S),
                                    hslab(name, k, 0, S, False, S)) for k in range(4)],
                                  start=j == 0, stop=j == 1).then_inc(*out_mm.tick(c, j, s))
                meet(pe, l + 2)

        @block.scalar
        def _(e):
            with nc.allow_non_contiguous_dma(reason="one gain per partition, once"):
                def column(i, rows, src):
                    e.dma_start(gains[rows, :, i:i + 1], src.rearrange("l (p o) -> p l o", o=1)
                                ).then_inc(*gains_in.tick(i, rows.start, by=16))
                column(0, slice(0, P), kv_norm_g)
                column(1, slice(0, P), q_norm_g[:, 0:P])
                column(2, slice(0, P), q_norm_g[:, P:2 * P])
                for i, g in ((3, mla_q_g), (4, mla_k_g)):
                    column(i, slice(0, QK), g)
                    column(i, slice(QK, QK + 16), g[:, NOPE + 16:QK])
                    column(i, slice(QK + 16, P), g[:, NOPE:NOPE + 16])
                for i, g in ((5, dsa_q_g), (6, dsa_k_g)):
                    column(i, slice(0, HD), g)
                    column(i, slice(HD, P), g)
                for ll in range(DEPTH):
                    for n in range(3):
                        e.dma_start(gains[:, ll, N_GAINS + 8 * n:N_GAINS + 8 + 8 * n],
                                    gate_b[ll, n].rearrange("(m p) -> p m", p=P)
                                    ).then_inc(*gains_in.tick("b", ll, n, by=16))
            e.wait_ge(*setup_dve.at("angle"))
            e.activation(ang[64:P, :], turns[64:P, :], ACT.Sin).then_inc(*cos_done.tick("sin"))
            for G in range(S // 16):
                w = P * (G // 8 + 1)
                e.wait_ge(*bias_mm.at(4 * G + 3))
                if G >= 2:
                    e.wait_ge(*bias_stored[G % 2].at(G - 2))
                e.copy(bias_out[:, G % 2, 0:w], bank[G % 2][:, 0:w]).then_inc(*bias_evac.tick(G))
            e.preload_act_table_set("natural_log_exp_and_others")
            meet(e, 1)
            with e.Fori(0, DEPTH) as l:
                def hi(s):
                    split_hi(e, l, SLABS[s])

                hi(0)
                for s in range(ST):
                    e.activation(x_sq[:, :], x_sb[:, s, :], ACT.Square, accum_out=stat[:, s:s + 1]
                                 ).then_inc(*x_stat.tick("sq", s))
                    e.wait_ge(*x_stat.at("sq", s))
                e.activation(stat[:, 4:8], stat[:, 0:4], ACT.Ln, bias=stat[:, 60:61], scale=1.0 / D).then_inc(*x_stat.tick("ln"))
                e.wait_ge(*x_stat.at("ln"))
                e.activation(stat[:, 8:12], stat[:, 4:8], ACT.Exp, scale=-0.5).then_inc(*x_stat.tick("rs"))
                for i in range(2 * ST):
                    s, j = i // 2, i % 2
                    e.wait_ge(*x_turned.at(i))
                    e.copy(h_hi[:, 4 * j:4 * j + 4, s * P:(s + 1) * P],
                           bank[i % 2][:, :].rearrange("p (k q) -> p k q", k=4)).then_inc(*h_hi_done.tick(i))
                hi(1)
                e.wait_ge(*dense.at("k_pe"))
                e.activation(k_sq[64:96, :], dbank("k_pe")[64:96, :], ACT.Square).then_inc(*act_evac.tick("k_pe"))
                hi(2)
                units = [(h, t) for h in range(HEADS) for t in range(1, ST)]
                for u, (h, t) in enumerate(units):
                    w = P * (t + 1)
                    e.wait_ge(*ix_mm.at(u))
                    if u >= 3:
                        e.wait_ge(*score_sum.at(u - 3))
                    e.activation(ix_relu[:, u % 3, 0:w], bank[2 + u % 4][:, 0:w], ACT.Relu, scale=IDX_DIM ** -0.5
                                 ).then_inc(*ix_relu_done.tick(u))
                hi(3)
                nxt = 4
                for part, dst in (("sa_q", sa_q), ("sa_k", sa_k)):
                    for j in range(4):
                        e.wait_ge(*dense.at(f"{part}{j}"))
                        e.copy(dst[:, j, :], dbank(f"{part}{j}")[:, :]).then_inc(*act_evac.tick(f"{part}{j}"))
                        if j % 2:
                            hi(nxt)
                            nxt += 1
                hi(8)
                for s in range(ST):
                    e.wait_ge(*dense.at("sa_v", 1, s))
                    e.copy(sa_v[:, s, :], bank[2 + s][:, :]).then_inc(*act_evac.tick("sa_v", s))
                hi(9)

                def rs_of(tile, n, dst, scale=1.0):
                    e.wait_ge(*norm_sum.at(tile))
                    e.activation(dst, bank[NORM][:, :], ACT.Ln, bias=stat[:, 60:61], scale=1.0 / n
                                 ).then_inc(*act_evac.tick(tile + "ln"))
                    e.wait_ge(*act_evac.at(tile + "ln"))
                    b = 0.0 if scale == 1.0 else stat[:, 61:62] if scale == HD ** -0.5 else stat[:, 62:63]
                    e.activation(dst, dst, ACT.Exp, scale=-0.5, bias=b).then_inc(*act_evac.tick(tile + "rs"))

                units = [(h, kt) for h in range(HEADS) for kt in reversed(range(ST))]
                fill = ["c_kv", "ds_k", "ds_q0", "ds_q1", "ds_q2", "ds_q3", "c_q0", "c_q1"]
                for i in range(len(units) + 5):
                    if i < len(units):
                        w = S - units[i][1] * P
                        v = soft[:, i % 3, 0:w]
                        e.wait_ge(*stick_clip.at(i))
                        e.activation(v, v, ACT.Exp).then_inc(*stick_exp.tick("exp", i))
                        e.wait_ge(*stick_exp.at("exp", i))
                        e.activation(v, v, ACT.Ln, bias=1.0).then_inc(*stick_exp.tick("ln", i))
                    k = i // 4
                    if i % 4 == 1 and k < len(fill):
                        tile = fill[k]
                        e.wait_ge(*dense.at(tile))
                        if k:
                            e.wait_ge(*norm_sum.at(fill[k - 1]))
                        e.activation(norm_sq[:, :], dbank(tile)[:, :], ACT.Square).then_inc(*act_evac.tick(tile + "sq"))
                        if k % 2:
                            hi(10 + k // 2)
                    if i % 4 == 3 and k < len(fill) and fill[k] != "c_q0":
                        tile = fill[k]
                        if k:
                            prev = fill[k - 1] if fill[k - 1] != "c_q0" else fill[k - 2]
                            e.wait_ge(*dve_evac.at(prev))
                        n = {"c_kv": KV_LORA, "c_q1": Q_LORA}.get(tile, HD)
                        rs_of(tile, n, norm_rs[:, :], HD ** -0.5 if tile.startswith("ds_q") else 1.0)
                    if i == 4:
                        e.wait_ge(*dve_evac.at("c_kv"))
                        e.copy(ckv_hi[:, :], norm_out[:, :]).then_inc(*act_evac.tick("ckv_hi"))
                    if i == 33:
                        for c in range(2):
                            e.wait_ge(*dve_evac.at(f"c_q{c}"))
                            e.copy(cq_hi[:, c, :], cq_out[c][:, :]).then_inc(*act_evac.tick(f"cq_hi{c}"))
                    if 0 <= i - 2 < len(units):
                        u = i - 2
                        w = S - units[u][1] * P
                        e.wait_ge(*stick_sum.at(u))
                        if u >= 2:
                            e.wait_ge(*pv_done.at("stick", u - 2))
                        e.activation(stick_a[:, u % 2, 0:w], bank[2 + u % 4][:, 0:w], ACT.Exp, scale=STICK_SCALE
                                     ).then_inc(*stick_prob.tick(u))

                for s in range(ST):
                    e.wait_ge(*dense.at(f"v_b{s}"))
                    if s == 0:
                        e.wait_ge(*pv_done.at("stick", len(units) - 1))
                    e.copy(v_b[:, s, :], dbank(f"v_b{s}")[:, :]).then_inc(*act_evac.tick(f"v_b{s}"))

                def sq_q(h):
                    e.wait_ge(*dense.at(f"qh{h}"))
                    e.activation(q_sq[:, :], dbank(f"qh{h}")[:, :], ACT.Square).then_inc(*act_evac.tick(f"qh{h}sq"))

                def sq_k(h):
                    e.wait_ge(*dense.at(f"kh{h}"))
                    if h:
                        e.wait_ge(*norm_sum.at(f"kh{h - 1}"))
                    e.activation(k_sq[0:NOPE, :], dbank(f"kh{h}")[0:NOPE, :], ACT.Square).then_inc(*act_evac.tick(f"kh{h}sq"))

                def rs_q(h):
                    if h:
                        e.wait_ge(*dve_evac.at(f"qh{h - 1}"))
                    rs_of(f"qh{h}", QK, q_rs[:, :], QK ** -0.5)

                def rs_k(h):
                    if h:
                        e.wait_ge(*dve_evac.at(f"kh{h - 1}"))
                        e.wait_ge(*pool_work.at(f"kh{h - 1}rope"))
                    rs_of(f"kh{h}", QK, k_rs[:, :])

                def exp_of(br, u, src):
                    w = P * (units[u][1] + 1)
                    e.wait_ge(*row_max.at(br, *units[u]))
                    if u >= 3:
                        e.wait_ge(*probs_turned.at(br, u - 3))
                    e.activation(probs[:, u % 3, 0:w], src, ACT.Exp, bias=stat[:, 16 + u % 4:17 + u % 4],
                                 accum_out=stat[:, 20 + u % 4:21 + u % 4]).then_inc(*probs_exp.tick(br, u))

                def y_of(br, pair, dst):
                    e.wait_ge(*pv_done.at(br, 8 * pair + 7))
                    e.copy(dst, bank[Y][:, :]).then_inc(*y_out[br].tick(pair))

                units = [(h, t) for h in range(HEADS) for t in range(ST)]
                sq_q(0)
                sq_k(0)
                rs_q(0)
                rs_k(0)
                for i in range(len(units) + 5):
                    if i < len(units):
                        h, t = units[i]
                        exp_of("mla", i, bank[2 + i % 2][:, 0:P * (t + 1)])
                        if h + 1 < HEADS:
                            if t == 0:
                                sq_q(h + 1)
                            if t == 1:
                                sq_k(h + 1)
                                rs_q(h + 1)
                            if t == 2:
                                rs_k(h + 1)
                    if i >= 4 and (i - 4) % 8 == 7:
                        y_of("mla", (i - 4) // 8, y[:, 4 + (i - 4) // 8, :])
                hi(SLAB_NO["z0_0"])
                hi(SLAB_NO["z0_1"])
                for i in range(len(units) + 5):
                    if i < len(units):
                        exp_of("dsa", i, probs[:, i % 3, 0:P * (units[i][1] + 1)])
                    if 0 <= i - 2 < len(units):
                        u = i - 2
                        w = P * (units[u][1] + 1)
                        e.wait_ge(*probs_turned.at("dsa", u))
                        if u >= 3:
                            e.wait_ge(*pv_done.at("dsa", u - 3))
                        e.copy(probs_t[:, u % 3, 0:w], bank[4 + u % 2][:, 0:w]).then_inc(*probs_t_ready["dsa"].tick(u))
                    if i >= 4 and (i - 4) % 8 == 7:
                        y_of("dsa", (i - 4) // 8, y_dsa[:, (i - 4) // 8, :])
                e.preload_act_table_set("sigmoid_and_others")
                ups = 0
                nxt = SLAB_NO["z0_0"] + 2
                for n in range(3):
                    for m in range(4):
                        e.wait_ge(*dense.at(f"z{n}_{m}"))
                        if 4 * n + m >= 2:
                            pn, pm = divmod(4 * n + m - 2, 4)
                            e.wait_ge(*branch.at(f"z{pn}_{pm}z"))
                        e.activation(z_sig[:, m % 2, :], dbank(f"z{n}_{m}")[:, :], ACT.Sigmoid).then_inc(*gate_sig.tick("z", n, m))
                        if m % 2:
                            hi(nxt)
                            nxt += 1
                        if m:
                            br_split(e, l, n, m - 1)
                    br_split(e, l, n, 3)
                    for half in range(2):
                        for m in range(4):
                            mm = 4 * half + m
                            e.wait_ge(*dense.at(f"g{n}_{mm}"))
                            g = 8 * n + mm
                            if g >= 4:
                                e.wait_ge(*merge.at("sum", g - 4))
                            e.activation(gate[:, m, :], dbank(f"g{n}_{mm}")[:, :], ACT.Sigmoid,
                                         bias=gain[:, N_GAINS + g:N_GAINS + 1 + g]).then_inc(*gate_sig.tick(f"g{n}_{mm}"))
                            if m % 2:
                                hi(nxt)
                                nxt += 1
                        if n == 2:
                            for m in range(4 * half, 4 * half + 4):
                                e.wait_ge(*merge.at("sum", 16 + m))
                                e.copy(m_hi[:, m, :], merged[:, m, :]).then_inc(*merged_hi.tick(m))
                        if nxt < NS:
                            hi(nxt)
                            nxt += 1
                while nxt < NS:
                    hi(nxt)
                    nxt += 1
                e.preload_act_table_set("natural_log_exp_and_others")
                meet(e, l + 2)

        @block.vector
        def _(e):
            e.memset(step_f[:, :], 0.0).then_inc(*setup_dve.tick("z0"))
            e.memset(prev_f[:, :], 0.0).then_inc(*setup_dve.tick("steps_zero"))
            e.memset(stat[:, 60:61], EPS).then_inc(*setup_dve.tick("c0"))
            e.memset(stat[:, 61:62], math.log(HD ** -0.5)).then_inc(*setup_dve.tick("c1"))
            e.memset(stat[:, 62:63], math.log(QK ** -0.5)).then_inc(*setup_dve.tick("c2"))
            e.wait_ge(*consts_in.at("mats"))
            e.tensor_copy(big_eye[:, :], big_eye_f).then_inc(*setup_dve.tick("be"))
            e.tensor_copy(causal[:, :], causal_f).then_inc(*setup_dve.tick("ca"))
            e.wait_ge(*pos_in.at("rbp", 3))
            e.tensor_copy(pos_f[:, :], pos_i[:, :]).then_inc(*setup_dve.tick("pos"))
            e.tensor_tensor(step_f[:, :], step_f[:, :], prev_f[:, :], ALU.subtract).then_inc(*setup_dve.tick("steps"))
            e.wait_ge(*setup_dve.at("steps"))
            for qq in range(4):
                r = slice(32 * qq, 32 * qq + 32)
                e.tensor_scalar(edge[r, :], pos_f[r, qq:S:4], thr[r, :], None, ALU.subtract).then_inc(*setup_dve.tick("edge", qq))
            hi_rows = slice(64, P)
            e.tensor_scalar(ang[hi_rows, :], pos_f[hi_rows, :], inv_freq[hi_rows, :], None, ALU.mult).then_inc(*setup_dve.tick("a0"))
            e.wait_ge(*setup_dve.at("a0"))
            tau = 2.0 * math.pi
            c1 = 6.28125
            c2 = float(np.float32(np.round((tau - c1) * 2 ** 21) / 2 ** 21))
            c3 = tau - c1 - c2
            e.tensor_scalar(stat[hi_rows, 58:59], phase[hi_rows, :], 1.0 / tau, None, ALU.mult).then_inc(*setup_dve.tick("ph"))
            e.wait_ge(*setup_dve.at("ph"))
            magic = 1.5 * 2.0 ** 23
            e.tensor_scalar(turns[hi_rows, :], ang[hi_rows, :], 1.0 / tau, stat[hi_rows, 58:59], ALU.mult, ALU.add).then_inc(*setup_dve.tick("t0"))
            e.wait_ge(*setup_dve.at("t0"))
            e.tensor_scalar(turns[hi_rows, :], turns[hi_rows, :], magic, None, ALU.add).then_inc(*setup_dve.tick("t1"))
            e.wait_ge(*setup_dve.at("t1"))
            e.tensor_scalar(turns[hi_rows, :], turns[hi_rows, :], magic, None, ALU.subtract).then_inc(*setup_dve.tick("t2"))
            e.wait_ge(*setup_dve.at("t2"))
            for i, c in enumerate((c1, c2, c3)):
                e.scalar_tensor_tensor(ang[hi_rows, :], turns[hi_rows, :], -c, ang[hi_rows, :], ALU.mult, ALU.add
                                       ).then_inc(*setup_dve.tick("r", i))
                e.wait_ge(*setup_dve.at("r", i))
            e.tensor_scalar(ang[hi_rows, :], ang[hi_rows, :], phase[hi_rows, :], 3.1415925, ALU.add, ALU.min).then_inc(*setup_dve.tick("r3"))
            e.wait_ge(*setup_dve.at("r3"))
            e.tensor_scalar(turns[hi_rows, :], ang[hi_rows, :], -3.1415925, None, ALU.max).then_inc(*setup_dve.tick("angle"))
            e.wait_ge(*cos_done.at("sin"))
            e.tensor_scalar(cos_sin[hi_rows, :], ang[hi_rows, :], sign[hi_rows, :], None, ALU.mult).then_inc(*setup_dve.tick("cs"))
            for g in range(S // 4):
                w = P * (g // 32 + 1)
                if g >= 8:
                    e.wait_ge(*bias_mm.at(g - 8))
                e.tensor_scalar(reach[:, g % 8, 0:w], pos_f[:, 0:w], edge[:, g:g + 1], None, ALU.is_le
                                ).then_inc(*reach_ready.tick(g))
            e.wait_ge(*gains_in.at("b", DEPTH - 1, 2))
            e.wait_ge(*x_in.at("x", ST - 1))
            meet(e, 1)
            with e.Fori(0, DEPTH) as l:
                v, t, r0, r = (stat[:, i:i + 4] for i in (24, 28, 8, 12))
                e.wait_ge(*x_stat.at("rs"))
                e.tensor_copy(gain[:, :], gains[:, l, :]).then_inc(*dve_stat.tick("gain"))
                e.tensor_scalar(v, stat[:, 0:4], 1.0 / D, EPS, ALU.mult, ALU.add).then_inc(*dve_stat.tick("v"))
                e.tensor_tensor(t, r0, r0, ALU.mult).then_inc(*dve_stat.tick("t0"))
                e.wait_ge(*dve_stat.at("t0"))
                e.tensor_tensor(t, t, v, ALU.mult).then_inc(*dve_stat.tick("t1"))
                e.wait_ge(*dve_stat.at("t1"))
                e.tensor_scalar(t, t, -0.5, 1.5, ALU.mult, ALU.add).then_inc(*dve_stat.tick("t2"))
                e.wait_ge(*dve_stat.at("t2"))
                e.tensor_tensor(r, r0, t, ALU.mult).then_inc(*dve_stat.tick("r"))
                e.wait_ge(*dve_stat.at("r"))
                e.wait_ge(*gain_row_in.at("row"))

                def h_lo_of(i):
                    s, j = i // 2, i % 2
                    e.wait_ge(*h_hi_done.at(i))
                    cols = (slice(None), slice(4 * j, 4 * j + 4), slice(s * P, (s + 1) * P))
                    e.tensor_tensor(h_lo[cols], bank[i % 2][:, :].rearrange("p (k q) -> p k q", k=4),
                                    h_hi[cols].bitcast(F32), ALU.subtract).then_inc(*h_lo_done.tick(i))

                for s in range(ST):
                    if s >= 2:
                        e.wait_ge(*x_turned.at(2 * (s - 2) + 1))
                    e.scalar_tensor_tensor(xn[:, s % 2, :], x_sb[:, s, :], r[:, s:s + 1], gain_row[:, :],
                                           ALU.mult, ALU.mult).then_inc(*xn_ready.tick(s))
                    if s:
                        h_lo_of(2 * s - 2)
                        h_lo_of(2 * s - 1)
                h_lo_of(2 * ST - 2)
                h_lo_of(2 * ST - 1)
                e.wait_ge(*dense.at("ix_k"))
                e.tensor_copy(ix_k[:, :], dbank("ix_k")[:, :]).then_inc(*dve_evac.tick("ix_k"))
                e.wait_ge(*act_evac.at("k_pe"))
                b = dbank("k_pe")
                e.scalar_tensor_tensor(k_rope[64:96, :], b[64:96, :], gain[64:96, 4:5], cos_sin[64:96, :],
                                       ALU.mult, ALU.mult).then_inc(*dve_evac.tick("kr0"))
                e.scalar_tensor_tensor(norm_out[64:96, :], b[96:P, :], gain[96:P, 4:5], cos_sin[96:P, :],
                                       ALU.mult, ALU.mult).then_inc(*dve_evac.tick("k_pe"))
                e.wait_ge(*dve_evac.at("k_pe"))
                e.tensor_tensor(k_rope[64:96, :], k_rope[64:96, :], norm_out[64:96, :], ALU.add).then_inc(*dve_evac.tick("kr"))
                for s in range(ST):
                    b = dbank(f"nat{s}")
                    e.wait_ge(*dense.at(f"nat{s}"))
                    e.tensor_copy(ds_v[:, s, :], b[:, 0:HD]).then_inc(*dve_evac.tick("dv", s))
                    e.tensor_scalar(ix_w[:, s, :], b[:, P:P + HEADS], HEADS ** -0.5, None, ALU.mult
                                    ).then_inc(*dve_evac.tick(f"nat{s}"))
                for j in range(2):
                    e.wait_ge(*dense.at(f"ix_q{j}"))
                    e.tensor_copy(ix_q[:, j, :], dbank(f"ix_q{j}")[:, :]).then_inc(*dve_evac.tick(f"ix_q{j}"))
                units = [(h, t) for h in range(HEADS) for t in range(1, ST)]
                for u, (h, t) in enumerate(units):
                    w = P * (t + 1)
                    dst, src, wt = score[:, OFF[t]:OFF[t] + w], ix_relu[:, u % 3, 0:w], ix_w[:, t, h:h + 1]
                    e.wait_ge(*ix_relu_done.at(u))
                    if h == 0:
                        e.tensor_scalar(dst, src, wt, None, ALU.mult).then_inc(*score_sum.tick(u))
                    else:
                        e.wait_ge(*score_sum.at(u - 3))
                        e.scalar_tensor_tensor(dst, src, wt, dst, ALU.mult, ALU.add).then_inc(*score_sum.tick(u))
                for rnd in range(TOPK // 8):
                    for t in range(1, ST):
                        row, best = score[:, OFF[t]:OFF[t] + P * (t + 1)], stat[:, 32 + 8 * (t - 1):40 + 8 * (t - 1)]
                        if rnd == 0:
                            e.wait_ge(*score_masked.at(t))
                        else:
                            e.wait_ge(*topk.at("replace", rnd - 1, t))
                        e.max(best, row).then_inc(*topk.tick("max", rnd, t))
                    for t in range(1, ST):
                        row, best = score[:, OFF[t]:OFF[t] + P * (t + 1)], stat[:, 32 + 8 * (t - 1):40 + 8 * (t - 1)]
                        e.wait_ge(*topk.at("max", rnd, t))
                        e.match_replace(row, best, row, TAKEN).then_inc(*topk.tick("replace", rnd, t))
                for t in range(1, ST):
                    r = slice(OFF[t], OFF[t] + P * (t + 1))
                    e.wait_ge(*topk.at("replace", TOPK // 8 - 1, t))
                    e.tensor_scalar(chosen[:, r], score[:, r], TAKEN, 1.0, ALU.is_equal, ALU.subtract
                                    ).then_inc(*topk.tick("chosen", t))

                units = [(h, kt) for h in range(HEADS) for kt in reversed(range(ST))]
                fill = ["c_kv", "ds_k", "ds_q0", "ds_q1", "ds_q2", "ds_q3", "c_q0", "c_q1"]
                gain_of = {"c_kv": 0, "ds_k": 6, "c_q0": 1, "c_q1": 2}

                def normed(tile, dst, rs):
                    g = gain_of.get(tile, 5)
                    e.scalar_tensor_tensor(dst, dbank(tile)[:, :], gain[:, g:g + 1], rs, ALU.mult, ALU.mult
                                           ).then_inc(*dve_evac.tick(tile))

                for i in range(len(units) + 5):
                    if i < len(units):
                        w = S - units[i][1] * P
                        e.wait_ge(*stick_z.at(i))
                        if i >= 3:
                            e.wait_ge(*stick_sp.at(i - 3))
                        e.tensor_scalar(soft[:, i % 3, 0:w], bank[2 + i % 4][:, 0:w], STICK_SCALE, CLIP, ALU.mult, ALU.min
                                        ).then_inc(*stick_clip.tick(i))
                    if 0 <= i - 1 < len(units):
                        u = i - 1
                        h, kt = units[u]
                        w = S - kt * P
                        e.wait_ge(*stick_exp.at("ln", u))
                        if h >= 2:
                            e.wait_ge(*stick_sum.at(4 * (h - 2) + 3))
                        e.scalar_tensor_tensor(sp[:, h % 2, SOFF[kt]:SOFF[kt] + w], bank[2 + u % 4][:, 0:w], STICK_SCALE,
                                               soft[:, u % 3, 0:w], ALU.mult, ALU.max).then_inc(*stick_sp.tick(u))
                    k = i // 4
                    if i % 4 == 3 and k < len(fill) and fill[k] != "c_q0":
                        tile = fill[k]
                        e.wait_ge(*act_evac.at(tile + "rs"))
                        if tile == "c_kv":
                            normed(tile, norm_out[:, :], norm_rs[:, :])
                        elif tile == "ds_k":
                            normed(tile, ds_k[:, :], norm_rs[:, :])
                        elif tile == "c_q1":
                            normed("c_q0", cq_out[0][:, :], norm_rs[:, :])
                            normed("c_q1", cq_out[1][:, :], norm_rs[:, :])
                        else:
                            normed(tile, ds_q[:, int(tile[-1]), :], norm_rs[:, :])
                    if i >= 4 and (i - 4) % 8 == 7:
                        pair = (i - 4) // 8
                        e.wait_ge(*pv_done.at("stick", 8 * pair + 7))
                        e.tensor_copy(y[:, pair, :], bank[Y][:, :]).then_inc(*y_out["stick"].tick(pair))

                def head_q(h):
                    e.wait_ge(*act_evac.at(f"qh{h}rs"))
                    if h >= 2:
                        e.wait_ge(*logits.at("mla", 4 * (h - 2) + 3))
                        e.wait_ge(*pool_work.at(f"qh{h - 1}rope"))
                    e.scalar_tensor_tensor(q_head[:, h % 2, :], dbank(f"qh{h}")[:, :], gain[:, 3:4], q_rs[:, :],
                                           ALU.mult, ALU.mult).then_inc(*dve_evac.tick(f"qh{h}"))
                    e.wait_ge(*dve_evac.at(f"qh{h}"))
                    if h:
                        e.wait_ge(*pool_work.at(f"qh{h - 1}rope"))
                    e.tensor_tensor(q_rot[64:96, :], q_head[96:P, h % 2, :], cos_sin[96:P, :], ALU.mult
                                    ).then_inc(*dve_evac.tick(f"qh{h}rot"))

                def head_k(h):
                    e.wait_ge(*act_evac.at(f"kh{h}rs"))
                    if h >= 2:
                        e.wait_ge(*logits.at("mla", 4 * (h - 2) + 3))
                    e.scalar_tensor_tensor(k_head[0:NOPE, h % 2, :], dbank(f"kh{h}")[0:NOPE, :], gain[0:NOPE, 4:5],
                                           k_rs[0:NOPE, :], ALU.mult, ALU.mult).then_inc(*dve_evac.tick(f"kh{h}"))

                def inverse(br, u):
                    e.wait_ge(*probs_exp.at(br, u))
                    if u >= 4:
                        e.wait_ge(*probs_normed.at(br, u - 4))
                    elif br == "dsa":
                        e.wait_ge(*probs_normed.at("mla", len(units) - 4 + u))
                    e.reciprocal(stat[:, 24 + u % 4:25 + u % 4], stat[:, 20 + u % 4:21 + u % 4]).then_inc(*row_inv.tick(br, u))

                units = [(h, t) for h in range(HEADS) for t in range(ST)]
                head_q(0)
                head_k(0)
                for i in range(len(units) + 3):
                    if i < len(units):
                        h, t = units[i]
                        e.wait_ge(*logits.at("mla", i))
                        if i >= 4:
                            e.wait_ge(*probs_exp.at("mla", i - 4))
                        e.tensor_reduce(stat[:, 16 + i % 4:17 + i % 4], bank[2 + i % 2][:, 0:P * (t + 1)], AX_X, ALU.max,
                                        negate=True).then_inc(*row_max.tick("mla", h, t))
                    if 0 <= i - 1 < len(units):
                        inverse("mla", i - 1)
                    if 0 <= i - 2 < len(units):
                        u = i - 2
                        w = P * (units[u][1] + 1)
                        e.wait_ge(*probs_turned.at("mla", u))
                        if u >= 3:
                            e.wait_ge(*pv_done.at("mla", u - 3))
                        e.tensor_copy(probs_t[:, u % 3, 0:w], bank[4 + u % 2][:, 0:w]).then_inc(*probs_t_ready["mla"].tick(u))
                    if i < len(units) and h + 1 < HEADS:
                        if t == 2:
                            head_q(h + 1)
                        if t == 3:
                            head_k(h + 1)
                for i in range(len(units) + 1):
                    if i < len(units):
                        h, t = units[i]
                        w = P * (t + 1)
                        e.wait_ge(*logits.at("dsa", i))
                        if t == 0:
                            e.wait_ge(*bias_in[h % 2].at(h))
                        if i >= 3:
                            e.wait_ge(*probs_turned.at("dsa", i - 3))
                        e.tensor_tensor_reduce(out=probs[:, i % 3, 0:w], in0=bank[2 + i % 2][:, 0:w],
                                               in1=bias[:, h % 2, OFF[t]:OFF[t] + w], scale=1.0, scalar=TAKEN,
                                               op0=ALU.add, op1=ALU.max, accum_out=stat[:, 12 + i % 4:13 + i % 4]
                                               ).then_inc(*row_max.tick("dsa_max", h, t))
                        e.wait_ge(*row_max.at("dsa_max", h, t))
                        if i >= 4:
                            e.wait_ge(*probs_exp.at("dsa", i - 4))
                        e.tensor_scalar(stat[:, 16 + i % 4:17 + i % 4], stat[:, 12 + i % 4:13 + i % 4], -1.0, None, ALU.mult
                                        ).then_inc(*row_max.tick("dsa", h, t))
                    if 0 <= i - 1 < len(units):
                        inverse("dsa", i - 1)
                ups = 0
                for n in range(3):
                    for m in range(4):
                        tile = f"z{n}_{m}"
                        e.wait_ge(*gate_sig.at("z", n, m))
                        zs = z_sig[:, m % 2, :]
                        yt = (y[:, 4 * n + m, :] if n < 2 else y_dsa[:, m, :])
                        e.tensor_tensor(zs, zs, dbank(tile)[:, :], ALU.mult).then_inc(*branch.tick(tile + "z"))
                        e.wait_ge(*branch.at(tile + "z"))
                        if n == 0 and m == 0:
                            e.wait_ge(*y_out["mla"].at(3))
                        if n == 2 and m == 0:
                            e.wait_ge(*y_out["dsa"].at(3))
                        e.tensor_tensor(yt, yt, zs, ALU.mult).then_inc(*branch.tick(tile + "y"))
                        e.wait_ge(*merged_hi.at("br", n, m))
                        e.tensor_tensor(br_lo[:, m, :], yt, br_hi[:, m, :].bitcast(F32), ALU.subtract
                                        ).then_inc(*branch.tick(tile + "lo"))
                    for half in range(2):
                        for m in range(4 * half, 4 * half + 4):
                            e.wait_ge(*up_done.at(ups))
                            e.wait_ge(*gate_sig.at(f"g{n}_{m}"))
                            b = bank[2 + ups % 2]
                            if n == 0:
                                e.tensor_tensor(merged[:, m, :], gate[:, m % 4, :], b[:, :], ALU.mult).then_inc(*merge.tick("sum", ups))
                            else:
                                g = gate[:, m % 4, :]
                                e.tensor_tensor(g, g, b[:, :], ALU.mult).then_inc(*up_gated.tick(ups))
                                e.wait_ge(*up_gated.at(ups))
                                e.tensor_tensor(merged[:, m, :], merged[:, m, :], g, ALU.add).then_inc(*merge.tick("sum", ups))
                            ups += 1
                        if n == 2:
                            for m in range(4 * half, 4 * half + 4):
                                e.wait_ge(*merged_hi.at(m))
                                e.tensor_tensor(m_lo[:, m, :], merged[:, m, :], m_hi[:, m, :].bitcast(F32), ALU.subtract
                                                ).then_inc(*merge.tick("lo", m))
                for c in range(2):
                    for s in range(ST):
                        e.wait_ge(*out_mm.at(c, 1, s))
                        xs = x_sb[:, s, c * S:(c + 1) * S]
                        e.tensor_tensor(xs, xs, bank[2 + s][:, :], ALU.add).then_inc(*x_new.tick(c, s))
                meet(e, l + 2)

        @block.gpsimd
        def _(e):
            meet(e, 1)
            with e.Fori(0, DEPTH) as l:
                def lo(s):
                    split_lo(e, l, SLABS[s])

                lo(0)
                lo(1)
                lo(2)
                n_ix = 3 * HEADS
                for t in range(1, ST):
                    e.wait_ge(*score_sum.at(n_ix - 4 + t))
                    d = score[:, OFF[t] + P * t:OFF[t] + P * (t + 1)]
                    e.affine_select(out=d, in_=d, pattern=[[-1, P]], compare_op=ALU.is_ge, fill=MASKED, base=0,
                                    channel_multiplier=1).then_inc(*score_masked.tick(t))
                for s in range(3, 10):
                    lo(s)
                units = [(h, kt) for h in range(HEADS) for kt in reversed(range(ST))]
                for i in range(len(units) + 4):
                    if 0 <= i - 1 < len(units):
                        u = i - 1
                        h, kt = units[u]
                        d = sp[:, h % 2, SOFF[kt]:SOFF[kt] + P]
                        e.wait_ge(*stick_sp.at(u))
                        e.affine_select(out=d, in_=d, pattern=[[1, P]], compare_op=ALU.is_gt, fill=0.0, base=0,
                                        channel_multiplier=-1).then_inc(*sp_masked.tick(u))
                    if 0 <= i - 2 < len(units):
                        u = i - 2
                        d = stick_a[:, u % 2, 0:P]
                        e.wait_ge(*stick_prob.at(u))
                        e.affine_select(out=d, in_=d, pattern=[[1, P]], compare_op=ALU.is_gt, fill=0.0, base=0,
                                        channel_multiplier=-1).then_inc(*prob_masked.tick(u))
                    k = i // 4
                    if i % 4 == 2 and k < 8 and k % 2:
                        lo(10 + k // 2)
                    if i == 5:
                        e.wait_ge(*act_evac.at("ckv_hi"))
                        e.tensor_tensor(ckv_lo[:, :], norm_out[:, :], ckv_hi[:, :].bitcast(F32), ALU.subtract
                                        ).then_inc(*pool_work.tick("ckv_lo"))
                    if i == 34:
                        for c in range(2):
                            e.wait_ge(*act_evac.at(f"cq_hi{c}"))
                            e.tensor_tensor(cq_lo[:, c, :], cq_out[c][:, :], cq_hi[:, c, :].bitcast(F32), ALU.subtract
                                            ).then_inc(*pool_work.tick(f"c_q{c}lo"))

                def rope_q(h):
                    e.wait_ge(*dve_evac.at(f"qh{h}rot"))
                    qr = q_head[64:96, h % 2, :]
                    e.tensor_tensor(qr, qr, cos_sin[64:96, :], ALU.mult).then_inc(*pool_work.tick(f"qh{h}cos"))
                    e.wait_ge(*pool_work.at(f"qh{h}cos"))
                    e.tensor_tensor(qr, qr, q_rot[64:96, :], ALU.add).then_inc(*pool_work.tick(f"qh{h}rope"))

                def rope_k(h):
                    e.wait_ge(*act_evac.at(f"kh{h}rs"))
                    if h >= 2:
                        e.wait_ge(*logits.at("mla", 4 * (h - 2) + 3))
                    e.tensor_tensor(k_head[64:96, h % 2, :], k_rope[64:96, :], k_rs[64:96, :], ALU.mult
                                    ).then_inc(*pool_work.tick(f"kh{h}rope"))

                def norm_probs(br, u):
                    w = P * (units[u][1] + 1)
                    e.wait_ge(*row_inv.at(br, u))
                    e.tensor_scalar(probs[:, u % 3, 0:w], probs[:, u % 3, 0:w], stat[:, 24 + u % 4:25 + u % 4], 1.0,
                                    ALU.mult, ALU.mult).then_inc(*probs_normed.tick(br, u))

                units = [(h, t) for h in range(HEADS) for t in range(ST)]
                e.wait_ge(*pool_work.at("c_q1lo"))
                rope_q(0)
                rope_k(0)
                e.wait_ge(*pool_work.at("kh0rope"))
                for i in range(1, len(units) + 1):
                    norm_probs("mla", i - 1)
                    if i < len(units):
                        h, t = units[i]
                        if h + 1 < HEADS and t >= 2:
                            e.wait_ge(*probs_normed.at("mla", i - 1))
                            if t == 2:
                                rope_q(h + 1)
                                e.wait_ge(*pool_work.at(f"qh{h + 1}rope"))
                            else:
                                rope_k(h + 1)
                                e.wait_ge(*pool_work.at(f"kh{h + 1}rope"))
                lo(SLAB_NO["z0_0"])
                lo(SLAB_NO["z0_1"])
                for i in range(1, len(units) + 1):
                    norm_probs("dsa", i - 1)
                for s in range(SLAB_NO["z0_1"] + 1, NS):
                    lo(s)
                meet(e, l + 2)
    return {n: s.events for n, s in signals.items()}


_INS = ["x", "positions", "norm_g", "w_in", "mla_q_norm_g", "mla_kv_norm_g", "mla_w_uq", "mla_w_ukv",
        "mla_q_g", "mla_k_g", "dsa_q_g", "dsa_k_g", "rel_bias", "gate_b", "w_branch", "w_out"]


def program(nc, arrays, known):
    args = [nc.dram_tensor(n, a.shape, mybir.dt.from_np(a.dtype), kind="ExternalInput").ap() for n, a in arrays.items()]
    out = nc.dram_tensor("out_dram", (1, S, D), F32, kind="ExternalOutput").ap()
    bias_dram = nc.dram_tensor("bias_dram", (HEADS, S, S), F32).ap()
    return build(nc, *args, out, bias_dram, known)


def kernel(**inputs):
    import concourse.bacc as bacc
    from concourse.bass_utils import run_bass_kernel_spmd

    arrays = {f"in_{n}": np.ascontiguousarray(inputs[n]) for n in _INS}
    arrays["in_consts"] = constants()
    known = program(bacc.Bacc("TRN2", target_bir_lowering=False, num_devices=1), arrays, {})
    nc = bacc.Bacc("TRN2", target_bir_lowering=False, num_devices=1)
    program(nc, arrays, known)
    r = run_bass_kernel_spmd(nc, [arrays], core_ids=[0])
    return r.results[0]["out_dram"]
```

```python
from contextlib import ExitStack
import math

import numpy as np
import concourse.bass as bass
from concourse import mybir

ALU = mybir.AluOpType
ACT = mybir.ActivationFunctionType
F32 = mybir.dt.float32
F32R = mybir.dt.float32r
BF16 = mybir.dt.bfloat16
I32 = mybir.dt.int32
AX_X = mybir.AxisListType.X

P = 128
D = 1024
S = 512
DEPTH = 2
KT = D // P
ST = S // P
HEADS = 8
HD = 64
NOPE, ROPE = 64, 32
QK = NOPE + ROPE
Q_LORA, KV_LORA = 256, 128
IDX_DIM = 32
TOPK = min(256, S // 4)
BUCKETS, MAX_DIST = 32, 128
BW = 512
EPS = 1e-6
THETA = 10000.0

SIZES = dict(sa_q=512, sa_k=512, sa_v=512, c_q=Q_LORA, c_kv=KV_LORA, k_pe=ROPE, ds_q=512, ds_k=HD,
             ds_v=HD, ix_q=HEADS * IDX_DIM, ix_k=IDX_DIM, ix_w=HEADS, z=3 * BW, g=3 * D)
COL = {}
_at = 0
for _n, _w in SIZES.items():
    COL[_n] = _at
    _at += _w
D_IN = _at

SLAB = 264
MASKED = -1e30
TAKEN = -3e38
CLIP = 30.0
STICK_SCALE = HD ** -0.5
OFF = [P * (t * (t + 1) // 2) for t in range(ST)]
SOFF = [P * (t * ST - t * (t - 1) // 2) for t in range(ST)]
STRIPS = P * ST * (ST + 1) // 2


def bucket_thresholds():
    exact = BUCKETS // 2
    n = np.arange(1, 4 * MAX_DIST)
    large = exact + (np.log(n / exact) / math.log(MAX_DIST / exact) * (BUCKETS - exact) + 1e-9).astype(int)
    bucket = np.where(n < exact, n, np.minimum(large, BUCKETS - 1))
    least = [-float(2 ** 26)] + [float(n[np.argmax(bucket >= b)]) for b in range(1, BUCKETS)]
    return np.array(least, np.float32)


def constants():
    r = np.arange(P)
    eye = np.eye(P)
    suffix = np.where(r[:, None] >= r[None, :], -1.0 / STICK_SCALE, 0.0)
    all_later = np.full((P, P), -1.0 / STICK_SCALE)
    ones = np.ones((P, P))
    per_head = (r[:, None] // HD == r[None, :] // HD) * 1.0
    first_qk = (r[:, None] < QK) * np.ones((P, P))
    big_eye = eye * -MASKED
    causal = np.where(r[None, :] > r[:, None], -1.0, 0.0)
    mats = np.concatenate([eye, suffix, all_later, ones, per_head, first_qk, big_eye, causal], 1)
    half = ROPE // 2
    inv = (np.float32(THETA) ** (-(np.arange(half, dtype=np.float32) * np.float32(2.0)) / np.float32(ROPE))).astype(np.float32)
    cols = np.zeros((P, 4))
    cols[:, 0] = np.tile(bucket_thresholds(), P // BUCKETS)
    cols[64:, 1] = np.tile(inv, 4)
    cols[64:96, 2] = math.pi / 2
    cols[64:, 3] = 1.0
    cols[96:112, 3] = -1.0
    return np.concatenate([mats, cols], 1).astype(np.float32)


N_MATS = 8


def slab_plan():
    plan = ["small", "ix_q", "sa_q0", "sa_q1", "sa_k0", "sa_k1", "sa_v0", "sa_v1",
            "ckv_dsk", "ds_q0", "ds_q1", "c_q", "uq", "ukv"]
    for n in range(3):
        plan += [f"z{n}_0", f"z{n}_1"]
        for half in range(2):
            plan += [f"g{n}_{2 * half}", f"g{n}_{2 * half + 1}", f"up{n}_{half}"]
    plan += [f"out{c}_{j}" for c in range(2) for j in range(2)]
    return plan


SLABS = slab_plan()
NS = len(SLABS)
SLAB_NO = {n: i for i, n in enumerate(SLABS)}
RAW, RING = 2, 2
N_SOFT = 2 * HEADS * ST
S_RING, T_RING = 2, 2
T_LAG, AV_LAG = 3, 5
DVE_SLABS = SLABS[10:14]
PR, PTR = 4, 4
SPLIT_Z = N_SOFT // 2 + 4
N_GAINS = 7


class Signal:

    def __init__(self, sem, name, known):
        self.sem, self.name, self.known = sem, name, known
        self.n, self.events = 0, {}

    def tick(self, *event, by=1):
        self.n += by
        self.events[event] = self.n
        return self.sem, by

    def at(self, *event):
        return self.sem, self.known[self.name][event] if self.name in self.known else 1


def build(nc, x, positions, norm_g, w_in, q_norm_g, kv_norm_g, w_uq, w_ukv, mla_q_g, mla_k_g,
          dsa_q_g, dsa_k_g, rel_bias, gate_b, w_branch, w_out, consts, out, bias_dram, known):
    signals = {}
    ctx = ExitStack()
    with ctx:
        def signal(name):
            signals[name] = Signal(ctx.enter_context(nc.semaphore(name)), name, known)
            return signals[name]

        arena_bytes = 207 * 1024
        arena_base = (nc.sbuf_base + 63) // 64 * 64
        ctx.enter_context(nc.sbuf_tensor("arena", [P, arena_bytes // 4], F32))
        base = arena_base
        cursor = [base]

        def place(name, shape, dt, at=None):
            size = int(np.prod(shape[1:])) * (2 if dt == BF16 else 4)
            size = (size + 31) // 32 * 32
            if at is None:
                at = cursor[0]
                cursor[0] += size
                assert cursor[0] <= base + arena_bytes, (name, cursor[0] - base)
            return nc.alloc_sbuf_tensor_at(name, shape, dt, offset=at), at + size

        def sb(name, shape, dt=F32):
            return place(name, shape, dt)[0]

        mats = sb("mats", [P, N_MATS * P + 4])
        eye, suffix, all_later, ones, per_head, first_qk, big_eye_f, causal_f = (
            mats[:, i * P:(i + 1) * P] for i in range(N_MATS))
        thr, inv_freq, phase, sign = (mats[:, N_MATS * P + i:N_MATS * P + i + 1] for i in range(4))
        big_eye = sb("big_eye", [P, P], BF16)
        causal = sb("causal", [P, P], BF16)
        cos_sin = sb("cos_sin", [P, S])
        k_rope = sb("k_rope", [P, S])
        k_sq = sb("k_sq", [P, S])
        gain = sb("gain", [P, N_GAINS + 3 * KT])
        gains = sb("gains", [P, DEPTH, N_GAINS + 3 * KT])
        stat = sb("stat", [P, 64])
        x_sb = sb("x_sb", [P, ST, D])
        h_hi = sb("h_hi", [P, KT, S], F32R)
        h_lo = sb("h_lo", [P, KT, S], F32R)
        raw = sb("raw", [P, RAW, KT * SLAB])
        w_hi = sb("w_hi", [P, RING, KT * SLAB], F32R)
        w_lo = sb("w_lo", [P, RING, KT * SLAB], F32R)
        y_at = cursor[0]
        y = sb("y", [P, 8, S])
        xn = place("xn", [P, 2, D], F32, y_at)[0]
        x_sq = place("x_sq", [P, D], F32, y_at + 8192)[0]
        u_at = cursor[0]
        ds_q = sb("ds_q", [P, 4, S])
        ds_k = sb("ds_k", [P, S])
        ds_v = sb("ds_v", [P, ST, HD])
        ix_w = sb("ix_w", [P, ST, HEADS])
        score = sb("score", [P, STRIPS])
        chosen = sb("chosen", [P, STRIPS], BF16)
        sa_q_at = cursor[0]
        sa_q = sb("sa_q", [P, 4, S])
        sa_k = sb("sa_k", [P, 4, S])
        sa_v_at = cursor[0]
        sa_v = sb("sa_v", [P, ST, BW])
        q_head, at = place("q_head", [P, 2, S], F32, sa_q_at)
        k_head, at = place("k_head", [P, 2, S], F32, at)
        q_sq, at = place("q_sq", [P, S], F32, at)
        q_rs, at = place("q_rs", [P, S], F32, at)
        k_rs, at = place("k_rs", [P, S], F32, at)
        v_b = place("v_b", [P, ST, BW], F32, sa_v_at)[0]
        y_dsa = place("y_dsa", [P, 4, S], F32, sa_v_at)[0]
        lora_at = cursor[0]
        cq_hi = sb("cq_hi", [P, 2, S], F32R)
        cq_lo = sb("cq_lo", [P, 2, S], F32R)
        ckv_hi = sb("ckv_hi", [P, S], F32R)
        ckv_lo = sb("ckv_lo", [P, S], F32R)
        bias = place("bias", [P, 2, STRIPS], F32, lora_at)[0]
        norm_sq = sb("norm_sq", [P, S])
        norm_rs = sb("norm_rs", [P, S])
        norm_out = sb("norm_out", [P, S])
        cq_out = [norm_out, norm_sq]
        tmp_at = cursor[0]
        soft, at = place("soft", [P, 3, S], F32, tmp_at)
        sp, at = place("sp", [P, 2, STRIPS], F32, at)
        gain_row = place("gain_row", [P, D], F32, at)[0]
        stick_a, end = place("stick_a", [P, 2, S], F32, at)
        probs, at = place("probs", [P, PR, S], F32, tmp_at)
        probs_t, at = place("probs_t", [P, PTR, S], F32, at)
        ix_q, at = place("ix_q_sb", [P, 2, S], F32, tmp_at)
        ix_k, at = place("ix_k_sb", [P, S], F32, at)
        ix_relu, at = place("ix_relu", [P, 3, S], F32, at)
        cursor[0] = end
        assert cursor[0] <= base + arena_bytes, cursor[0] - base
        br_hi, at = place("br_hi", [P, 4, S], F32R, u_at)
        br_lo, at = place("br_lo", [P, 4, S], F32R, at)
        merged, at = place("merged", [P, KT, S], F32, at)
        assert at <= sa_v_at, (at, sa_v_at)
        gate, at = place("gate", [P, 4, S], F32, sa_v_at + 4 * S * 4)
        z_sig, at = place("z_sig", [P, 2, S], F32, at)
        m_lo, at = place("m_lo", [P, KT, S], F32R, at)
        assert at <= base + arena_bytes, at - base
        m_hi = place("m_hi", [P, KT, S], F32R, y_at)[0]
        pos_i = place("pos_i", [P, S], I32, u_at)[0]
        pos_f = place("pos_f", [P, S], F32, u_at + 2048)[0]
        edge = place("edge", [P, P], F32, u_at + 4096)[0]
        step = place("step", [P, 4, P // 4], F32, u_at + 8192)[0]
        step_f = place("step_w", [P, 32], F32, u_at + 10240)[0]
        prev_f = place("prev_w", [P, 32], F32, u_at + 11264)[0]
        reach = place("reach", [P, 8, S], F32, y_at)[0]
        bias_out = place("bias_out", [P, 2, S], F32, u_at + 12288)[0]
        ang = place("ang", [P, S], F32, u_at + 16384)[0]
        turns = place("turns", [P, S], F32, u_at + 18432)[0]

        bank = [ctx.enter_context(nc.psum_tensor(f"bank{i}", [P, S], F32)) for i in range(8)]
        NORM, Y = 6, 7

        consts_in = signal("consts_in")
        pos_in = signal("pos_in")
        x_in = signal("x_in")
        setup_dve = signal("setup_dve")
        cos_done = signal("cos_done")
        reach_ready = signal("reach_ready")
        bias_mm = signal("bias_mm")
        bias_evac = signal("bias_evac")
        bias_stored = [signal(f"bias_stored{i}") for i in range(2)]
        gains_in = signal("gains_in")
        gain_row_in = signal("gain_row_in")
        raw_in = [signal(f"raw_in{i}") for i in range(RAW)]
        raw_used = signal("raw_used")
        dve_split = signal("dve_split")
        hi_ready = signal("hi_ready")
        x_stat = signal("x_stat")
        dve_stat = signal("dve_stat")
        xn_ready = signal("xn_ready")
        x_turned = signal("x_turned")
        h_hi_done = signal("h_hi_done")
        h_lo_done = signal("h_lo_done")
        dense = signal("dense")
        act_evac = signal("act_evac")
        dve_evac = signal("dve_evac")
        pool_work = signal("pool_work")
        norm_sum = signal("norm_sum")
        ix_mm = signal("ix_mm")
        ix_relu_done = signal("ix_relu_done")
        score_sum = signal("score_sum")
        score_masked = signal("score_masked")
        topk = signal("topk")
        stick_z = signal("stick_z")
        stick_clip = signal("stick_clip")
        stick_exp = signal("stick_exp")
        stick_sp = signal("stick_sp")
        sp_masked = signal("sp_masked")
        stick_sum = signal("stick_sum")
        stick_prob = signal("stick_prob")
        prob_masked = signal("prob_masked")
        pv_done = signal("pv_done")
        y_out = {br: signal(f"y_out_{br}") for br in ("stick", "mla", "dsa")}
        logits = signal("logits")
        row_max = signal("row_max")
        probs_exp = signal("probs_exp")
        row_inv = signal("row_inv")
        probs_normed = signal("probs_normed")
        probs_turned = signal("probs_turned")
        probs_t_ready = {br: signal(f"probs_t_ready_{br}") for br in ("mla", "dsa")}
        bias_in = [signal(f"bias_in{i}") for i in range(2)]
        gate_sig = signal("gate_sig")
        branch = signal("branch")
        up_done = signal("up_done")
        up_gated = signal("up_gated")
        merge = signal("merge")
        merged_hi = signal("merged_hi")
        out_mm = signal("out_mm")
        x_new = signal("x_new")
        stored = signal("stored")

        arrived = ctx.enter_context(nc.semaphore("arrived"))
        cleared = ctx.enter_context(nc.semaphore("cleared"))

        def clear_signals(e):
            e.sem_clear(arrived)
            for s in signals.values():
                e.sem_clear(s.sem)

        def meet(e, n):
            e.drain().then_inc(arrived, 1)
            e.wait_ge(cleared, n)

        dense_tiles = (["ix_k", "k_pe"] + [f"nat{s}" for s in range(ST)] + ["ix_q0", "ix_q1"]
                       + [f"sa_q{j}" for j in range(4)] + [f"sa_k{j}" for j in range(4)]
                       + ["c_kv", "ds_k"] + [f"ds_q{j}" for j in range(4)] + ["c_q0", "c_q1"]
                       + [f"v_b{s}" for s in range(ST)]
                       + [f"{a}{h}" for h in range(HEADS) for a in ("qh", "kh")])
        for n in range(3):
            dense_tiles += [f"z{n}_{m}" for m in range(4)]
            for half in range(2):
                dense_tiles += [f"g{n}_{4 * half + m}" for m in range(4)]
        TILE = {t: i for i, t in enumerate(dense_tiles)}

        def dbank(tile):
            return bank[TILE[tile] % 2]

        def reader(tile):
            if tile.startswith(("sa_q", "sa_k", "v_b")):
                return act_evac, tile
            if tile.startswith("g"):
                return gate_sig, tile
            if tile.startswith("z"):
                return branch, tile + "z"
            return dve_evac, tile

        def hslab(name, kt, a, b, hi=True, width=2 * P):
            t = w_hi if hi else w_lo
            return t[:, SLAB_NO[name] % RING, kt * width + a:kt * width + b]

        def br_split(e, l, n, m):
            yt = (y[:, 4 * n + m, :] if n < 2 else y_dsa[:, m, :])
            e.wait_ge(*branch.at(f"z{n}_{m}y"))
            if n and m == 0:
                e.wait_ge(*up_done.at(8 * n - 1))
            e.copy(br_hi[:, m, :], yt).then_inc(*merged_hi.tick("br", n, m))

        def lo_signal(name):
            return dve_split if name in DVE_SLABS else raw_used

        block = ctx.enter_context(nc.Block())

        @block.sync
        def _(sp_eng):
            e = sp_eng
            e.dma_start(mats[:], consts).then_inc(*consts_in.tick("mats", by=16))
            e.dma_start(pos_i[:], positions[0:1, :].to_broadcast([P, S])).then_inc(*pos_in.tick("pos", by=16))
            e.wait_ge(*setup_dve.at("steps_zero"))
            for qq in range(4):
                e.dma_start(step_f[32 * qq:32 * qq + 32, 8 * qq:8 * qq + 8], rel_bias).then_inc(*pos_in.tick("rb", qq, by=16))
                e.dma_start(prev_f[32 * qq + 1:32 * qq + 32, 8 * qq:8 * qq + 8],
                            rel_bias[0:BUCKETS - 1, :]).then_inc(*pos_in.tick("rbp", qq, by=16))
            for s in range(ST):
                e.dma_start(x_sb[:, s, :], x[0, s * P:(s + 1) * P, :]).then_inc(*x_in.tick("x", s, by=16))
            for G in range(S // 16):
                w = P * (G // 8 + 1)
                e.wait_ge(*bias_evac.at(G))
                e.dma_start(bias_dram[:, 16 * G:16 * G + 16, 0:w].rearrange("h q k -> q h k"),
                            bias_out[:, G % 2, 0:w]).then_inc(*bias_stored[G % 2].tick(G, by=16))

            def pieces(name, l):
                slot = raw[:, SLAB_NO[name] % RAW, :]
                wl = w_in[l].rearrange("(c p) n -> p c n", p=P)

                def cols(view, a, col, n):
                    return view[:, :, a:a + n], wl[:, :, col:col + n]

                v8 = slot[:, 0:KT * SLAB].rearrange("p (c n) -> p c n", c=KT)
                v256 = slot[:, 0:KT * 2 * P].rearrange("p (c n) -> p c n", c=KT)
                v512 = slot[:, 0:4 * S].rearrange("p (c n) -> p c n", c=4)
                if name == "small":
                    return ([cols(v8, 32 * i, COL["ix_k"], 32) for i in range(4)]
                            + [cols(v8, 128, COL["ds_v"], HD), cols(v8, 192, COL["k_pe"], 32),
                               cols(v8, 224, COL["k_pe"] + 16, 16), cols(v8, 240, COL["k_pe"], 16),
                               cols(v8, 256, COL["ix_w"], HEADS)])
                if name == "ckv_dsk":
                    return [cols(v256, 0, COL["c_kv"], P), cols(v256, P, COL["ds_k"], HD),
                            cols(v256, P + HD, COL["ds_k"], HD)]
                if name == "uq":
                    v = slot[:, 0:2 * 8 * P].rearrange("p (c h n) -> p c h n", c=2, h=HEADS)
                    src = w_uq[l].rearrange("(c p) (h n) -> p c h n", p=P, h=HEADS)
                    return [r for c in range(2) for r in (
                        (v[:, c, :, 0:QK], src[:, c, :, :]),
                        (v[:, c, :, QK:QK + 16], src[:, c, :, NOPE + 16:QK]),
                        (v[:, c, :, QK + 16:P], src[:, c, :, NOPE:NOPE + 16]))]
                if name == "ukv":
                    return [(slot[:, 0:HEADS * P], w_ukv[l])]
                if name.startswith("sa_v"):
                    j = int(name[-1])
                    return [(v512, wl[:, 4 * j:4 * j + 4, COL["sa_v"]:COL["sa_v"] + BW])]
                if name.startswith("up"):
                    n, half = int(name[2]), int(name[4])
                    return [(v512, w_branch[l, n].rearrange("(c p) n -> p c n", p=P)[:, :, half * S:(half + 1) * S])]
                if name.startswith("out"):
                    c, j = int(name[3]), int(name[5])
                    return [(v512, w_out[l].rearrange("(c p) n -> p c n", p=P)[:, 4 * j:4 * j + 4, c * S:(c + 1) * S])]
                if name[0] in "zg":
                    n, j = int(name[1]), int(name[3])
                    col = COL[name[0]] + n * (BW if name[0] == "z" else D) + 2 * P * j
                elif name in ("ix_q", "c_q"):
                    col = COL[name]
                else:
                    col = COL[name[:-1]] + 2 * P * int(name[-1])
                return [cols(v256, 0, col, 2 * P)]

            for i in range(2):
                e.wait_ge(*bias_stored[i].at(S // 16 - 2 + i))
            e.wait_ge(arrived, 4)
            clear_signals(e)
            e.sem_inc(cleared, 1)
            with e.Fori(0, DEPTH) as l:
                def load(name):
                    if SLAB_NO[name] >= RAW:
                        last = SLABS[SLAB_NO[name] - RAW]
                        e.wait_ge(*lo_signal(last).at(last))
                    for dst, src in pieces(name, l):
                        e.dma_start(dst, src).then_inc(*raw_in[SLAB_NO[name] % RAW].tick(name, by=16))

                e.dma_start(gain_row[:], norm_g[bass.ds(l, 1), :].to_broadcast([P, D])).then_inc(*gain_row_in.tick("row", by=16))
                for name in SLABS[:SLAB_NO["ukv"] + 1]:
                    load(name)
                load("z0_0")
                load("z0_1")
                for h in range(HEADS):
                    if h >= 2:
                        e.wait_ge(*row_max.at(N_SOFT // 2 + 4 * (h - 2) + ST - 1))
                    else:
                        e.wait_ge(*dense.at(f"kh{HEADS - 1}"))
                    for t in range(ST):
                        e.dma_start(bias[:, h % 2, OFF[t]:OFF[t] + P * (t + 1)],
                                    bias_dram[h, t * P:(t + 1) * P, 0:P * (t + 1)]
                                    ).then_inc(*bias_in[h % 2].tick(h, by=16))
                for name in SLABS[SLAB_NO["z0_1"] + 1:]:
                    load(name)
                e.wait_ge(arrived, 4)
                clear_signals(e)
                e.sem_inc(cleared, 1)
            for s in range(ST):
                e.dma_start(out[0, s * P:(s + 1) * P, :], x_sb[:, s, :]).then_inc(stored.sem, 16)
            e.wait_ge(stored.sem, 16 * ST)

        def slab_size(name):
            if name == "small":
                return KT * SLAB
            if name == "ukv":
                return HEADS * P
            return KT * 2 * P

        def last_use(name):
            if name == "small":
                return dense, (f"nat{ST - 1}",)
            if name.startswith("sa_v"):
                return dense, ("sa_v", int(name[-1]), ST - 1)
            if name == "ckv_dsk":
                return dense, ("ds_k",)
            if name in ("ix_q", "c_q"):
                return dense, (f"{name}1",)
            if name == "uq":
                return dense, (f"qh{HEADS - 1}",)
            if name == "ukv":
                return dense, (f"kh{HEADS - 1}",)
            if name.startswith("up"):
                return up_done, (8 * int(name[2]) + 4 * int(name[4]) + 3,)
            if name.startswith("out"):
                return out_mm, (int(name[3]), int(name[5]), ST - 1)
            if name[0] in "zg":
                return dense, (f"{name[0]}{name[1]}_{2 * int(name[3]) + 1}",)
            return dense, (f"{name[:-1]}{2 * int(name[-1]) + 1}",)

        def gated(u):
            return (merge, ("sum", u)) if u < KT else (up_gated, (u,))

        def wait_ring_slot(e, name):
            s = SLAB_NO[name]
            if s >= RING:
                sig, event = last_use(SLABS[s - RING])
                e.wait_ge(*sig.at(*event))

        def split_hi(e, name, part=None):
            s, n = SLAB_NO[name], slab_size(name)
            a, b = (0, n) if part is None else (part * n // 2, (part + 1) * n // 2)
            if not part:
                e.wait_ge(*raw_in[s % RAW].at(name))
                wait_ring_slot(e, name)
            e.copy(w_hi[:, s % RING, a:b], raw[:, s % RAW, a:b]).then_inc(*hi_ready.tick(name, part or 0))

        def split_lo(e, name, part=None):
            s, n = SLAB_NO[name], slab_size(name)
            a, b = (0, n) if part is None else (part * n // 2, (part + 1) * n // 2)
            e.wait_ge(*hi_ready.at(name, part or 0))
            e.tensor_tensor(w_lo[:, s % RING, a:b], raw[:, s % RAW, a:b],
                            w_hi[:, s % RING, a:b].bitcast(F32), ALU.subtract).then_inc(*lo_signal(name).tick(name))

        soft_units = [(br, h, t) for br in ("mla", "dsa") for h in range(HEADS) for t in range(ST)]

        def s_bank(u):
            return bank[2 + u % S_RING]

        def t_bank(u):
            return bank[2 + S_RING + u % T_RING]

        def turned_copied(u):
            return probs_t_ready[soft_units[u][0]].at(u)

        @block.tensor
        def _(pe):
            pe.wait_ge(*consts_in.at("mats"))
            for G in range(S // 16):
                w = P * (G // 8 + 1)
                if G >= 2:
                    pe.wait_ge(*bias_evac.at(G - 2))
                for g4 in range(4):
                    g = 4 * G + g4
                    pe.wait_ge(*reach_ready.at(g))
                    mm = pe.matmul(bank[G % 2][32 * g4:32 * g4 + 32, 0:w], step_f[:, 0:32],
                                   reach[:, g % 8, 0:w], start=True, stop=True)
                    mm.then_inc(*bias_mm.tick(g))
            meet(pe, 1)
            with pe.Fori(0, DEPTH) as l:
                def use(name):
                    pe.wait_ge(*lo_signal(name).at(name))

                def tile_bank(tile):
                    i = TILE[tile]
                    if i >= 2:
                        sig, key = reader(dense_tiles[i - 2])
                        pe.wait_ge(*sig.at(key))
                    return bank[i % 2]

                def three(out_ap, terms, start=True, stop=True):
                    n = len(terms)
                    for i, (lh, ll, rh, rl) in enumerate(terms):
                        pe.matmul(out_ap, lh, rh, start=start and i == 0, stop=False)
                        pe.matmul(out_ap, lh, rl, start=False, stop=False)
                        mm = pe.matmul(out_ap, ll, rh, start=False, stop=stop and i == n - 1)
                    return mm

                def project(tile, name, a, m, width=2 * P):
                    b = tile_bank(tile)
                    return three(b[0:m, :], [(hslab(name, k, a, a + m, True, width), hslab(name, k, a, a + m, False, width),
                                              h_hi[:, k, :], h_lo[:, k, :]) for k in range(KT)])

                for s in range(ST):
                    for j in range(2):
                        i = 2 * s + j
                        if j == 0:
                            pe.wait_ge(*xn_ready.at(s))
                        if i >= 2:
                            pe.wait_ge(*h_lo_done.at(i - 2))
                        for k in range(4):
                            mm = pe.transpose(bank[i % 2][:, k * P:(k + 1) * P],
                                              xn[:, s % 2, (4 * j + k) * P:(4 * j + k + 1) * P], eye)
                        mm.then_inc(*x_turned.tick(i))
                pe.wait_ge(*h_lo_done.at(7))
                use("small")
                project("ix_k", "small", 0, P, SLAB).then_inc(*dense.tick("ix_k"))
                project("k_pe", "small", P, P, SLAB).then_inc(*dense.tick("k_pe"))
                for s in range(ST):
                    b = tile_bank(f"nat{s}")
                    q = slice(s * P, (s + 1) * P)
                    mm = three(b[:, 0:136], [(h_hi[:, k, q], h_lo[:, k, q], hslab("small", k, P, SLAB, True, SLAB),
                                              hslab("small", k, P, SLAB, False, SLAB)) for k in range(KT)])
                    mm.then_inc(*dense.tick(f"nat{s}"))
                use("ix_q")
                for j in range(2):
                    project(f"ix_q{j}", "ix_q", j * P, P).then_inc(*dense.tick(f"ix_q{j}"))
                pe.wait_ge(*dve_evac.at("ix_q1"))
                units = [(h, t) for h in range(HEADS) for t in range(1, ST)]
                for u, (h, t) in enumerate(units):
                    if u >= 4:
                        pe.wait_ge(*ix_relu_done.at(u - 4))
                    r = slice(IDX_DIM * (h % 4), IDX_DIM * (h % 4) + IDX_DIM)
                    pe.matmul(bank[2 + u % 4][:, 0:P * (t + 1)], ix_q[r, h // 4, t * P:(t + 1) * P],
                              ix_k[r, 0:P * (t + 1)], start=True, stop=True).then_inc(*ix_mm.tick(u))
                for part in ("sa_q", "sa_k"):
                    for j in range(4):
                        if j % 2 == 0:
                            use(f"{part}{j // 2}")
                        project(f"{part}{j}", f"{part}{j // 2}", (j % 2) * P, P).then_inc(*dense.tick(f"{part}{j}"))
                pe.wait_ge(*ix_relu_done.at(len(units) - 1))
                for j in range(2):
                    use(f"sa_v{j}")
                    for s in range(ST):
                        q = slice(s * P, (s + 1) * P)
                        mm = three(bank[2 + s][:, :],
                                   [(h_hi[:, 4 * j + k, q], h_lo[:, 4 * j + k, q], hslab(f"sa_v{j}", k, 0, S, True, S),
                                     hslab(f"sa_v{j}", k, 0, S, False, S)) for k in range(4)],
                                   start=j == 0, stop=j == 1)
                        mm.then_inc(*dense.tick("sa_v", j, s))
                pe.wait_ge(*act_evac.at("sa_k3"))

                units = [(h, kt) for h in range(HEADS) for kt in reversed(range(ST))]
                fill = ["c_kv", "ds_k", "ds_q0", "ds_q1", "ds_q2", "ds_q3", "c_q0", "c_q1"]
                place_of = {"c_kv": ("ckv_dsk", 0), "ds_k": ("ckv_dsk", P), "c_q0": ("c_q", 0), "c_q1": ("c_q", P)}
                for j in range(4):
                    place_of[f"ds_q{j}"] = (f"ds_q{j // 2}", (j % 2) * P)

                def norm(tile, weights, src, start=True, stop=True, k=P):
                    mm = pe.matmul(bank[NORM][:, :], weights[0:k, :], src[0:k, :], start=start, stop=stop)
                    mm.then_inc(*norm_sum.tick(tile))

                def z_of(u):
                    h, kt = units[u]
                    b, w, r = bank[2 + u % 4], S - kt * P, slice(HD * (h % 2), HD * (h % 2) + HD)
                    if u >= 4:
                        pe.wait_ge(*stick_prob.at(u - 4))
                    elif u < 4:
                        pe.wait_ge(*act_evac.at("sa_v", u))
                    pe.matmul(b[:, 0:w], sa_k[r, h // 2, kt * P:(kt + 1) * P], sa_q[r, h // 2, kt * P:S],
                              start=True, stop=True).then_inc(*stick_z.tick(u))

                def suffix_of(u):
                    h, kt = units[u]
                    b, w = bank[2 + u % 4], S - kt * P
                    pe.wait_ge(*sp_masked.at(u))
                    pe.matmul(b[:, 0:w], suffix, sp[:, h % 2, SOFF[kt]:SOFF[kt] + w], start=False,
                              stop=kt == ST - 1, skip_group_check=True)
                    mm = None
                    for later in range(kt + 1, ST):
                        wl = S - later * P
                        mm = pe.matmul(b[:, (later - kt) * P:w], all_later, sp[:, h % 2, SOFF[later]:SOFF[later] + wl],
                                       start=False, stop=later == ST - 1, skip_group_check=True)
                    return mm

                def pv_of(u):
                    h, kt = units[u]
                    w = S - kt * P
                    pe.wait_ge(*prob_masked.at(u))
                    if kt == ST - 1 and h % 2 == 0 and h:
                        pe.wait_ge(*y_out["stick"].at(h // 2 - 1))
                    pe.matmul(bank[Y][HD * (h % 2):HD * (h % 2) + HD, kt * P:S], sa_v[:, kt, h * HD:(h + 1) * HD],
                              stick_a[:, u % 2, 0:w], start=kt == ST - 1, stop=kt == 0,
                              skip_group_check=True).then_inc(*pv_done.tick("stick", u))

                for i in range(len(units) + 3):
                    if i < len(units):
                        z_of(i)
                    if i % 4 == 1 and i // 4 < len(fill):
                        tile = fill[i // 4]
                        name, a = place_of[tile]
                        if a == 0:
                            use(name)
                        project(tile, name, a, P).then_inc(*dense.tick(tile))
                    if i % 4 == 2 and i // 4 < len(fill):
                        tile = fill[i // 4]
                        pe.wait_ge(*act_evac.at(tile + "sq"))
                        if tile == "c_q0":
                            norm(tile, ones, norm_sq, True, False)
                        elif tile == "c_q1":
                            norm(tile, ones, norm_sq, False, True)
                        else:
                            prev = fill[i // 4 - 1] if i // 4 else None
                            norm(tile, ones if tile == "c_kv" else per_head, norm_sq)
                    if 0 <= i - 2 < len(units):
                        u = i - 2
                        h, kt = units[u]
                        if kt == ST - 1:
                            pe.wait_ge(*sp_masked.at(u))
                            pe.matmul(bank[2 + u % 4][:, 0:P], suffix, sp[:, h % 2, SOFF[kt]:SOFF[kt] + P], start=False,
                                      stop=True, skip_group_check=True).then_inc(*stick_sum.tick(u))
                        else:
                            suffix_of(u).then_inc(*stick_sum.tick(u))
                    if 0 <= i - 3 < len(units):
                        pv_of(i - 3)

                use("uq")
                use("ukv")
                pe.wait_ge(*pool_work.at("c_q1lo"))
                pe.wait_ge(*y_out["stick"].at(3))
                uq = [w[:, SLAB_NO["uq"] % RING, 0:16 * P].rearrange("p (c h n) -> p c h n", c=2, h=HEADS) for w in (w_hi, w_lo)]
                ukv = [w[:, SLAB_NO["ukv"] % RING, 0:HEADS * P].rearrange("p (h n) -> p h n", h=HEADS) for w in (w_hi, w_lo)]
                for s in range(ST):
                    b = tile_bank(f"v_b{s}")
                    q = slice(s * P, (s + 1) * P)
                    three(b[:, :], [(ckv_hi[:, q], ckv_lo[:, q], ukv[0][:, :, NOPE:P], ukv[1][:, :, NOPE:P])]
                          ).then_inc(*dense.tick(f"v_b{s}"))

                def prep_q(h):
                    b = tile_bank(f"qh{h}")
                    three(b[:, :], [(uq[0][:, c, h, :], uq[1][:, c, h, :], cq_hi[:, c, :], cq_lo[:, c, :]) for c in range(2)]
                          ).then_inc(*dense.tick(f"qh{h}"))

                def prep_k(h):
                    b = tile_bank(f"kh{h}")
                    three(b[0:NOPE, :], [(ukv[0][:, h, 0:NOPE], ukv[1][:, h, 0:NOPE], ckv_hi[:, :], ckv_lo[:, :])]
                          ).then_inc(*dense.tick(f"kh{h}"))

                def norm_q(h):
                    pe.wait_ge(*act_evac.at(f"qh{h}sq"))
                    if h == 0:
                        pe.wait_ge(*act_evac.at("c_q1rs"))
                    norm(f"qh{h}", first_qk, q_sq)

                def norm_k(h):
                    pe.wait_ge(*act_evac.at(f"kh{h}sq"))
                    pe.wait_ge(*act_evac.at(f"qh{h}ln"))
                    norm(f"kh{h}", ones, k_sq, k=QK)

                def s_of(u):
                    br, h, t = soft_units[u]
                    b, w = s_bank(u), P * (t + 1)
                    q = slice(t * P, (t + 1) * P)
                    if u >= S_RING:
                        p_br = soft_units[u - S_RING][0]
                        pe.wait_ge(*(probs_exp if p_br == "mla" else row_max).at(u - S_RING))
                    if br == "mla":
                        if t == 0:
                            pe.wait_ge(*dve_evac.at(f"qh{h}rope"))
                            pe.wait_ge(*pool_work.at(f"kh{h}rope"))
                            pe.wait_ge(*dve_evac.at(f"kh{h}"))
                        pe.matmul(b[:, 0:w], q_head[:, h % 2, q], k_head[:, h % 2, 0:w], start=True, stop=True)
                        mm = pe.matmul(b[:, w - P:w], big_eye[:, :], causal[:, :], start=False, stop=True, skip_group_check=True)
                    else:
                        if h == 0 and t == 0:
                            pe.wait_ge(*dve_evac.at("ds_q3"))
                            pe.wait_ge(*topk.at("chosen", ST - 1))
                        r = slice(HD * (h % 2), HD * (h % 2) + HD)
                        pe.matmul(b[:, 0:w], ds_q[r, h // 2, q], ds_k[r, 0:w], start=True, stop=True)
                        m = causal[:, :] if t == 0 else chosen[:, OFF[t]:OFF[t] + w]
                        mm = pe.matmul(b[:, 0:w], big_eye[:, :], m, start=False, stop=True, skip_group_check=True)
                    mm.then_inc(*logits.tick(u))

                def t_of(u):
                    br, h, t = soft_units[u]
                    pe.wait_ge(*probs_normed.at(u))
                    if u >= T_RING:
                        pe.wait_ge(*turned_copied(u - T_RING))
                    for k in range(t + 1):
                        mm = pe.transpose(t_bank(u)[:, k * P:(k + 1) * P], probs[:, u % PR, k * P:(k + 1) * P], eye)
                    mm.then_inc(*probs_turned.tick(u))

                def av_of(u):
                    br, h, t = soft_units[u]
                    pe.wait_ge(*turned_copied(u))
                    if t == 0 and h % 2 == 0:
                        if h:
                            pe.wait_ge(*y_out[br].at(h // 2 - 1))
                        elif br == "dsa":
                            pe.wait_ge(*y_out["mla"].at(3))
                    if u == 0:
                        pe.wait_ge(*act_evac.at(f"v_b{ST - 1}"))
                    for k in range(t + 1):
                        v = v_b[:, k, h * HD:(h + 1) * HD] if br == "mla" else ds_v[:, k, :]
                        mm = pe.matmul(bank[Y][HD * (h % 2):HD * (h % 2) + HD, t * P:(t + 1) * P], v,
                                       probs_t[:, u % PTR, k * P:(k + 1) * P], start=k == 0, stop=k == t)
                    mm.then_inc(*pv_done.tick("soft", u))

                prep_q(0)
                prep_k(0)
                norm_q(0)
                norm_k(0)
                prep_q(1)
                for i in range(N_SOFT + AV_LAG):
                    if i < N_SOFT:
                        s_of(i)
                        br, h, t = soft_units[i]
                        if br == "mla" and h + 1 < HEADS:
                            if t == 0:
                                norm_q(h + 1)
                                prep_k(h + 1)
                            if t == 1:
                                norm_k(h + 1)
                            if t == 3 and h + 2 < HEADS:
                                prep_q(h + 2)
                    if 0 <= i - T_LAG < N_SOFT:
                        t_of(i - T_LAG)
                    if 0 <= i - AV_LAG < N_SOFT:
                        av_of(i - AV_LAG)
                ups = 0
                for n in range(3):
                    for m in range(4):
                        if m % 2 == 0:
                            use(f"z{n}_{m // 2}")
                        project(f"z{n}_{m}", f"z{n}_{m // 2}", (m % 2) * P, P).then_inc(*dense.tick(f"z{n}_{m}"))
                    for half in range(2):
                        for m in range(4):
                            if m % 2 == 0:
                                use(f"g{n}_{2 * half + m // 2}")
                            project(f"g{n}_{4 * half + m}", f"g{n}_{2 * half + m // 2}", (m % 2) * P, P
                                    ).then_inc(*dense.tick(f"g{n}_{4 * half + m}"))
                        use(f"up{n}_{half}")
                        for m in range(4):
                            if n == 0 and half == 0 and m == 0:
                                pe.wait_ge(*y_out["dsa"].at(3))
                                pe.wait_ge(*row_max.at(N_SOFT - 1))
                            if ups >= 2:
                                sig, event = gated(ups - 2)
                                pe.wait_ge(*sig.at(*event))
                            if half == 0 and m == 0:
                                pe.wait_ge(*branch.at(f"z{n}_3lo"))
                            name = f"up{n}_{half}"
                            three(bank[2 + ups % 2][:, :],
                                  [(hslab(name, k, m * P, (m + 1) * P, True, S), hslab(name, k, m * P, (m + 1) * P, False, S),
                                    br_hi[:, k, :], br_lo[:, k, :]) for k in range(4)]).then_inc(*up_done.tick(ups))
                            ups += 1
                pe.wait_ge(*merge.at("lo", KT - 1))
                for c in range(2):
                    for j in range(2):
                        use(f"out{c}_{j}")
                        for s in range(ST):
                            if j == 0 and c == 1:
                                pe.wait_ge(*x_new.at(0, s))
                            elif j == 0 and s < 2:
                                pe.wait_ge(*up_gated.at(ups - 2 + s))
                            q = slice(s * P, (s + 1) * P)
                            name = f"out{c}_{j}"
                            three(bank[2 + s][:, :],
                                  [(m_hi[:, 4 * j + k, q], m_lo[:, 4 * j + k, q], hslab(name, k, 0, S, True, S),
                                    hslab(name, k, 0, S, False, S)) for k in range(4)],
                                  start=j == 0, stop=j == 1).then_inc(*out_mm.tick(c, j, s))
                meet(pe, l + 2)

        @block.scalar
        def _(e):
            with nc.allow_non_contiguous_dma(reason="one gain per partition, once"):
                def column(i, rows, src):
                    e.dma_start(gains[rows, :, i:i + 1], src.rearrange("l (p o) -> p l o", o=1)
                                ).then_inc(*gains_in.tick(i, rows.start, by=16))
                column(0, slice(0, P), kv_norm_g)
                column(1, slice(0, P), q_norm_g[:, 0:P])
                column(2, slice(0, P), q_norm_g[:, P:2 * P])
                for i, g in ((3, mla_q_g), (4, mla_k_g)):
                    column(i, slice(0, QK), g)
                    column(i, slice(QK, QK + 16), g[:, NOPE + 16:QK])
                    column(i, slice(QK + 16, P), g[:, NOPE:NOPE + 16])
                for i, g in ((5, dsa_q_g), (6, dsa_k_g)):
                    column(i, slice(0, HD), g)
                    column(i, slice(HD, P), g)
                for ll in range(DEPTH):
                    for n in range(3):
                        e.dma_start(gains[:, ll, N_GAINS + 8 * n:N_GAINS + 8 + 8 * n],
                                    gate_b[ll, n].rearrange("(m p) -> p m", p=P)
                                    ).then_inc(*gains_in.tick("b", ll, n, by=16))
            e.wait_ge(*setup_dve.at("angle"))
            e.activation(ang[64:P, :], turns[64:P, :], ACT.Sin).then_inc(*cos_done.tick("sin"))
            for G in range(S // 16):
                w = P * (G // 8 + 1)
                e.wait_ge(*bias_mm.at(4 * G + 3))
                if G >= 2:
                    e.wait_ge(*bias_stored[G % 2].at(G - 2))
                e.copy(bias_out[:, G % 2, 0:w], bank[G % 2][:, 0:w]).then_inc(*bias_evac.tick(G))
            e.preload_act_table_set("natural_log_exp_and_others")
            meet(e, 1)
            with e.Fori(0, DEPTH) as l:
                def hi(s, part=None):
                    split_hi(e, SLABS[s], part)

                hi(0)
                for s in range(ST):
                    e.activation(x_sq[:, :], x_sb[:, s, :], ACT.Square, accum_out=stat[:, s:s + 1]
                                 ).then_inc(*x_stat.tick("sq", s))
                    e.wait_ge(*x_stat.at("sq", s))
                e.activation(stat[:, 4:8], stat[:, 0:4], ACT.Ln, bias=stat[:, 60:61], scale=1.0 / D).then_inc(*x_stat.tick("ln"))
                e.wait_ge(*x_stat.at("ln"))
                e.activation(stat[:, 8:12], stat[:, 4:8], ACT.Exp, scale=-0.5).then_inc(*x_stat.tick("rs"))
                for i in range(2 * ST):
                    s, j = i // 2, i % 2
                    e.wait_ge(*x_turned.at(i))
                    e.copy(h_hi[:, 4 * j:4 * j + 4, s * P:(s + 1) * P],
                           bank[i % 2][:, :].rearrange("p (k q) -> p k q", k=4)).then_inc(*h_hi_done.tick(i))
                hi(1)
                e.wait_ge(*dense.at("k_pe"))
                e.activation(k_sq[64:96, :], dbank("k_pe")[64:96, :], ACT.Square).then_inc(*act_evac.tick("k_pe"))
                hi(2)
                units = [(h, t) for h in range(HEADS) for t in range(1, ST)]
                for u, (h, t) in enumerate(units):
                    w = P * (t + 1)
                    e.wait_ge(*ix_mm.at(u))
                    if u >= 3:
                        e.wait_ge(*score_sum.at(u - 3))
                    e.activation(ix_relu[:, u % 3, 0:w], bank[2 + u % 4][:, 0:w], ACT.Relu, scale=IDX_DIM ** -0.5
                                 ).then_inc(*ix_relu_done.tick(u))
                hi(3)
                nxt = 4
                for part, dst in (("sa_q", sa_q), ("sa_k", sa_k)):
                    for j in range(4):
                        e.wait_ge(*dense.at(f"{part}{j}"))
                        e.copy(dst[:, j, :], dbank(f"{part}{j}")[:, :]).then_inc(*act_evac.tick(f"{part}{j}"))
                        if j % 2:
                            hi(nxt)
                            nxt += 1
                hi(8)
                for s in range(ST):
                    e.wait_ge(*dense.at("sa_v", 1, s))
                    e.copy(sa_v[:, s, :], bank[2 + s][:, :]).then_inc(*act_evac.tick("sa_v", s))
                hi(9)

                def rs_of(tile, n, dst, scale=1.0):
                    e.wait_ge(*norm_sum.at(tile))
                    e.activation(dst, bank[NORM][:, :], ACT.Ln, bias=stat[:, 60:61], scale=1.0 / n
                                 ).then_inc(*act_evac.tick(tile + "ln"))
                    e.wait_ge(*act_evac.at(tile + "ln"))
                    b = 0.0 if scale == 1.0 else stat[:, 61:62] if scale == HD ** -0.5 else stat[:, 62:63]
                    e.activation(dst, dst, ACT.Exp, scale=-0.5, bias=b).then_inc(*act_evac.tick(tile + "rs"))

                units = [(h, kt) for h in range(HEADS) for kt in reversed(range(ST))]
                fill = ["c_kv", "ds_k", "ds_q0", "ds_q1", "ds_q2", "ds_q3", "c_q0", "c_q1"]
                for i in range(len(units) + 5):
                    if i < len(units):
                        w = S - units[i][1] * P
                        v = soft[:, i % 3, 0:w]
                        e.wait_ge(*stick_clip.at(i))
                        e.activation(v, v, ACT.Exp).then_inc(*stick_exp.tick("exp", i))
                        e.wait_ge(*stick_exp.at("exp", i))
                        e.activation(v, v, ACT.Ln, bias=1.0).then_inc(*stick_exp.tick("ln", i))
                    k = i // 4
                    if i % 4 == 1 and k < len(fill):
                        tile = fill[k]
                        e.wait_ge(*dense.at(tile))
                        if k:
                            e.wait_ge(*norm_sum.at(fill[k - 1]))
                        e.activation(norm_sq[:, :], dbank(tile)[:, :], ACT.Square).then_inc(*act_evac.tick(tile + "sq"))
                        if k % 2:
                            hi(10 + k // 2, 0)
                    if i % 4 == 2 and k % 2 and k < len(fill):
                        hi(10 + k // 2, 1)
                    if i % 4 == 3 and k < len(fill) and fill[k] != "c_q0":
                        tile = fill[k]
                        if k:
                            prev = fill[k - 1] if fill[k - 1] != "c_q0" else fill[k - 2]
                            e.wait_ge(*dve_evac.at(prev))
                        n = {"c_kv": KV_LORA, "c_q1": Q_LORA}.get(tile, HD)
                        rs_of(tile, n, norm_rs[:, :], HD ** -0.5 if tile.startswith("ds_q") else 1.0)
                    if i == 4:
                        e.wait_ge(*dve_evac.at("c_kv"))
                        e.copy(ckv_hi[:, :], norm_out[:, :]).then_inc(*act_evac.tick("ckv_hi"))
                    if i == 33:
                        for c in range(2):
                            e.wait_ge(*dve_evac.at(f"c_q{c}"))
                            e.copy(cq_hi[:, c, :], cq_out[c][:, :]).then_inc(*act_evac.tick(f"cq_hi{c}"))
                    if 0 <= i - 2 < len(units):
                        u = i - 2
                        w = S - units[u][1] * P
                        e.wait_ge(*stick_sum.at(u))
                        if u >= 2:
                            e.wait_ge(*pv_done.at("stick", u - 2))
                        e.activation(stick_a[:, u % 2, 0:w], bank[2 + u % 4][:, 0:w], ACT.Exp, scale=STICK_SCALE
                                     ).then_inc(*stick_prob.tick(u))

                for s in range(ST):
                    e.wait_ge(*dense.at(f"v_b{s}"))
                    if s == 0:
                        e.wait_ge(*pv_done.at("stick", len(units) - 1))
                    e.copy(v_b[:, s, :], dbank(f"v_b{s}")[:, :]).then_inc(*act_evac.tick(f"v_b{s}"))

                def sq_q(h):
                    e.wait_ge(*dense.at(f"qh{h}"))
                    e.activation(q_sq[:, :], dbank(f"qh{h}")[:, :], ACT.Square).then_inc(*act_evac.tick(f"qh{h}sq"))

                def sq_k(h):
                    e.wait_ge(*dense.at(f"kh{h}"))
                    if h:
                        e.wait_ge(*norm_sum.at(f"kh{h - 1}"))
                    e.activation(k_sq[0:NOPE, :], dbank(f"kh{h}")[0:NOPE, :], ACT.Square).then_inc(*act_evac.tick(f"kh{h}sq"))

                def rs_q(h):
                    if h:
                        e.wait_ge(*dve_evac.at(f"qh{h - 1}"))
                    rs_of(f"qh{h}", QK, q_rs[:, :], QK ** -0.5)

                def rs_k(h):
                    if h:
                        e.wait_ge(*dve_evac.at(f"kh{h - 1}"))
                        e.wait_ge(*pool_work.at(f"kh{h - 1}rope"))
                    rs_of(f"kh{h}", QK, k_rs[:, :])

                def exp_of(u):
                    br, h, t = soft_units[u]
                    w = P * (t + 1)
                    e.wait_ge(*row_max.at(u))
                    if br == "mla" and u >= PR:
                        e.wait_ge(*probs_turned.at(u - PR))
                    dst = probs[:, u % PR, 0:w]
                    e.activation(dst, s_bank(u)[:, 0:w] if br == "mla" else dst, ACT.Exp, bias=stat[:, 16 + u % 4:17 + u % 4],
                                 accum_out=stat[:, 20 + u % 4:21 + u % 4]).then_inc(*probs_exp.tick(u))

                sq_q(0)
                sq_k(0)
                rs_q(0)
                rs_k(0)
                sq_q(1)
                for i in range(N_SOFT + AV_LAG + 1):
                    u = i - AV_LAG - 1
                    if 0 <= u and u % 8 == 7:
                        e.wait_ge(*pv_done.at("soft", u))
                        pair = u // 8
                        dst = y[:, 4 + pair, :] if pair < 4 else y_dsa[:, pair - 4, :]
                        e.copy(dst, bank[Y][:, :]).then_inc(*y_out["mla" if pair < 4 else "dsa"].tick(pair % 4))
                    if i < N_SOFT:
                        br, h, t = soft_units[i]
                        exp_of(i)
                        if br == "mla" and h + 1 < HEADS:
                            if t == 0:
                                rs_q(h + 1)
                                sq_k(h + 1)
                            if t == 1:
                                rs_k(h + 1)
                            if t == 3 and h + 2 < HEADS:
                                sq_q(h + 2)
                    u = i - T_LAG
                    if 0 <= u < N_SOFT and soft_units[u][0] == "dsa":
                        w = P * (soft_units[u][2] + 1)
                        e.wait_ge(*probs_turned.at(u))
                        e.wait_ge(*pv_done.at("soft", u - PTR))
                        e.copy(probs_t[:, u % PTR, 0:w], t_bank(u)[:, 0:w]).then_inc(*probs_t_ready["dsa"].tick(u))
                    if i == SPLIT_Z:
                        hi(SLAB_NO["z0_0"])
                        hi(SLAB_NO["z0_1"])
                e.preload_act_table_set("sigmoid_and_others")
                ups = 0
                nxt = SLAB_NO["z0_0"] + 2
                for n in range(3):
                    for m in range(4):
                        e.wait_ge(*dense.at(f"z{n}_{m}"))
                        if 4 * n + m >= 2:
                            pn, pm = divmod(4 * n + m - 2, 4)
                            e.wait_ge(*branch.at(f"z{pn}_{pm}z"))
                        e.activation(z_sig[:, m % 2, :], dbank(f"z{n}_{m}")[:, :], ACT.Sigmoid).then_inc(*gate_sig.tick("z", n, m))
                        if m % 2:
                            hi(nxt)
                            nxt += 1
                        if m:
                            br_split(e, l, n, m - 1)
                    br_split(e, l, n, 3)
                    for half in range(2):
                        for m in range(4):
                            mm = 4 * half + m
                            e.wait_ge(*dense.at(f"g{n}_{mm}"))
                            g = 8 * n + mm
                            if g >= 4:
                                e.wait_ge(*merge.at("sum", g - 4))
                            e.activation(gate[:, m, :], dbank(f"g{n}_{mm}")[:, :], ACT.Sigmoid,
                                         bias=gain[:, N_GAINS + g:N_GAINS + 1 + g]).then_inc(*gate_sig.tick(f"g{n}_{mm}"))
                            if m % 2:
                                hi(nxt)
                                nxt += 1
                        if n == 2:
                            for m in range(4 * half, 4 * half + 4):
                                e.wait_ge(*merge.at("sum", 16 + m))
                                e.copy(m_hi[:, m, :], merged[:, m, :]).then_inc(*merged_hi.tick(m))
                        if nxt < NS:
                            hi(nxt)
                            nxt += 1
                while nxt < NS:
                    hi(nxt)
                    nxt += 1
                e.preload_act_table_set("natural_log_exp_and_others")
                meet(e, l + 2)

        @block.vector
        def _(e):
            e.memset(step_f[:, :], 0.0).then_inc(*setup_dve.tick("z0"))
            e.memset(prev_f[:, :], 0.0).then_inc(*setup_dve.tick("steps_zero"))
            e.memset(stat[:, 60:61], EPS).then_inc(*setup_dve.tick("c0"))
            e.memset(stat[:, 61:62], math.log(HD ** -0.5)).then_inc(*setup_dve.tick("c1"))
            e.memset(stat[:, 62:63], math.log(QK ** -0.5)).then_inc(*setup_dve.tick("c2"))
            e.wait_ge(*consts_in.at("mats"))
            e.tensor_copy(big_eye[:, :], big_eye_f).then_inc(*setup_dve.tick("be"))
            e.tensor_copy(causal[:, :], causal_f).then_inc(*setup_dve.tick("ca"))
            e.wait_ge(*pos_in.at("rbp", 3))
            e.tensor_copy(pos_f[:, :], pos_i[:, :]).then_inc(*setup_dve.tick("pos"))
            e.tensor_tensor(step_f[:, :], step_f[:, :], prev_f[:, :], ALU.subtract).then_inc(*setup_dve.tick("steps"))
            e.wait_ge(*setup_dve.at("steps"))
            for qq in range(4):
                r = slice(32 * qq, 32 * qq + 32)
                e.tensor_scalar(edge[r, :], pos_f[r, qq:S:4], thr[r, :], None, ALU.subtract).then_inc(*setup_dve.tick("edge", qq))
            hi_rows = slice(64, P)
            e.tensor_scalar(ang[hi_rows, :], pos_f[hi_rows, :], inv_freq[hi_rows, :], None, ALU.mult).then_inc(*setup_dve.tick("a0"))
            e.wait_ge(*setup_dve.at("a0"))
            tau = 2.0 * math.pi
            c1 = 6.28125
            c2 = float(np.float32(np.round((tau - c1) * 2 ** 21) / 2 ** 21))
            c3 = tau - c1 - c2
            e.tensor_scalar(stat[hi_rows, 58:59], phase[hi_rows, :], 1.0 / tau, None, ALU.mult).then_inc(*setup_dve.tick("ph"))
            e.wait_ge(*setup_dve.at("ph"))
            magic = 1.5 * 2.0 ** 23
            e.tensor_scalar(turns[hi_rows, :], ang[hi_rows, :], 1.0 / tau, stat[hi_rows, 58:59], ALU.mult, ALU.add).then_inc(*setup_dve.tick("t0"))
            e.wait_ge(*setup_dve.at("t0"))
            e.tensor_scalar(turns[hi_rows, :], turns[hi_rows, :], magic, None, ALU.add).then_inc(*setup_dve.tick("t1"))
            e.wait_ge(*setup_dve.at("t1"))
            e.tensor_scalar(turns[hi_rows, :], turns[hi_rows, :], magic, None, ALU.subtract).then_inc(*setup_dve.tick("t2"))
            e.wait_ge(*setup_dve.at("t2"))
            for i, c in enumerate((c1, c2, c3)):
                e.scalar_tensor_tensor(ang[hi_rows, :], turns[hi_rows, :], -c, ang[hi_rows, :], ALU.mult, ALU.add
                                       ).then_inc(*setup_dve.tick("r", i))
                e.wait_ge(*setup_dve.at("r", i))
            e.tensor_scalar(ang[hi_rows, :], ang[hi_rows, :], phase[hi_rows, :], 3.1415925, ALU.add, ALU.min).then_inc(*setup_dve.tick("r3"))
            e.wait_ge(*setup_dve.at("r3"))
            e.tensor_scalar(turns[hi_rows, :], ang[hi_rows, :], -3.1415925, None, ALU.max).then_inc(*setup_dve.tick("angle"))
            e.wait_ge(*cos_done.at("sin"))
            e.tensor_scalar(cos_sin[hi_rows, :], ang[hi_rows, :], sign[hi_rows, :], None, ALU.mult).then_inc(*setup_dve.tick("cs"))
            for g in range(S // 4):
                w = P * (g // 32 + 1)
                if g >= 8:
                    e.wait_ge(*bias_mm.at(g - 8))
                e.tensor_scalar(reach[:, g % 8, 0:w], pos_f[:, 0:w], edge[:, g:g + 1], None, ALU.is_le
                                ).then_inc(*reach_ready.tick(g))
            e.wait_ge(*gains_in.at("b", DEPTH - 1, 2))
            e.wait_ge(*x_in.at("x", ST - 1))
            meet(e, 1)
            with e.Fori(0, DEPTH) as l:
                v, t, r0, r = (stat[:, i:i + 4] for i in (24, 28, 8, 12))
                e.wait_ge(*x_stat.at("rs"))
                e.tensor_copy(gain[:, :], gains[:, l, :]).then_inc(*dve_stat.tick("gain"))
                e.tensor_scalar(v, stat[:, 0:4], 1.0 / D, EPS, ALU.mult, ALU.add).then_inc(*dve_stat.tick("v"))
                e.tensor_tensor(t, r0, r0, ALU.mult).then_inc(*dve_stat.tick("t0"))
                e.wait_ge(*dve_stat.at("t0"))
                e.tensor_tensor(t, t, v, ALU.mult).then_inc(*dve_stat.tick("t1"))
                e.wait_ge(*dve_stat.at("t1"))
                e.tensor_scalar(t, t, -0.5, 1.5, ALU.mult, ALU.add).then_inc(*dve_stat.tick("t2"))
                e.wait_ge(*dve_stat.at("t2"))
                e.tensor_tensor(r, r0, t, ALU.mult).then_inc(*dve_stat.tick("r"))
                e.wait_ge(*dve_stat.at("r"))
                e.wait_ge(*gain_row_in.at("row"))

                def h_lo_of(i):
                    s, j = i // 2, i % 2
                    e.wait_ge(*h_hi_done.at(i))
                    cols = (slice(None), slice(4 * j, 4 * j + 4), slice(s * P, (s + 1) * P))
                    e.tensor_tensor(h_lo[cols], bank[i % 2][:, :].rearrange("p (k q) -> p k q", k=4),
                                    h_hi[cols].bitcast(F32), ALU.subtract).then_inc(*h_lo_done.tick(i))

                for s in range(ST):
                    if s >= 2:
                        e.wait_ge(*x_turned.at(2 * (s - 2) + 1))
                    e.scalar_tensor_tensor(xn[:, s % 2, :], x_sb[:, s, :], r[:, s:s + 1], gain_row[:, :],
                                           ALU.mult, ALU.mult).then_inc(*xn_ready.tick(s))
                    if s:
                        h_lo_of(2 * s - 2)
                        h_lo_of(2 * s - 1)
                h_lo_of(2 * ST - 2)
                h_lo_of(2 * ST - 1)
                e.wait_ge(*dense.at("ix_k"))
                e.tensor_copy(ix_k[:, :], dbank("ix_k")[:, :]).then_inc(*dve_evac.tick("ix_k"))
                e.wait_ge(*act_evac.at("k_pe"))
                b = dbank("k_pe")
                e.scalar_tensor_tensor(k_rope[64:96, :], b[64:96, :], gain[64:96, 4:5], cos_sin[64:96, :],
                                       ALU.mult, ALU.mult).then_inc(*dve_evac.tick("kr0"))
                e.scalar_tensor_tensor(norm_out[64:96, :], b[96:P, :], gain[96:P, 4:5], cos_sin[96:P, :],
                                       ALU.mult, ALU.mult).then_inc(*dve_evac.tick("k_pe"))
                e.wait_ge(*dve_evac.at("k_pe"))
                e.tensor_tensor(k_rope[96:P, :], k_rope[64:96, :], norm_out[64:96, :], ALU.add).then_inc(*dve_evac.tick("kr1"))
                e.tensor_tensor(k_rope[64:96, :], k_rope[64:96, :], norm_out[64:96, :], ALU.add).then_inc(*dve_evac.tick("kr"))
                for s in range(ST):
                    b = dbank(f"nat{s}")
                    e.wait_ge(*dense.at(f"nat{s}"))
                    e.tensor_copy(ds_v[:, s, :], b[:, 0:HD]).then_inc(*dve_evac.tick("dv", s))
                    e.tensor_scalar(ix_w[:, s, :], b[:, P:P + HEADS], HEADS ** -0.5, None, ALU.mult
                                    ).then_inc(*dve_evac.tick(f"nat{s}"))
                for j in range(2):
                    e.wait_ge(*dense.at(f"ix_q{j}"))
                    e.tensor_copy(ix_q[:, j, :], dbank(f"ix_q{j}")[:, :]).then_inc(*dve_evac.tick(f"ix_q{j}"))
                units = [(h, t) for h in range(HEADS) for t in range(1, ST)]
                for u, (h, t) in enumerate(units):
                    w = P * (t + 1)
                    dst, src, wt = score[:, OFF[t]:OFF[t] + w], ix_relu[:, u % 3, 0:w], ix_w[:, t, h:h + 1]
                    e.wait_ge(*ix_relu_done.at(u))
                    if h == 0:
                        e.tensor_scalar(dst, src, wt, None, ALU.mult).then_inc(*score_sum.tick(u))
                    else:
                        e.wait_ge(*score_sum.at(u - 3))
                        e.scalar_tensor_tensor(dst, src, wt, dst, ALU.mult, ALU.add).then_inc(*score_sum.tick(u))
                for rnd in range(TOPK // 8):
                    for t in range(1, ST):
                        row, best = score[:, OFF[t]:OFF[t] + P * (t + 1)], stat[:, 32 + 8 * (t - 1):40 + 8 * (t - 1)]
                        if rnd == 0:
                            e.wait_ge(*score_masked.at(t))
                        else:
                            e.wait_ge(*topk.at("replace", rnd - 1, t))
                        e.max(best, row).then_inc(*topk.tick("max", rnd, t))
                    for t in range(1, ST):
                        row, best = score[:, OFF[t]:OFF[t] + P * (t + 1)], stat[:, 32 + 8 * (t - 1):40 + 8 * (t - 1)]
                        e.wait_ge(*topk.at("max", rnd, t))
                        e.match_replace(row, best, row, TAKEN).then_inc(*topk.tick("replace", rnd, t))
                for t in range(1, ST):
                    r = slice(OFF[t], OFF[t] + P * (t + 1))
                    e.wait_ge(*topk.at("replace", TOPK // 8 - 1, t))
                    e.tensor_scalar(chosen[:, r], score[:, r], TAKEN, 1.0, ALU.is_equal, ALU.subtract
                                    ).then_inc(*topk.tick("chosen", t))

                units = [(h, kt) for h in range(HEADS) for kt in reversed(range(ST))]
                fill = ["c_kv", "ds_k", "ds_q0", "ds_q1", "ds_q2", "ds_q3", "c_q0", "c_q1"]
                gain_of = {"c_kv": 0, "ds_k": 6, "c_q0": 1, "c_q1": 2}

                def normed(tile, dst, rs):
                    g = gain_of.get(tile, 5)
                    e.scalar_tensor_tensor(dst, dbank(tile)[:, :], gain[:, g:g + 1], rs, ALU.mult, ALU.mult
                                           ).then_inc(*dve_evac.tick(tile))

                for i in range(len(units) + 5):
                    if i >= 4 and (i - 4) % 8 == 7:
                        pair = (i - 4) // 8
                        e.wait_ge(*pv_done.at("stick", 8 * pair + 7))
                        e.tensor_copy(y[:, pair, :], bank[Y][:, :]).then_inc(*y_out["stick"].tick(pair))
                    if i < len(units):
                        w = S - units[i][1] * P
                        e.wait_ge(*stick_z.at(i))
                        if i >= 3:
                            e.wait_ge(*stick_sp.at(i - 3))
                        e.tensor_scalar(soft[:, i % 3, 0:w], bank[2 + i % 4][:, 0:w], STICK_SCALE, CLIP, ALU.mult, ALU.min
                                        ).then_inc(*stick_clip.tick(i))
                    if 0 <= i - 1 < len(units):
                        u = i - 1
                        h, kt = units[u]
                        w = S - kt * P
                        e.wait_ge(*stick_exp.at("ln", u))
                        if h >= 2:
                            e.wait_ge(*stick_sum.at(4 * (h - 2) + 3))
                        e.scalar_tensor_tensor(sp[:, h % 2, SOFF[kt]:SOFF[kt] + w], bank[2 + u % 4][:, 0:w], STICK_SCALE,
                                               soft[:, u % 3, 0:w], ALU.mult, ALU.max).then_inc(*stick_sp.tick(u))
                    k = i // 4
                    if i % 4 == 3 and k < len(fill) and fill[k] != "c_q0":
                        tile = fill[k]
                        e.wait_ge(*act_evac.at(tile + "rs"))
                        if tile == "c_kv":
                            normed(tile, norm_out[:, :], norm_rs[:, :])
                        elif tile == "ds_k":
                            normed(tile, ds_k[:, :], norm_rs[:, :])
                        elif tile == "c_q1":
                            normed("c_q0", cq_out[0][:, :], norm_rs[:, :])
                            normed("c_q1", cq_out[1][:, :], norm_rs[:, :])
                        else:
                            normed(tile, ds_q[:, int(tile[-1]), :], norm_rs[:, :])
                    if i % 4 in (2, 3) and k % 2 and k < len(fill):
                        split_lo(e, SLABS[10 + k // 2], i % 4 - 2)

                def head_q(h):
                    e.wait_ge(*act_evac.at(f"qh{h}rs"))
                    if h >= 2:
                        e.wait_ge(*logits.at(4 * (h - 2) + 3))
                    e.scalar_tensor_tensor(q_head[:, h % 2, :], dbank(f"qh{h}")[:, :], gain[:, 3:4], q_rs[:, :],
                                           ALU.mult, ALU.mult).then_inc(*dve_evac.tick(f"qh{h}"))
                    e.wait_ge(*dve_evac.at(f"qh{h}"))
                    qr = q_head[64:P, h % 2, :]
                    e.tensor_tensor(qr, qr, cos_sin[64:P, :], ALU.mult).then_inc(*dve_evac.tick(f"qh{h}rope"))

                def head_k(h):
                    e.wait_ge(*act_evac.at(f"kh{h}rs"))
                    if h >= 2:
                        e.wait_ge(*logits.at(4 * (h - 2) + 3))
                    e.scalar_tensor_tensor(k_head[0:NOPE, h % 2, :], dbank(f"kh{h}")[0:NOPE, :], gain[0:NOPE, 4:5],
                                           k_rs[0:NOPE, :], ALU.mult, ALU.mult).then_inc(*dve_evac.tick(f"kh{h}"))

                def inverse(u):
                    e.wait_ge(*probs_exp.at(u))
                    if u >= 4:
                        e.wait_ge(*probs_normed.at(u - 4))
                    e.reciprocal(stat[:, 24 + u % 4:25 + u % 4], stat[:, 20 + u % 4:21 + u % 4]).then_inc(*row_inv.tick(u))

                head_q(0)
                head_k(0)
                for i in range(N_SOFT + T_LAG):
                    if i < N_SOFT:
                        br, h, t = soft_units[i]
                        w = P * (t + 1)
                        negated = stat[:, 16 + i % 4:17 + i % 4]
                        e.wait_ge(*logits.at(i))
                        if i >= 4:
                            e.wait_ge(*probs_exp.at(i - 4))
                        if br == "mla":
                            e.tensor_reduce(negated, s_bank(i)[:, 0:w], AX_X, ALU.max, negate=True
                                            ).then_inc(*row_max.tick(i))
                        else:
                            if t == 0:
                                e.wait_ge(*bias_in[h % 2].at(h))
                            e.wait_ge(*probs_turned.at(i - PR))
                            top = stat[:, 12 + i % 4:13 + i % 4]
                            e.tensor_tensor_reduce(out=probs[:, i % PR, 0:w], in0=s_bank(i)[:, 0:w],
                                                   in1=bias[:, h % 2, OFF[t]:OFF[t] + w], scale=1.0, scalar=TAKEN,
                                                   op0=ALU.add, op1=ALU.max, accum_out=top).then_inc(*row_max.tick("max", i))
                            e.wait_ge(*row_max.at("max", i))
                            e.tensor_scalar(negated, top, -1.0, None, ALU.mult).then_inc(*row_max.tick(i))
                    if 0 <= i - 1 < N_SOFT:
                        inverse(i - 1)
                    u = i - T_LAG
                    if 0 <= u < N_SOFT and soft_units[u][0] == "mla":
                        w = P * (soft_units[u][2] + 1)
                        e.wait_ge(*probs_turned.at(u))
                        if u >= PTR:
                            e.wait_ge(*pv_done.at("soft", u - PTR))
                        e.tensor_copy(probs_t[:, u % PTR, 0:w], t_bank(u)[:, 0:w]).then_inc(*probs_t_ready["mla"].tick(u))
                    if i < N_SOFT and br == "mla" and h + 1 < HEADS:
                        if t == 1:
                            head_q(h + 1)
                        if t == 2:
                            head_k(h + 1)
                ups = 0
                for n in range(3):
                    for m in range(4):
                        tile = f"z{n}_{m}"
                        e.wait_ge(*gate_sig.at("z", n, m))
                        zs = z_sig[:, m % 2, :]
                        yt = (y[:, 4 * n + m, :] if n < 2 else y_dsa[:, m, :])
                        e.tensor_tensor(zs, zs, dbank(tile)[:, :], ALU.mult).then_inc(*branch.tick(tile + "z"))
                        e.wait_ge(*branch.at(tile + "z"))
                        if n == 0 and m == 0:
                            e.wait_ge(*y_out["mla"].at(3))
                        if n == 2 and m == 0:
                            e.wait_ge(*y_out["dsa"].at(3))
                        e.tensor_tensor(yt, yt, zs, ALU.mult).then_inc(*branch.tick(tile + "y"))
                        e.wait_ge(*merged_hi.at("br", n, m))
                        e.tensor_tensor(br_lo[:, m, :], yt, br_hi[:, m, :].bitcast(F32), ALU.subtract
                                        ).then_inc(*branch.tick(tile + "lo"))
                    for half in range(2):
                        for m in range(4 * half, 4 * half + 4):
                            e.wait_ge(*up_done.at(ups))
                            e.wait_ge(*gate_sig.at(f"g{n}_{m}"))
                            b = bank[2 + ups % 2]
                            if n == 0:
                                e.tensor_tensor(merged[:, m, :], gate[:, m % 4, :], b[:, :], ALU.mult).then_inc(*merge.tick("sum", ups))
                            else:
                                g = gate[:, m % 4, :]
                                e.tensor_tensor(g, g, b[:, :], ALU.mult).then_inc(*up_gated.tick(ups))
                                e.wait_ge(*up_gated.at(ups))
                                e.tensor_tensor(merged[:, m, :], merged[:, m, :], g, ALU.add).then_inc(*merge.tick("sum", ups))
                            ups += 1
                        if n == 2:
                            for m in range(4 * half, 4 * half + 4):
                                e.wait_ge(*merged_hi.at(m))
                                e.tensor_tensor(m_lo[:, m, :], merged[:, m, :], m_hi[:, m, :].bitcast(F32), ALU.subtract
                                                ).then_inc(*merge.tick("lo", m))
                for c in range(2):
                    for s in range(ST):
                        e.wait_ge(*out_mm.at(c, 1, s))
                        xs = x_sb[:, s, c * S:(c + 1) * S]
                        e.tensor_tensor(xs, xs, bank[2 + s][:, :], ALU.add).then_inc(*x_new.tick(c, s))
                meet(e, l + 2)

        @block.gpsimd
        def _(e):
            meet(e, 1)
            with e.Fori(0, DEPTH) as l:
                def lo(s):
                    split_lo(e, SLABS[s])

                lo(0)
                lo(1)
                lo(2)
                n_ix = 3 * HEADS
                for t in range(1, ST):
                    e.wait_ge(*score_sum.at(n_ix - 4 + t))
                    d = score[:, OFF[t] + P * t:OFF[t] + P * (t + 1)]
                    e.affine_select(out=d, in_=d, pattern=[[-1, P]], compare_op=ALU.is_ge, fill=MASKED, base=0,
                                    channel_multiplier=1).then_inc(*score_masked.tick(t))
                for s in range(3, 10):
                    lo(s)
                units = [(h, kt) for h in range(HEADS) for kt in reversed(range(ST))]
                for i in range(len(units) + 4):
                    if 0 <= i - 1 < len(units):
                        u = i - 1
                        h, kt = units[u]
                        d = sp[:, h % 2, SOFF[kt]:SOFF[kt] + P]
                        e.wait_ge(*stick_sp.at(u))
                        e.affine_select(out=d, in_=d, pattern=[[1, P]], compare_op=ALU.is_gt, fill=0.0, base=0,
                                        channel_multiplier=-1).then_inc(*sp_masked.tick(u))
                    if 0 <= i - 2 < len(units):
                        u = i - 2
                        d = stick_a[:, u % 2, 0:P]
                        e.wait_ge(*stick_prob.at(u))
                        e.affine_select(out=d, in_=d, pattern=[[1, P]], compare_op=ALU.is_gt, fill=0.0, base=0,
                                        channel_multiplier=-1).then_inc(*prob_masked.tick(u))
                    if i == 5:
                        e.wait_ge(*act_evac.at("ckv_hi"))
                        e.tensor_tensor(ckv_lo[:, :], norm_out[:, :], ckv_hi[:, :].bitcast(F32), ALU.subtract
                                        ).then_inc(*pool_work.tick("ckv_lo"))
                    if i == 34:
                        for c in range(2):
                            e.wait_ge(*act_evac.at(f"cq_hi{c}"))
                            e.tensor_tensor(cq_lo[:, c, :], cq_out[c][:, :], cq_hi[:, c, :].bitcast(F32), ALU.subtract
                                            ).then_inc(*pool_work.tick(f"c_q{c}lo"))

                def rope_k(h):
                    e.wait_ge(*act_evac.at(f"kh{h}rs"))
                    if h >= 2:
                        e.wait_ge(*logits.at(4 * (h - 2) + 3))
                    e.tensor_tensor(k_head[64:P, h % 2, :], k_rope[64:P, :], k_rs[64:P, :], ALU.mult
                                    ).then_inc(*pool_work.tick(f"kh{h}rope"))

                e.wait_ge(*pool_work.at("c_q1lo"))
                rope_k(0)
                e.wait_ge(*pool_work.at("kh0rope"))
                for i in range(N_SOFT + 1):
                    if i:
                        u = i - 1
                        w = P * (soft_units[u][2] + 1)
                        e.wait_ge(*row_inv.at(u))
                        e.tensor_scalar(probs[:, u % PR, 0:w], probs[:, u % PR, 0:w], stat[:, 24 + u % 4:25 + u % 4], 1.0,
                                        ALU.mult, ALU.mult).then_inc(*probs_normed.tick(u))
                    if i < N_SOFT:
                        br, h, t = soft_units[i]
                        if br == "mla" and h + 1 < HEADS and t == 2:
                            e.wait_ge(*probs_normed.at(i - 1))
                            rope_k(h + 1)
                            e.wait_ge(*pool_work.at(f"kh{h + 1}rope"))
                    if i == SPLIT_Z:
                        lo(SLAB_NO["z0_0"])
                        lo(SLAB_NO["z0_1"])
                for s in range(SLAB_NO["z0_1"] + 1, NS):
                    lo(s)
                meet(e, l + 2)
    return {n: s.events for n, s in signals.items()}


_INS = ["x", "positions", "norm_g", "w_in", "mla_q_norm_g", "mla_kv_norm_g", "mla_w_uq", "mla_w_ukv",
        "mla_q_g", "mla_k_g", "dsa_q_g", "dsa_k_g", "rel_bias", "gate_b", "w_branch", "w_out"]


def program(nc, arrays, known):
    args = [nc.dram_tensor(n, a.shape, mybir.dt.from_np(a.dtype), kind="ExternalInput").ap() for n, a in arrays.items()]
    out = nc.dram_tensor("out_dram", (1, S, D), F32, kind="ExternalOutput").ap()
    bias_dram = nc.dram_tensor("bias_dram", (HEADS, S, S), F32).ap()
    return build(nc, *args, out, bias_dram, known)


def kernel(**inputs):
    import concourse.bacc as bacc
    from concourse.bass_utils import run_bass_kernel_spmd

    arrays = {f"in_{n}": np.ascontiguousarray(inputs[n]) for n in _INS}
    arrays["in_consts"] = constants()
    known = program(bacc.Bacc("TRN2", target_bir_lowering=False, num_devices=1), arrays, {})
    nc = bacc.Bacc("TRN2", target_bir_lowering=False, num_devices=1)
    program(nc, arrays, known)
    r = run_bass_kernel_spmd(nc, [arrays], core_ids=[0])
    return r.results[0]["out_dram"]
```

```python
from contextlib import ExitStack
import math

import numpy as np
import concourse.bass as bass
from concourse import mybir

ALU = mybir.AluOpType
ACT = mybir.ActivationFunctionType
F32 = mybir.dt.float32
F32R = mybir.dt.float32r
BF16 = mybir.dt.bfloat16
I32 = mybir.dt.int32
AX_X = mybir.AxisListType.X

P = 128
D = 1024
S = 512
DEPTH = 2
KT = D // P
ST = S // P
HEADS = 8
HD = 64
NOPE, ROPE = 64, 32
QK = NOPE + ROPE
Q_LORA, KV_LORA = 256, 128
IDX_DIM = 32
TOPK = min(256, S // 4)
BUCKETS, MAX_DIST = 32, 128
BW = 512
EPS = 1e-6
THETA = 10000.0

SIZES = dict(sa_q=512, sa_k=512, sa_v=512, c_q=Q_LORA, c_kv=KV_LORA, k_pe=ROPE, ds_q=512, ds_k=HD,
             ds_v=HD, ix_q=HEADS * IDX_DIM, ix_k=IDX_DIM, ix_w=HEADS, z=3 * BW, g=3 * D)
COL = {}
_at = 0
for _n, _w in SIZES.items():
    COL[_n] = _at
    _at += _w

SLAB = 2 * P
SMALL = P + HD + HEADS
MASKED = -1e30
TAKEN = -3e38
CLIP = 30.0
STICK_SCALE = HD ** -0.5
OFF = [P * (t * (t + 1) // 2) for t in range(ST)]
SOFF = [P * (t * ST - t * (t - 1) // 2) for t in range(ST)]
STRIPS = P * ST * (ST + 1) // 2


def bucket_thresholds():
    exact = BUCKETS // 2
    n = np.arange(1, 4 * MAX_DIST)
    large = exact + (np.log(n / exact) / math.log(MAX_DIST / exact) * (BUCKETS - exact) + 1e-9).astype(int)
    bucket = np.where(n < exact, n, np.minimum(large, BUCKETS - 1))
    least = [-float(2 ** 26)] + [float(n[np.argmax(bucket >= b)]) for b in range(1, BUCKETS)]
    return np.array(least, np.float32)


def constants():
    r = np.arange(P)
    eye = np.eye(P)
    suffix = np.where(r[:, None] >= r[None, :], -1.0 / STICK_SCALE, 0.0)
    all_later = np.full((P, P), -1.0 / STICK_SCALE)
    ones = np.ones((P, P))
    per_head = (r[:, None] // HD == r[None, :] // HD) * 1.0
    first_qk = (r[:, None] < QK) * np.ones((P, P))
    big_eye = eye * -MASKED
    causal = np.where(r[None, :] > r[:, None], -1.0, 0.0)
    mats = np.concatenate([eye, suffix, all_later, ones, per_head, first_qk, big_eye, causal], 1)
    same = r[:, None] % IDX_DIM == r[None, :] % IDX_DIM
    take_hi = same * (r[None, :] // IDX_DIM % 2 == 0)
    take_lo = same * (r[None, :] // IDX_DIM % 2 == 1)
    take_k = same * (r[:, None] // IDX_DIM == r[None, :] // IDX_DIM // 2)
    half = ROPE // 2
    inv = (np.float32(THETA) ** (-(np.arange(half, dtype=np.float32) * np.float32(2.0)) / np.float32(ROPE))).astype(np.float32)
    cols = np.zeros((P, 4))
    cols[:, 0] = np.tile(bucket_thresholds(), P // BUCKETS)
    cols[64:, 1] = np.tile(inv, 4)
    cols[64:96, 2] = math.pi / 2
    cols[64:, 3] = 1.0
    cols[96:112, 3] = -1.0
    return np.concatenate([mats, cols, take_hi, take_lo, take_k], 1).astype(np.float32)


N_MATS = 8


def slab_plan():
    plan = ["small", "ix_q", "sa_q0", "sa_k0", "sa_v0", "sa_v1",
            "ckv_dsk", "sa_q1", "ds_q0", "sa_k1", "c_q", "ds_q1", "uq", "ukv"]
    for n in range(3):
        plan += [f"z{n}_0", f"z{n}_1"]
        for half in range(2):
            plan += [f"g{n}_{2 * half}", f"g{n}_{2 * half + 1}", f"up{n}_{half}"]
    plan += [f"out{c}_{j}" for c in range(2) for j in range(2)]
    return plan


SLABS = slab_plan()
NS = len(SLABS)
SLAB_NO = {n: i for i, n in enumerate(SLABS)}
RAW, RING = 2, 2
INDEX_UNITS = [(h, t) for h in range(HEADS) for t in range(1, ST)]
N_STICK = HEADS * ST
N_SOFT = 2 * HEADS * ST
S_RING, T_RING = 2, 2
T_LAG, AV_LAG = 3, 5
DVE_SLABS = SLABS[8:16]
PR, PTR = 4, 4
SPLIT_Z = {N_SOFT // 2 + 6: ("z0_0", 0), N_SOFT // 2 + 10: ("z0_0", 1),
           N_SOFT // 2 + 12: ("z0_1", 0), N_SOFT // 2 + 14: ("z0_1", 1)}
FILL = {1: "c_kv", 3: "sa_q2", 5: "ds_k", 7: "sa_q3", 9: "ds_q0", 10: "sa_k2", 13: "ds_q1", 16: "sa_k3",
        18: "c_q0", 21: "c_q1", 25: "ds_q2", 27: "ds_q3"}
NORMED = [FILL[i] for i in sorted(FILL) if not FILL[i].startswith("sa")]
FILL_SPLIT = {"ds_q0": 5, "sa_k1": 6, "c_q": 14, "ds_q1": 17, "uq": 21, "ukv": 27}
CQ_SPLIT = 25
SEQ = (2, 3, 0, 1)
FIRST_LOADS = 8
BIAS_OUT = 4
N_GAINS = 7


class Signal:

    def __init__(self, sem, name, known):
        self.sem, self.name, self.known = sem, name, known
        self.n, self.events = 0, {}

    def tick(self, *event, by=1):
        self.n += by
        self.events[event] = self.n
        return self.sem, by

    def at(self, *event):
        return self.sem, self.known[self.name][event] if self.name in self.known else 1


def build(nc, x, positions, norm_g, w_in, q_norm_g, kv_norm_g, w_uq, w_ukv, mla_q_g, mla_k_g,
          dsa_q_g, dsa_k_g, rel_bias, gate_b, w_branch, w_out, consts, out, bias_dram, known):
    signals = {}
    ctx = ExitStack()
    with ctx:
        def signal(name):
            signals[name] = Signal(ctx.enter_context(nc.semaphore(name)), name, known)
            return signals[name]

        arena_bytes = 207 * 1024
        arena_base = (nc.sbuf_base + 63) // 64 * 64
        ctx.enter_context(nc.sbuf_tensor("arena", [P, arena_bytes // 4], F32))
        base = arena_base
        cursor = [base]

        def place(name, shape, dt, at=None):
            size = int(np.prod(shape[1:])) * (2 if dt == BF16 else 4)
            size = (size + 31) // 32 * 32
            if at is None:
                at = cursor[0]
                cursor[0] += size
                assert cursor[0] <= base + arena_bytes, (name, cursor[0] - base)
            return nc.alloc_sbuf_tensor_at(name, shape, dt, offset=at), at + size

        def sb(name, shape, dt=F32):
            return place(name, shape, dt)[0]

        mats = sb("mats", [P, N_MATS * P + 4])
        eye, suffix, all_later, ones, per_head, first_qk, big_eye_f, causal_f = (
            mats[:, i * P:(i + 1) * P] for i in range(N_MATS))
        thr, inv_freq, phase, sign = (mats[:, N_MATS * P + i:N_MATS * P + i + 1] for i in range(4))
        big_eye = sb("big_eye", [P, P], BF16)
        causal = sb("causal", [P, P], BF16)
        take = sb("take", [P, 3 * P], F32R)
        cos_sin = sb("cos_sin", [P, S])
        k_rope = sb("k_rope", [P, S])
        k_sq = sb("k_sq", [P, S])
        gain = sb("gain", [P, N_GAINS + 3 * KT])
        gains = sb("gains", [P, DEPTH, N_GAINS + 3 * KT])
        later = sb("later", [P, 3 * P])
        stat = sb("stat", [P, 64])
        x_sb = sb("x_sb", [P, ST, D])
        h_hi = sb("h_hi", [P, KT, S], F32R)
        h_lo = sb("h_lo", [P, KT, S], F32R)
        raw = sb("raw", [P, RAW, KT * SLAB])
        w_hi = sb("w_hi", [P, RING, KT * SLAB], F32R)
        w_lo = sb("w_lo", [P, RING, KT * SLAB], F32R)
        y_at = cursor[0]
        y = sb("y", [P, 8, S])
        u_at = cursor[0]
        ds_q = sb("ds_q", [P, 4, S])
        ds_k = sb("ds_k", [P, S])
        ds_v = sb("ds_v", [P, ST, HD])
        ix_w = sb("ix_w", [P, ST, HEADS])
        score = sb("score", [P, STRIPS])
        chosen = sb("chosen", [P, STRIPS], BF16)
        sa_q_at = cursor[0]
        sa_q = sb("sa_q", [P, 4, S])
        sa_k = sb("sa_k", [P, 4, S])
        sa_v_at = cursor[0]
        sa_v = sb("sa_v", [P, ST, BW])
        tile_bytes = S * 4
        q_head = place("q_head", [P, 2, S], F32, sa_q_at)[0]
        q_rs = place("q_rs", [P, S], F32, sa_q_at + 2 * tile_bytes)[0]
        k_head = place("k_head", [P, 2, S], F32, sa_q_at + 4 * tile_bytes)[0]
        v_b = place("v_b", [P, ST, BW], F32, sa_v_at)[0]
        y_dsa = place("y_dsa", [P, 4, S], F32, sa_v_at)[0]
        lora_at = cursor[0]
        cq_hi = sb("cq_hi", [P, 2, S], F32R)
        cq_lo = sb("cq_lo", [P, 2, S], F32R)
        ckv_hi = sb("ckv_hi", [P, S], F32R)
        ckv_lo = sb("ckv_lo", [P, S], F32R)
        bias = place("bias", [P, 2, STRIPS], F32, lora_at)[0]
        norm_sq = sb("norm_sq", [P, S])
        norm_rs = sb("norm_rs", [P, S])
        norm_out = sb("norm_out", [P, S])
        cq_out = [norm_out, norm_sq]
        q_sq, k_rs = norm_sq, norm_rs
        tmp_at = cursor[0]
        soft, at = place("soft", [P, 3, S], F32, tmp_at)
        sp, at = place("sp", [P, 2, STRIPS], F32, at)
        gain_row = place("gain_row", [P, D], F32, at)[0]
        stick_a, end = place("stick_a", [P, 2, S], F32, at)
        probs, at = place("probs", [P, PR, S], F32, tmp_at)
        probs_t, at = place("probs_t", [P, PTR, S], F32, at)
        ix_q_hi, at = place("ix_q_hi", [P, 2, S], F32R, tmp_at)
        ix_q_lo, at = place("ix_q_lo", [P, 2, S], F32R, at)
        ix_k, at = place("ix_k_parts", [P, S], F32R, at)
        ix_relu, at = place("ix_relu", [P, 3, S], F32, at)
        ix_k_low, at = place("ix_k_low", [2 * IDX_DIM, S], F32R, at)
        assert at <= end, at - end
        ix_q = place("ix_q_parts", [P, HEADS, S], F32R, y_at)[0]
        cursor[0] = end
        assert cursor[0] <= base + arena_bytes, cursor[0] - base
        br_hi, at = place("br_hi", [P, 4, S], F32R, u_at)
        br_lo, at = place("br_lo", [P, 4, S], F32R, at)
        merged, at = place("merged", [P, KT, S], F32, at)
        assert at <= sa_v_at, (at, sa_v_at)
        gate, at = place("gate", [P, 4, S], F32, sa_v_at + 4 * S * 4)
        z_sig, at = place("z_sig", [P, 2, S], F32, at)
        m_lo, at = place("m_lo", [P, KT, S], F32R, at)
        assert at <= base + arena_bytes, at - base
        xn = place("xn", [P, ST, D], F32, u_at)[0]
        x_sq = place("x_sq", [P, D], F32, sa_v_at + 4 * S * 4)[0]
        m_hi = place("m_hi", [P, KT, S], F32R, y_at)[0]
        pos_i = place("pos_i", [P, S], I32, sa_q_at)[0]
        pos_f = place("pos_f", [P, S], F32, sa_q_at + 2048)[0]
        edge = place("edge", [P, P], F32, sa_q_at + 4096)[0]
        step_f = place("step_w", [P, 32], F32, sa_q_at + 10240)[0]
        prev_f = place("prev_w", [P, 32], F32, sa_q_at + 11264)[0]
        reach = place("reach", [P, 8, S], F32, y_at)[0]
        bias_out = place("bias_out", [P, BIAS_OUT, S], F32, sa_v_at + 6 * S * 4)[0]
        take_f = place("take_f", [P, 3 * P], F32, sa_q_at + 12288)[0]
        ang = place("ang", [P, S], F32, sa_q_at + 16384)[0]
        turns = place("turns", [P, S], F32, sa_q_at + 18432)[0]

        bank = [ctx.enter_context(nc.psum_tensor(f"bank{i}", [P, S], F32)) for i in range(8)]
        NORM, Y = 6, 7

        consts_in = signal("consts_in")
        pos_in = signal("pos_in")
        x_in = signal("x_in")
        setup_dve = signal("setup_dve")
        cos_done = signal("cos_done")
        reach_ready = signal("reach_ready")
        reach_pool = signal("reach_pool")
        bias_mm = signal("bias_mm")
        bias_evac = signal("bias_evac")
        bias_stored = [signal(f"bias_stored{i}") for i in range(BIAS_OUT)]
        gains_in = signal("gains_in")
        raw_in = [signal(f"raw_in{i}") for i in range(RAW)]
        raw_used = signal("raw_used")
        dve_split = signal("dve_split")
        hi_ready = signal("hi_ready")
        setup_stat = signal("setup_stat")
        x_stat = signal("x_stat")
        dve_stat = signal("dve_stat")
        x_turned = signal("x_turned")
        h_hi_done = signal("h_hi_done")
        h_lo_done = signal("h_lo_done")
        dense = signal("dense")
        act_evac = signal("act_evac")
        dve_evac = signal("dve_evac")
        pool_work = signal("pool_work")
        norm_sum = signal("norm_sum")
        ix_taken = signal("ix_taken")
        ix_parts = [signal(f"ix_parts{i}") for i in range(2)]
        ix_mm = signal("ix_mm")
        ix_relu_done = signal("ix_relu_done")
        score_sum = signal("score_sum")
        score_masked = signal("score_masked")
        topk = signal("topk")
        stick_z = signal("stick_z")
        stick_clip = signal("stick_clip")
        stick_exp = signal("stick_exp")
        stick_sp = signal("stick_sp")
        sp_masked = signal("sp_masked")
        later_ready = signal("later_ready")
        stick_sum = signal("stick_sum")
        stick_prob = signal("stick_prob")
        prob_masked = signal("prob_masked")
        pv_done = signal("pv_done")
        y_out = {br: signal(f"y_out_{br}") for br in ("stick", "mla", "dsa")}
        logits = signal("logits")
        row_max = signal("row_max")
        probs_exp = signal("probs_exp")
        row_inv = signal("row_inv")
        probs_normed = signal("probs_normed")
        probs_turned = signal("probs_turned")
        probs_t_ready = {br: signal(f"probs_t_ready_{br}") for br in ("mla", "dsa")}
        bias_in = [signal(f"bias_in{i}") for i in range(2)]
        gate_sig = signal("gate_sig")
        branch = signal("branch")
        up_done = signal("up_done")
        up_gated = signal("up_gated")
        merge = signal("merge")
        merged_hi = signal("merged_hi")
        out_mm = signal("out_mm")
        x_new = signal("x_new")
        stored = signal("stored")

        first_in = [ctx.enter_context(nc.semaphore(f"first_in{i}")) for i in range(2)]
        arrived = ctx.enter_context(nc.semaphore("arrived"))
        cleared = ctx.enter_context(nc.semaphore("cleared"))

        numbers = sorted(s.sem.num for s in signals.values())
        assert numbers == list(range(numbers[0], numbers[-1] + 1))

        def clear_signals(e):
            e.sem_clear(arrived)
            e.sem_clear(range(numbers[0], numbers[-1] + 1))

        def meet(e, n):
            e.drain().then_inc(arrived, 1)
            e.wait_ge(cleared, n)

        dense_tiles = (["k_pe"] + [f"nat{s}" for s in range(ST)] + ["ix_q0", "ix_q1"]
                       + ["sa_q0", "sa_q1", "sa_k0", "sa_k1"] + [FILL[i] for i in sorted(FILL)]
                       + [f"{a}{h}" for h in range(HEADS) for a in ("qh", "kh")])
        for n in range(3):
            dense_tiles += [f"z{n}_{m}" for m in range(4)]
            for half in range(2):
                dense_tiles += [f"g{n}_{4 * half + m}" for m in range(4)]
        TILE = {t: i for i, t in enumerate(dense_tiles)}

        def dbank(tile):
            return bank[TILE[tile] % 2]

        def reader(tile):
            if tile.startswith(("sa_q", "sa_k")):
                return act_evac, tile
            if tile.startswith("g"):
                return gate_sig, tile
            if tile.startswith("z"):
                return branch, tile + "z"
            return dve_evac, tile

        def hslab(name, kt, a, b, hi=True, width=2 * P):
            t = w_hi if hi else w_lo
            return t[:, SLAB_NO[name] % RING, kt * width + a:kt * width + b]

        def br_split(e, n, m):
            yt = (y[:, 4 * n + m, :] if n < 2 else y_dsa[:, m, :])
            e.wait_ge(*branch.at(f"z{n}_{m}y"))
            if n and m == 0:
                e.wait_ge(*up_done.at(8 * n - 1))
            e.copy(br_hi[:, m, :], yt).then_inc(*merged_hi.tick("br", n, m))

        def lo_signal(name):
            return dve_split if name in DVE_SLABS else raw_used

        def on_pool(g):
            return g % 8 == 7

        def reach_of(e, g, ready):
            w = P * (g // 32 + 1)
            if g >= 8:
                e.wait_ge(*bias_mm.at(g - 8))
            e.tensor_scalar(reach[:, g % 8, 0:w], pos_f[:, 0:w], edge[:, g:g + 1], 1.0, ALU.is_le, ALU.mult
                            ).then_inc(*ready.tick(g))

        block = ctx.enter_context(nc.Block())

        @block.sync
        def _(sp_eng):
            e = sp_eng
            def pieces(name, l):
                slot = raw[:, SLAB_NO[name] % RAW, :]
                wl = w_in[l].rearrange("(c p) n -> p c n", p=P)

                def cols(view, a, col, n):
                    return view[:, :, a:a + n], wl[:, :, col:col + n]

                v_small = slot[:, 0:KT * SMALL].rearrange("p (c n) -> p c n", c=KT)
                v256 = slot[:, 0:KT * 2 * P].rearrange("p (c n) -> p c n", c=KT)
                v512 = slot[:, 0:4 * S].rearrange("p (c n) -> p c n", c=4)
                if name == "small":
                    return [cols(v_small, 0, COL["ix_k"], IDX_DIM), cols(v_small, IDX_DIM, COL["ix_k"], IDX_DIM),
                            cols(v_small, 64, COL["k_pe"], ROPE), cols(v_small, 96, COL["k_pe"] + 16, 16),
                            cols(v_small, 112, COL["k_pe"], 16), cols(v_small, P, COL["ds_v"], HD),
                            cols(v_small, P + HD, COL["ix_w"], HEADS)]
                if name == "ckv_dsk":
                    return [cols(v256, 0, COL["c_kv"], P), cols(v256, P, COL["ds_k"], HD),
                            cols(v256, P + HD, COL["ds_k"], HD)]
                if name == "uq":
                    v = slot[:, 0:2 * 8 * P].rearrange("p (c h n) -> p c h n", c=2, h=HEADS)
                    src = w_uq[l].rearrange("(c p) (h n) -> p c h n", p=P, h=HEADS)
                    return [r for c in range(2) for r in (
                        (v[:, c, :, 0:QK], src[:, c, :, :]),
                        (v[:, c, :, QK:QK + 16], src[:, c, :, NOPE + 16:QK]),
                        (v[:, c, :, QK + 16:P], src[:, c, :, NOPE:NOPE + 16]))]
                if name == "ukv":
                    return [(slot[:, 0:HEADS * P], w_ukv[l])]
                if name.startswith("sa_v"):
                    j = int(name[-1])
                    return [(v512, wl[:, 4 * j:4 * j + 4, COL["sa_v"]:COL["sa_v"] + BW])]
                if name.startswith("up"):
                    n, half = int(name[2]), int(name[4])
                    return [(v512, w_branch[l, n].rearrange("(c p) n -> p c n", p=P)[:, :, half * S:(half + 1) * S])]
                if name.startswith("out"):
                    c, j = int(name[3]), int(name[5])
                    return [(v512, w_out[l].rearrange("(c p) n -> p c n", p=P)[:, 4 * j:4 * j + 4, c * S:(c + 1) * S])]
                if name[0] in "zg":
                    n, j = int(name[1]), int(name[3])
                    col = COL[name[0]] + n * (BW if name[0] == "z" else D) + 2 * P * j
                elif name in ("ix_q", "c_q"):
                    col = COL[name]
                else:
                    col = COL[name[:-1]] + 2 * P * int(name[-1])
                return [cols(v256, 0, col, 2 * P)]

            def load_first(l, i):
                if i == 0:
                    e.dma_start(gain_row[:], norm_g[bass.ds(l, 1), :].to_broadcast([P, D])).then_inc(first_in[0], 16)
                for dst, src in pieces(SLABS[i], l):
                    e.dma_start(dst, src).then_inc(first_in[i], 16)

            def first_loaded(e):
                e.wait_ge(first_in[1], 16 * len(pieces(SLABS[1], 0)))
                e.sem_clear(first_in[1])
                e.sem_clear(first_in[0])

            e.dma_start(pos_i[:], positions[0:1, :].to_broadcast([P, S])).then_inc(*pos_in.tick("pos", by=16))
            e.dma_start(mats[:], consts[:, 0:N_MATS * P + 4]).then_inc(*consts_in.tick("mats", by=16))
            e.dma_start(take_f[:], consts[:, N_MATS * P + 4:]).then_inc(*consts_in.tick("take", by=16))
            e.wait_ge(*setup_dve.at("steps_zero"))
            for qq in range(4):
                e.dma_start(step_f[32 * qq:32 * qq + 32, 8 * qq:8 * qq + 8], rel_bias).then_inc(*pos_in.tick("rb", qq, by=16))
                e.dma_start(prev_f[32 * qq + 1:32 * qq + 32, 8 * qq:8 * qq + 8],
                            rel_bias[0:BUCKETS - 1, :]).then_inc(*pos_in.tick("rbp", qq, by=16))
            for s in range(ST):
                e.dma_start(x_sb[:, s, :], x[0, s * P:(s + 1) * P, :]).then_inc(*x_in.tick("x", s, by=16))
            load_first(0, 0)
            load_first(0, 1)
            for G in range(S // 16):
                w = P * (G // 8 + 1)
                e.wait_ge(*bias_evac.at(G))
                e.dma_start(bias_dram[:, 16 * G:16 * G + 16, 0:w].rearrange("h q k -> q h k"),
                            bias_out[:, G % BIAS_OUT, 0:w]).then_inc(*bias_stored[G % BIAS_OUT].tick(G, by=16))

            for i in range(BIAS_OUT):
                e.wait_ge(*bias_stored[i].at(S // 16 - BIAS_OUT + i))
            e.wait_ge(arrived, 4)
            first_loaded(e)
            clear_signals(e)
            e.sem_inc(cleared, 1)
            with e.Fori(0, DEPTH) as l:
                def load(name):
                    if SLAB_NO[name] >= 2 * RAW:
                        last = SLABS[SLAB_NO[name] - RAW]
                        e.wait_ge(*lo_signal(last).at(last))
                    elif name == SLABS[RAW + 1]:
                        e.wait_ge(*raw_used.at(SLABS[1]))
                    for dst, src in pieces(name, l):
                        e.dma_start(dst, src).then_inc(*raw_in[SLAB_NO[name] % RAW].tick(name, by=16))

                for name in SLABS[RAW:SLAB_NO["ukv"] + 1]:
                    load(name)
                load("z0_0")
                load("z0_1")
                for h in range(HEADS):
                    if h >= 2:
                        e.wait_ge(*row_max.at(N_SOFT // 2 + 4 * (h - 2) + ST - 1))
                    else:
                        e.wait_ge(*dense.at(f"kh{HEADS - 1}"))
                    for t in range(ST):
                        e.dma_start(bias[:, h % 2, OFF[t]:OFF[t] + P * (t + 1)],
                                    bias_dram[h, t * P:(t + 1) * P, 0:P * (t + 1)]
                                    ).then_inc(*bias_in[h % 2].tick(h, by=16))
                for name in SLABS[SLAB_NO["z0_1"] + 1:]:
                    load(name)
                for i in range(RAW):
                    e.wait_ge(*raw_used.at(SLABS[NS - RAW + i]))
                    load_first((l + 1) % DEPTH, i)
                for s in SEQ:
                    e.wait_ge(*x_new.at(1, s))
                    e.dma_start(out[0, s * P:(s + 1) * P, :], x_sb[:, s, :]).then_inc(*stored.tick(s, by=16))
                e.wait_ge(*stored.at(SEQ[-1]))
                e.wait_ge(arrived, 4)
                first_loaded(e)
                clear_signals(e)
                e.sem_inc(cleared, 1)

        def slab_size(name):
            if name == "small":
                return KT * SMALL
            if name == "ukv":
                return HEADS * P
            return KT * 2 * P

        def last_use(name):
            if name == "small":
                return dense, (f"nat{ST - 1}",)
            if name.startswith("sa_v"):
                return dense, ("sa_v", int(name[-1]), ST - 1)
            if name == "ckv_dsk":
                return dense, ("ds_k",)
            if name in ("ix_q", "c_q"):
                return dense, (f"{name}1",)
            if name == "uq":
                return dense, (f"qh{HEADS - 1}",)
            if name == "ukv":
                return dense, (f"kh{HEADS - 1}",)
            if name.startswith("up"):
                return up_done, (8 * int(name[2]) + 4 * int(name[4]) + 3,)
            if name.startswith("out"):
                return out_mm, (int(name[3]), int(name[5]), 1)
            if name[0] in "zg":
                return dense, (f"{name[0]}{name[1]}_{2 * int(name[3]) + 1}",)
            return dense, (f"{name[:-1]}{2 * int(name[-1]) + 1}",)

        def gated(u):
            return (merge, ("sum", u)) if u < KT else (up_gated, (u,))

        def wait_ring_slot(e, name):
            s = SLAB_NO[name]
            if s >= RING:
                sig, event = last_use(SLABS[s - RING])
                e.wait_ge(*sig.at(*event))

        def split_hi(e, name, part=None):
            s, n = SLAB_NO[name], slab_size(name)
            a, b = (0, n) if part is None else (part * n // 2, (part + 1) * n // 2)
            if not part and s >= RAW:
                e.wait_ge(*raw_in[s % RAW].at(name))
                wait_ring_slot(e, name)
            e.copy(w_hi[:, s % RING, a:b], raw[:, s % RAW, a:b]).then_inc(*hi_ready.tick(name, part or 0))

        def split_lo(e, name, part=None):
            s, n = SLAB_NO[name], slab_size(name)
            a, b = (0, n) if part is None else (part * n // 2, (part + 1) * n // 2)
            e.wait_ge(*hi_ready.at(name, part or 0))
            e.tensor_tensor(w_lo[:, s % RING, a:b], raw[:, s % RAW, a:b],
                            w_hi[:, s % RING, a:b].bitcast(F32), ALU.subtract).then_inc(*lo_signal(name).tick(name))

        soft_units = [(br, h, t) for br in ("mla", "dsa") for h in range(HEADS) for t in range(ST)]

        def s_bank(u):
            return bank[2 + u % S_RING]

        def t_bank(u):
            return bank[2 + S_RING + u % T_RING]

        def turned_copied(u):
            return probs_t_ready[soft_units[u][0]].at(u)

        def copy_parts(e, h):
            e.wait_ge(*ix_taken.at(h))
            copy = e.copy if h % 2 == 0 else e.tensor_copy
            copy(ix_q[:, h, :], bank[6 + h % 2][:, :]).then_inc(*ix_parts[h % 2].tick(h))

        @block.tensor
        def _(pe):
            pe.wait_ge(*consts_in.at("take"))
            for G in range(S // 16):
                w = P * (G // 8 + 1)
                if G >= 8:
                    pe.wait_ge(*bias_evac.at(G - 8))
                for g4 in range(4):
                    g = 4 * G + g4
                    pe.wait_ge(*(reach_pool if on_pool(g) else reach_ready).at(g))
                    mm = pe.matmul(bank[G % 8][32 * g4:32 * g4 + 32, 0:w], step_f[:, 0:32],
                                   reach[:, g % 8, 0:w], start=True, stop=True)
                    mm.then_inc(*bias_mm.tick(g))
            meet(pe, 1)
            with pe.Fori(0, DEPTH) as l:
                def use(name):
                    pe.wait_ge(*lo_signal(name).at(name))

                def tile_bank(tile):
                    i = TILE[tile]
                    if i >= 2:
                        sig, key = reader(dense_tiles[i - 2])
                        pe.wait_ge(*sig.at(key))
                    return bank[i % 2]

                def three(out_ap, terms, start=True, stop=True):
                    n = len(terms)
                    for i, (lh, ll, rh, rl) in enumerate(terms):
                        pe.matmul(out_ap, lh, rh, start=start and i == 0, stop=False)
                        pe.matmul(out_ap, lh, rl, start=False, stop=False)
                        mm = pe.matmul(out_ap, ll, rh, start=False, stop=stop and i == n - 1)
                    return mm

                def project(tile, name, a, m, width=2 * P, part=None):
                    b = bank[TILE[tile] % 2] if part == 1 else tile_bank(tile)
                    ks = range(KT) if part is None else range(part * KT // 2, (part + 1) * KT // 2)
                    return three(b[0:m, :], [(hslab(name, k, a, a + m, True, width), hslab(name, k, a, a + m, False, width),
                                              h_hi[:, k, :], h_lo[:, k, :]) for k in ks], start=not part, stop=part != 0)

                for i in range(2 * ST):
                    s, j = i % ST, i // ST
                    for k in range(4):
                        mm = pe.transpose(bank[i][:, k * P:(k + 1) * P],
                                          xn[:, s, (4 * j + k) * P:(4 * j + k + 1) * P], eye)
                    mm.then_inc(*x_turned.tick(i))
                pe.wait_ge(*h_lo_done.at(ST - 1))
                project("k_pe", "small", 0, P, SMALL, part=0)
                pe.wait_ge(*h_lo_done.at(2 * ST - 1))
                project("k_pe", "small", 0, P, SMALL, part=1).then_inc(*dense.tick("k_pe"))
                for s in range(ST):
                    b = tile_bank(f"nat{s}")
                    q = slice(s * P, (s + 1) * P)
                    mm = three(b[:, 0:SMALL - P], [(h_hi[:, k, q], h_lo[:, k, q], hslab("small", k, P, SMALL, True, SMALL),
                                                    hslab("small", k, P, SMALL, False, SMALL)) for k in range(KT)])
                    mm.then_inc(*dense.tick(f"nat{s}"))
                pe.wait_ge(*dve_evac.at("ix_k"))
                pe.matmul(bank[5][:, :], take[0:2 * IDX_DIM, 2 * P:3 * P], ix_k_low[0:2 * IDX_DIM, :], start=True, stop=True
                          ).then_inc(*ix_taken.tick("key"))
                use("ix_q")
                for j in range(2):
                    project(f"ix_q{j}", "ix_q", j * P, P).then_inc(*dense.tick(f"ix_q{j}"))

                def take_heads(hs):
                    for h in hs:
                        r = slice(IDX_DIM * (h % 4), IDX_DIM * (h % 4) + IDX_DIM)
                        if h >= 2:
                            pe.wait_ge(*ix_parts[h % 2].at(h - 2))
                        pe.matmul(bank[6 + h % 2][:, :], take[r, 0:P], ix_q_hi[r, h // 4, :], start=True, stop=False)
                        pe.matmul(bank[6 + h % 2][:, :], take[r, P:2 * P], ix_q_lo[r, h // 4, :], start=False, stop=True
                                  ).then_inc(*ix_taken.tick(h))

                def index_scores(group):
                    for u in range(4 * group, 4 * group + 4):
                        h, t = INDEX_UNITS[u]
                        if u >= 4:
                            pe.wait_ge(*ix_relu_done.at(u - 4))
                        pe.wait_ge(*ix_parts[h % 2].at(h))
                        if u == 0:
                            pe.wait_ge(*dve_evac.at("ix_k parts"))
                        pe.matmul(bank[2 + u % 4][:, 0:P * (t + 1)], ix_q[:, h, t * P:(t + 1) * P],
                                  ix_k[:, 0:P * (t + 1)], start=True, stop=True).then_inc(*ix_mm.tick(u))

                use("sa_q0")
                project("sa_q0", "sa_q0", 0, P, part=0)
                pe.wait_ge(*dve_evac.at("ix_q1"))
                take_heads((0, 1))
                project("sa_q0", "sa_q0", 0, P, part=1).then_inc(*dense.tick("sa_q0"))
                take_heads((2, 3))
                index_scores(0)
                project("sa_q1", "sa_q0", P, P, part=0)
                index_scores(1)
                take_heads((4, 5))
                project("sa_q1", "sa_q0", P, P, part=1).then_inc(*dense.tick("sa_q1"))
                index_scores(2)
                take_heads((6, 7))
                use("sa_k0")
                project("sa_k0", "sa_k0", 0, P, part=0)
                index_scores(3)
                project("sa_k0", "sa_k0", 0, P, part=1).then_inc(*dense.tick("sa_k0"))
                index_scores(4)
                project("sa_k1", "sa_k0", P, P, part=0)
                index_scores(5)
                project("sa_k1", "sa_k0", P, P, part=1).then_inc(*dense.tick("sa_k1"))
                pe.wait_ge(*ix_relu_done.at(len(INDEX_UNITS) - 1))
                for j in range(2):
                    use(f"sa_v{j}")
                    for s in range(ST):
                        q = slice(s * P, (s + 1) * P)
                        mm = three(bank[2 + s][:, :],
                                   [(h_hi[:, 4 * j + k, q], h_lo[:, 4 * j + k, q], hslab(f"sa_v{j}", k, 0, S, True, S),
                                     hslab(f"sa_v{j}", k, 0, S, False, S)) for k in range(4)],
                                   start=j == 0, stop=j == 1)
                        mm.then_inc(*dense.tick("sa_v", j, s))
                pe.wait_ge(*act_evac.at("sa_k1"))

                units = [(h, kt) for h in range(HEADS) for kt in reversed(range(ST))]
                place_of = {"c_kv": ("ckv_dsk", 0), "ds_k": ("ckv_dsk", P), "c_q0": ("c_q", 0), "c_q1": ("c_q", P)}
                for part in ("sa_q", "sa_k", "ds_q"):
                    for j in range(4):
                        place_of[f"{part}{j}"] = (f"{part}{j // 2}", (j % 2) * P)

                def norm(tile, weights, src, start=True, stop=True, k=P):
                    mm = pe.matmul(bank[NORM][:, :], weights[0:k, :], src[0:k, :], start=start, stop=stop)
                    mm.then_inc(*norm_sum.tick(tile))

                def z_of(u):
                    h, kt = units[u]
                    b, w, r = bank[2 + u % 4], S - kt * P, slice(HD * (h % 2), HD * (h % 2) + HD)
                    if kt == ST - 1 and h in (4, 6):
                        pe.wait_ge(*act_evac.at(f"sa_k{h // 2}"))
                        pe.wait_ge(*act_evac.at(f"sa_q{h // 2}"))
                    if u >= 4:
                        pe.wait_ge(*stick_prob.at(u - 4))
                    elif u < 4:
                        pe.wait_ge(*act_evac.at("sa_v", u))
                    pe.matmul(b[:, 0:w], sa_k[r, h // 2, kt * P:(kt + 1) * P], sa_q[r, h // 2, kt * P:S],
                              start=True, stop=True).then_inc(*stick_z.tick(u))

                def suffix_of(u):
                    h, kt = units[u]
                    b, w = bank[2 + u % 4], S - kt * P
                    pe.wait_ge(*sp_masked.at(u))
                    pe.matmul(b[:, 0:w], suffix, sp[:, h % 2, SOFF[kt]:SOFF[kt] + w], start=False,
                              stop=kt == ST - 1, skip_group_check=True)
                    mm = None
                    nxt = sp[:, h % 2, SOFF[kt + 1]:SOFF[kt + 1] + P]
                    mm = pe.matmul(b[:, P:2 * P], all_later, nxt, start=False, stop=kt == ST - 2, skip_group_check=True)
                    if kt < ST - 2:
                        pe.wait_ge(*later_ready.at(u))
                        src = later[:, 0:P] if kt == ST - 3 else later[:, P:3 * P]
                        mm = pe.matmul(b[:, 2 * P:w], all_later, src, start=False, stop=True, skip_group_check=True)
                    return mm

                def pv_of(u):
                    h, kt = units[u]
                    w = S - kt * P
                    pe.wait_ge(*prob_masked.at(u))
                    if kt == ST - 1 and h % 2 == 0 and h:
                        pe.wait_ge(*y_out["stick"].at(h // 2 - 1))
                    pe.matmul(bank[Y][HD * (h % 2):HD * (h % 2) + HD, kt * P:S], sa_v[:, kt, h * HD:(h + 1) * HD],
                              stick_a[:, u % 2, 0:w], start=kt == ST - 1, stop=kt == 0,
                              skip_group_check=True).then_inc(*pv_done.tick("stick", u))

                uq = [w[:, SLAB_NO["uq"] % RING, 0:16 * P].rearrange("p (c h n) -> p c h n", c=2, h=HEADS) for w in (w_hi, w_lo)]
                ukv = [w[:, SLAB_NO["ukv"] % RING, 0:HEADS * P].rearrange("p (h n) -> p h n", h=HEADS) for w in (w_hi, w_lo)]
                def values_b(s):
                    b = t_bank(s)
                    q = slice(s * P, (s + 1) * P)
                    if s >= T_RING:
                        pe.wait_ge(*act_evac.at(f"v_b{s - T_RING}"))
                    else:
                        pe.wait_ge(*stick_prob.at(N_STICK - 1))
                    three(b[:, :], [(ckv_hi[:, q], ckv_lo[:, q], ukv[0][:, :, NOPE:P], ukv[1][:, :, NOPE:P])]
                          ).then_inc(*dense.tick(f"v_b{s}"))

                def prep_q(h):
                    if h == 0:
                        use("uq")
                        pe.wait_ge(*dve_evac.at("c_q1lo"))
                    b = tile_bank(f"qh{h}")
                    three(b[:, :], [(uq[0][:, c, h, :], uq[1][:, c, h, :], cq_hi[:, c, :], cq_lo[:, c, :]) for c in range(2)]
                          ).then_inc(*dense.tick(f"qh{h}"))

                def prep_k(h):
                    if h == 0:
                        use("ukv")
                    b = tile_bank(f"kh{h}")
                    three(b[0:NOPE, :], [(ukv[0][:, h, 0:NOPE], ukv[1][:, h, 0:NOPE], ckv_hi[:, :], ckv_lo[:, :])]
                          ).then_inc(*dense.tick(f"kh{h}"))

                def norm_q(h):
                    pe.wait_ge(*act_evac.at(f"qh{h}sq"))
                    norm(f"qh{h}", first_qk, q_sq)

                def norm_k(h):
                    pe.wait_ge(*act_evac.at(f"kh{h}sq"))
                    pe.wait_ge(*act_evac.at(f"qh{h}ln"))
                    norm(f"kh{h}", ones, k_sq, k=QK)

                for i in range(len(units) + 3):
                    if i < len(units):
                        z_of(i)
                    if 0 <= i - 2 < len(units):
                        u = i - 2
                        h, kt = units[u]
                        if kt == ST - 1:
                            pe.wait_ge(*sp_masked.at(u))
                            pe.matmul(bank[2 + u % 4][:, 0:P], suffix, sp[:, h % 2, SOFF[kt]:SOFF[kt] + P], start=False,
                                      stop=True, skip_group_check=True).then_inc(*stick_sum.tick(u))
                        else:
                            suffix_of(u).then_inc(*stick_sum.tick(u))
                    if 0 <= i - 3 < len(units):
                        pv_of(i - 3)
                    if FILL.get(i - 2) in NORMED:
                        tile = FILL[i - 2]
                        k = NORMED.index(tile)
                        if k and tile != "c_q1":
                            pe.wait_ge(*act_evac.at(NORMED[k - 1] + "ln"))
                        pe.wait_ge(*act_evac.at(tile + "sq"))
                        if tile == "c_q0":
                            norm(tile, ones, norm_sq, True, False)
                        elif tile == "c_q1":
                            norm(tile, ones, norm_sq, False, True)
                        else:
                            norm(tile, ones if tile == "c_kv" else per_head, norm_sq)
                    if i in FILL:
                        tile = FILL[i]
                        name, a = place_of[tile]
                        if a == 0:
                            use(name)
                        project(tile, name, a, P).then_inc(*dense.tick(tile))
                    if i == 29:
                        prep_q(0)
                    if i == 31:
                        prep_k(0)
                    if i == 32:
                        norm_q(0)
                    if i == 33:
                        norm_k(0)
                    if i == 34:
                        prep_q(1)

                def s_of(u):
                    br, h, t = soft_units[u]
                    b, w = s_bank(u), P * (t + 1)
                    q = slice(t * P, (t + 1) * P)
                    if u >= S_RING:
                        p_br = soft_units[u - S_RING][0]
                        pe.wait_ge(*(probs_exp if p_br == "mla" else row_max).at(u - S_RING))
                    else:
                        pe.wait_ge(*stick_prob.at(N_STICK - 1))
                    if br == "mla":
                        if t == 0:
                            pe.wait_ge(*dve_evac.at(f"qh{h}rope"))
                            pe.wait_ge(*pool_work.at(f"kh{h}rope"))
                            pe.wait_ge(*dve_evac.at(f"kh{h}"))
                        pe.matmul(b[:, 0:w], q_head[:, h % 2, q], k_head[:, h % 2, 0:w], start=True, stop=True)
                        mm = pe.matmul(b[:, w - P:w], big_eye[:, :], causal[:, :], start=False, stop=True, skip_group_check=True)
                    else:
                        if h == 0 and t == 0:
                            pe.wait_ge(*dve_evac.at("ds_q3"))
                            pe.wait_ge(*topk.at("chosen", ST - 1))
                        r = slice(HD * (h % 2), HD * (h % 2) + HD)
                        pe.matmul(b[:, 0:w], ds_q[r, h // 2, q], ds_k[r, 0:w], start=True, stop=True)
                        m = causal[:, :] if t == 0 else chosen[:, OFF[t]:OFF[t] + w]
                        mm = pe.matmul(b[:, 0:w], big_eye[:, :], m, start=False, stop=True, skip_group_check=True)
                    mm.then_inc(*logits.tick(u))

                def t_of(u):
                    br, h, t = soft_units[u]
                    pe.wait_ge(*probs_normed.at(u))
                    if u >= T_RING:
                        pe.wait_ge(*turned_copied(u - T_RING))
                    else:
                        pe.wait_ge(*act_evac.at(f"v_b{ST - T_RING + u}"))
                    for k in range(t + 1):
                        mm = pe.transpose(t_bank(u)[:, k * P:(k + 1) * P], probs[:, u % PR, k * P:(k + 1) * P], eye)
                    mm.then_inc(*probs_turned.tick(u))

                def av_of(u):
                    br, h, t = soft_units[u]
                    pe.wait_ge(*turned_copied(u))
                    if t == 0 and h % 2 == 0:
                        if h:
                            pe.wait_ge(*y_out[br].at(h // 2 - 1))
                        elif br == "dsa":
                            pe.wait_ge(*y_out["mla"].at(3))
                    for k in range(t + 1):
                        v = v_b[:, k, h * HD:(h + 1) * HD] if br == "mla" else ds_v[:, k, :]
                        mm = pe.matmul(bank[Y][HD * (h % 2):HD * (h % 2) + HD, t * P:(t + 1) * P], v,
                                       probs_t[:, u % PTR, k * P:(k + 1) * P], start=k == 0, stop=k == t)
                    mm.then_inc(*pv_done.tick("soft", u))

                for i in range(N_SOFT + AV_LAG):
                    if i < N_SOFT:
                        s_of(i)
                        if i < 2:
                            if i == 0:
                                pe.wait_ge(*y_out["stick"].at(3))
                            values_b(2 * i)
                            values_b(2 * i + 1)
                        br, h, t = soft_units[i]
                        if br == "mla" and h + 1 < HEADS:
                            if t == 0:
                                prep_k(h + 1)
                            if t == 2 and h + 2 < HEADS:
                                prep_q(h + 2)
                    if 0 <= i - T_LAG < N_SOFT:
                        t_of(i - T_LAG)
                    if i < N_SOFT and br == "mla" and h + 1 < HEADS:
                        if i == 0:
                            norm_q(1)
                        if t == 1:
                            norm_k(h + 1)
                        if t == 3 and h + 2 < HEADS:
                            norm_q(h + 2)
                    if 0 <= i - AV_LAG < N_SOFT:
                        av_of(i - AV_LAG)
                ups = 0
                for n in range(3):
                    for m in range(4):
                        if m % 2 == 0:
                            use(f"z{n}_{m // 2}")
                        project(f"z{n}_{m}", f"z{n}_{m // 2}", (m % 2) * P, P).then_inc(*dense.tick(f"z{n}_{m}"))
                    for half in range(2):
                        for m in range(4):
                            if m % 2 == 0:
                                use(f"g{n}_{2 * half + m // 2}")
                            project(f"g{n}_{4 * half + m}", f"g{n}_{2 * half + m // 2}", (m % 2) * P, P
                                    ).then_inc(*dense.tick(f"g{n}_{4 * half + m}"))
                        use(f"up{n}_{half}")
                        for m in range(4):
                            if n == 0 and half == 0 and m == 0:
                                pe.wait_ge(*y_out["dsa"].at(3))
                                pe.wait_ge(*row_max.at(N_SOFT - 1))
                            if ups >= 2:
                                sig, event = gated(ups - 2)
                                pe.wait_ge(*sig.at(*event))
                            if half == 0 and m == 0:
                                pe.wait_ge(*branch.at(f"z{n}_3lo"))
                            name = f"up{n}_{half}"
                            three(bank[2 + ups % 2][:, :],
                                  [(hslab(name, k, m * P, (m + 1) * P, True, S), hslab(name, k, m * P, (m + 1) * P, False, S),
                                    br_hi[:, k, :], br_lo[:, k, :]) for k in range(4)]).then_inc(*up_done.tick(ups))
                            ups += 1
                for c in range(2):
                    for j in range(2):
                        use(f"out{c}_{j}")
                        if c == 0:
                            pe.wait_ge(*merge.at("lo", 4 * j + 3))
                        for s in SEQ:
                            if j == 0 and c == 1:
                                pe.wait_ge(*x_new.at(0, s))
                            elif j == 0 and s < 2:
                                pe.wait_ge(*up_gated.at(ups - 2 + s))
                            q = slice(s * P, (s + 1) * P)
                            name = f"out{c}_{j}"
                            three(bank[2 + s][:, :],
                                  [(m_hi[:, 4 * j + k, q], m_lo[:, 4 * j + k, q], hslab(name, k, 0, S, True, S),
                                    hslab(name, k, 0, S, False, S)) for k in range(4)],
                                  start=j == 0, stop=j == 1).then_inc(*out_mm.tick(c, j, s))
                meet(pe, l + 2)

        @block.scalar
        def _(e):
            def next_start(e, setup=False):
                stats = setup_stat if setup else x_stat
                for s in SEQ:
                    sq, ln, rs = (stat[:, i + s:i + s + 1] for i in (0, 4, 8))
                    e.wait_ge(*(x_in.at("x", ST - 1) if setup else x_new.at(1, s)))
                    e.activation(x_sq[:, :], x_sb[:, s, :], ACT.Square, accum_out=sq).then_inc(*stats.tick("sq", s))
                    e.wait_ge(*stats.at("sq", s))
                    e.activation(ln, sq, ACT.Ln, bias=stat[:, 60:61], scale=1.0 / D).then_inc(*stats.tick("ln", s))
                    e.wait_ge(*stats.at("ln", s))
                    e.activation(rs, ln, ACT.Exp, scale=-0.5).then_inc(*stats.tick("rs", s))

            def first_hi(e, setup=False):
                e.wait_ge(first_in[0], 16 * FIRST_LOADS)
                if not setup:
                    e.wait_ge(*out_mm.at(1, 0, 1))
                n = slab_size(SLABS[0])
                e.copy(w_hi[:, 0, 0:n], raw[:, 0, 0:n]).then_inc(*(setup_stat if setup else x_stat).tick("first_hi"))

            def load_gains(e):
                with nc.allow_non_contiguous_dma(reason="one gain per partition, once"):
                    def column(i, rows, src):
                        e.dma_start(gains[rows, :, i:i + 1], src.rearrange("l (p o) -> p l o", o=1)
                                    ).then_inc(*gains_in.tick(i, rows.start, by=16))
                    column(0, slice(0, P), kv_norm_g)
                    column(1, slice(0, P), q_norm_g[:, 0:P])
                    column(2, slice(0, P), q_norm_g[:, P:2 * P])
                    for i, g in ((3, mla_q_g), (4, mla_k_g)):
                        column(i, slice(0, QK), g)
                        column(i, slice(QK, QK + 16), g[:, NOPE + 16:QK])
                        column(i, slice(QK + 16, P), g[:, NOPE:NOPE + 16])
                    for i, g in ((5, dsa_q_g), (6, dsa_k_g)):
                        column(i, slice(0, HD), g)
                        column(i, slice(HD, P), g)
                    for ll in range(DEPTH):
                        for n in range(3):
                            e.dma_start(gains[:, ll, N_GAINS + 8 * n:N_GAINS + 8 + 8 * n],
                                        gate_b[ll, n].rearrange("(m p) -> p m", p=P)
                                        ).then_inc(*gains_in.tick("b", ll, n, by=16))

            e.preload_act_table_set("natural_log_exp_and_others")
            e.wait_ge(*setup_dve.at("c0"))
            for G in range(S // 16):
                w = P * (G // 8 + 1)
                if G == 4:
                    next_start(e, True)
                if G == 8:
                    first_hi(e, True)
                    load_gains(e)
                if G == S // 32 + 4:
                    e.wait_ge(*setup_dve.at("angle"))
                    e.activation(ang[64:P, :], turns[64:P, :], ACT.Sin).then_inc(*cos_done.tick("sin"))
                    e.preload_act_table_set("natural_log_exp_and_others")
                e.wait_ge(*bias_mm.at(4 * G + 3))
                if G >= BIAS_OUT:
                    e.wait_ge(*bias_stored[G % BIAS_OUT].at(G - BIAS_OUT))
                e.copy(bias_out[:, G % BIAS_OUT, 0:w], bank[G % 8][:, 0:w]).then_inc(*bias_evac.tick(G))
            meet(e, 1)
            with e.Fori(0, DEPTH) as l:
                def hi(s, part=None):
                    split_hi(e, SLABS[s], part)

                for i in range(2 * ST):
                    s, j = i % ST, i // ST
                    e.wait_ge(*x_turned.at(i))
                    e.copy(h_hi[:, 4 * j:4 * j + 4, s * P:(s + 1) * P],
                           bank[i][:, :].rearrange("p (k q) -> p k q", k=4)).then_inc(*h_hi_done.tick(i))
                hi(1)
                e.wait_ge(*dense.at("k_pe"))
                e.activation(k_sq[64:96, :], dbank("k_pe")[64:96, :], ACT.Square).then_inc(*act_evac.tick("k_pe"))
                hi(2)

                def copy_sa(part, j):
                    e.wait_ge(*dense.at(f"{part}{j}"))
                    dst = sa_q if part == "sa_q" else sa_k
                    e.copy(dst[:, j, :], dbank(f"{part}{j}")[:, :]).then_inc(*act_evac.tick(f"{part}{j}"))

                def index_relus(group):
                    for u in range(4 * group, 4 * group + 4):
                        w = P * (INDEX_UNITS[u][1] + 1)
                        e.wait_ge(*ix_mm.at(u))
                        if u >= 3:
                            e.wait_ge(*score_sum.at(u - 3))
                        e.activation(ix_relu[:, u % 3, 0:w], bank[2 + u % 4][:, 0:w], ACT.Relu, scale=IDX_DIM ** -0.5
                                     ).then_inc(*ix_relu_done.tick(u))

                copy_parts(e, 0)
                hi(3)
                copy_sa("sa_q", 0)
                copy_parts(e, 2)
                index_relus(0)
                index_relus(1)
                copy_parts(e, 4)
                copy_sa("sa_q", 1)
                index_relus(2)
                copy_parts(e, 6)
                hi(4)
                index_relus(3)
                copy_sa("sa_k", 0)
                index_relus(4)
                index_relus(5)
                copy_sa("sa_k", 1)
                hi(5)
                hi(6)
                for s in range(ST):
                    e.wait_ge(*dense.at("sa_v", 1, s))
                    e.copy(sa_v[:, s, :], bank[2 + s][:, :]).then_inc(*act_evac.tick("sa_v", s))
                hi(7)

                def rs_of(tile, n, dst, scale=1.0):
                    e.wait_ge(*norm_sum.at(tile))
                    e.activation(dst, bank[NORM][:, :], ACT.Ln, bias=stat[:, 60:61], scale=1.0 / n
                                 ).then_inc(*act_evac.tick(tile + "ln"))
                    e.wait_ge(*act_evac.at(tile + "ln"))
                    b = 0.0 if scale == 1.0 else stat[:, 61:62] if scale == HD ** -0.5 else stat[:, 62:63]
                    e.activation(dst, dst, ACT.Exp, scale=-0.5, bias=b).then_inc(*act_evac.tick(tile + "rs"))

                def sq_q(h):
                    e.wait_ge(*dense.at(f"qh{h}"))
                    e.wait_ge(*norm_sum.at(f"qh{h - 1}" if h else "ds_q3"))
                    e.activation(q_sq[:, :], dbank(f"qh{h}")[:, :], ACT.Square).then_inc(*act_evac.tick(f"qh{h}sq"))

                def sq_k(h):
                    e.wait_ge(*dense.at(f"kh{h}"))
                    if h:
                        e.wait_ge(*norm_sum.at(f"kh{h - 1}"))
                    e.activation(k_sq[0:NOPE, :], dbank(f"kh{h}")[0:NOPE, :], ACT.Square).then_inc(*act_evac.tick(f"kh{h}sq"))

                def rs_q(h):
                    if h:
                        e.wait_ge(*dve_evac.at(f"qh{h - 1}"))
                    rs_of(f"qh{h}", QK, q_rs[:, :], QK ** -0.5)

                def rs_k(h):
                    if h == 0:
                        e.wait_ge(*dve_evac.at("ds_q3"))
                    else:
                        e.wait_ge(*dve_evac.at(f"kh{h - 1}"))
                        e.wait_ge(*pool_work.at(f"kh{h - 1}rope"))
                    rs_of(f"kh{h}", QK, k_rs[:, :])

                units = [(h, kt) for h in range(HEADS) for kt in reversed(range(ST))]
                for i in range(len(units) + 5):
                    if i < len(units):
                        w = S - units[i][1] * P
                        v = soft[:, i % 3, 0:w]
                        e.wait_ge(*stick_clip.at(i))
                        e.activation(v, v, ACT.Exp).then_inc(*stick_exp.tick("exp", i))
                        e.wait_ge(*stick_exp.at("exp", i))
                        e.activation(v, v, ACT.Ln, bias=1.0).then_inc(*stick_exp.tick("ln", i))
                    if 0 <= i - 2 < len(units):
                        u = i - 2
                        w = S - units[u][1] * P
                        e.wait_ge(*stick_sum.at(u))
                        if u >= 2:
                            e.wait_ge(*pv_done.at("stick", u - 2))
                        e.activation(stick_a[:, u % 2, 0:w], bank[2 + u % 4][:, 0:w], ACT.Exp, scale=STICK_SCALE
                                     ).then_inc(*stick_prob.tick(u))
                    if i == CQ_SPLIT:
                        for c in range(2):
                            e.wait_ge(*dve_evac.at(f"c_q{c}"))
                            e.copy(cq_hi[:, c, :], cq_out[c][:, :]).then_inc(*act_evac.tick(f"cq_hi{c}"))
                    tile = FILL.get(i - 1)
                    if tile in NORMED:
                        if tile == "ds_q2":
                            e.wait_ge(*dve_evac.at("c_q1lo"))
                        e.wait_ge(*dense.at(tile))
                        k = NORMED.index(tile)
                        if k:
                            e.wait_ge(*norm_sum.at(NORMED[k - 1]))
                        e.activation(norm_sq[:, :], dbank(tile)[:, :], ACT.Square).then_inc(*act_evac.tick(tile + "sq"))
                    elif tile:
                        copy_sa(tile[:-1], int(tile[-1]))
                    if i == 31:
                        sq_q(0)
                    if i == 32:
                        rs_q(0)
                        sq_k(0)
                    if i == 33:
                        rs_k(0)
                    if i == 34:
                        sq_q(1)
                    for name, at in FILL_SPLIT.items():
                        if i - at in (1, 2):
                            split_hi(e, name, i - at - 1)
                    tile = FILL.get(i - 3)
                    if tile in NORMED and tile != "c_q0":
                        k = NORMED.index(tile)
                        if k:
                            prev = NORMED[k - 1] if NORMED[k - 1] != "c_q0" else NORMED[k - 2]
                            e.wait_ge(*dve_evac.at(prev))
                        n = {"c_kv": KV_LORA, "c_q1": Q_LORA}.get(tile, HD)
                        rs_of(tile, n, norm_rs[:, :], HD ** -0.5 if tile.startswith("ds_q") else 1.0)
                    if i == 4:
                        e.wait_ge(*dve_evac.at("c_kv"))
                        e.copy(ckv_hi[:, :], norm_out[:, :]).then_inc(*act_evac.tick("ckv_hi"))

                def exp_of(u):
                    br, h, t = soft_units[u]
                    w = P * (t + 1)
                    e.wait_ge(*row_max.at(u))
                    if br == "mla" and u >= PR:
                        e.wait_ge(*probs_turned.at(u - PR))
                    dst = probs[:, u % PR, 0:w]
                    e.activation(dst, s_bank(u)[:, 0:w] if br == "mla" else dst, ACT.Exp, bias=stat[:, 16 + u % 4:17 + u % 4],
                                 accum_out=stat[:, 20 + u % 4:21 + u % 4]).then_inc(*probs_exp.tick(u))

                for i in range(N_SOFT + AV_LAG + 1):
                    u = i - AV_LAG - 1
                    if 0 <= u and u % 8 == 7:
                        e.wait_ge(*pv_done.at("soft", u))
                        pair = u // 8
                        dst = y[:, 4 + pair, :] if pair < 4 else y_dsa[:, pair - 4, :]
                        e.copy(dst, bank[Y][:, :]).then_inc(*y_out["mla" if pair < 4 else "dsa"].tick(pair % 4))
                    if i < N_SOFT:
                        br, h, t = soft_units[i]
                        exp_of(i)
                        if i < 2:
                            for s in (2 * i, 2 * i + 1):
                                e.wait_ge(*dense.at(f"v_b{s}"))
                                e.copy(v_b[:, s, :], t_bank(s)[:, :]).then_inc(*act_evac.tick(f"v_b{s}"))
                        if br == "mla" and h + 1 < HEADS:
                            if i == 0:
                                rs_q(1)
                            if t == 0:
                                sq_k(h + 1)
                            if t == 1:
                                rs_k(h + 1)
                            if t == 2 and h + 2 < HEADS:
                                sq_q(h + 2)
                            if t == 3 and h + 2 < HEADS:
                                rs_q(h + 2)
                    u = i - T_LAG
                    if 0 <= u < N_SOFT and soft_units[u][0] == "dsa":
                        w = P * (soft_units[u][2] + 1)
                        e.wait_ge(*probs_turned.at(u))
                        e.wait_ge(*pv_done.at("soft", u - PTR))
                        e.copy(probs_t[:, u % PTR, 0:w], t_bank(u)[:, 0:w]).then_inc(*probs_t_ready["dsa"].tick(u))
                    if i in SPLIT_Z:
                        split_hi(e, *SPLIT_Z[i])
                e.preload_act_table_set("sigmoid_and_others")
                ups = 0
                nxt = SLAB_NO["z0_0"] + 2
                for n in range(3):
                    for m in range(4):
                        e.wait_ge(*dense.at(f"z{n}_{m}"))
                        if 4 * n + m >= 2:
                            pn, pm = divmod(4 * n + m - 2, 4)
                            e.wait_ge(*branch.at(f"z{pn}_{pm}z"))
                        e.activation(z_sig[:, m % 2, :], dbank(f"z{n}_{m}")[:, :], ACT.Sigmoid).then_inc(*gate_sig.tick("z", n, m))
                        if m % 2:
                            hi(nxt)
                            nxt += 1
                        if m:
                            br_split(e, n, m - 1)
                    br_split(e, n, 3)
                    for half in range(2):
                        for m in range(4):
                            mm = 4 * half + m
                            e.wait_ge(*dense.at(f"g{n}_{mm}"))
                            g = 8 * n + mm
                            if g >= 4:
                                e.wait_ge(*merge.at("sum", g - 4))
                            e.activation(gate[:, m, :], dbank(f"g{n}_{mm}")[:, :], ACT.Sigmoid,
                                         bias=gain[:, N_GAINS + g:N_GAINS + 1 + g]).then_inc(*gate_sig.tick(f"g{n}_{mm}"))
                            if m % 2:
                                hi(nxt)
                                nxt += 1
                        if n == 2:
                            for m in range(4 * half, 4 * half + 4):
                                e.wait_ge(*merge.at("sum", 16 + m))
                                e.copy(m_hi[:, m, :], merged[:, m, :]).then_inc(*merged_hi.tick(m))
                        if nxt < NS:
                            hi(nxt)
                            nxt += 1
                e.preload_act_table_set("natural_log_exp_and_others")
                while nxt < NS:
                    hi(nxt)
                    nxt += 1
                first_hi(e)
                next_start(e)
                meet(e, l + 2)

        @block.vector
        def _(e):
            def next_start(e, s, stats, mine):
                sq, r0, v, t, r = (stat[:, i + s:i + s + 1] for i in (0, 8, 24, 28, 12))
                e.wait_ge(*stats.at("rs", s))
                e.tensor_scalar(v, sq, 1.0 / D, EPS, ALU.mult, ALU.add).then_inc(*mine.tick("rms v", s))
                e.tensor_tensor(t, r0, r0, ALU.mult).then_inc(*mine.tick("rms t0", s))
                e.wait_ge(*mine.at("rms t0", s))
                e.tensor_tensor(t, t, v, ALU.mult).then_inc(*mine.tick("rms t1", s))
                e.wait_ge(*mine.at("rms t1", s))
                e.tensor_scalar(t, t, -0.5, 1.5, ALU.mult, ALU.add).then_inc(*mine.tick("rms t2", s))
                e.wait_ge(*mine.at("rms t2", s))
                e.tensor_tensor(r, r0, t, ALU.mult).then_inc(*mine.tick("rms r", s))
                e.wait_ge(*mine.at("rms r", s))
                e.wait_ge(first_in[0], 16 * FIRST_LOADS)
                e.scalar_tensor_tensor(xn[:, s, :], x_sb[:, s, :], r, gain_row[:, :], ALU.mult, ALU.mult)

            e.memset(step_f[:, :], 0.0).then_inc(*setup_dve.tick("z0"))
            e.memset(prev_f[:, :], 0.0).then_inc(*setup_dve.tick("steps_zero"))
            e.memset(stat[:, 60:61], EPS).then_inc(*setup_dve.tick("c0"))
            e.memset(stat[:, 61:62], math.log(HD ** -0.5)).then_inc(*setup_dve.tick("c1"))
            e.memset(stat[:, 62:63], math.log(QK ** -0.5)).then_inc(*setup_dve.tick("c2"))
            e.wait_ge(*consts_in.at("take"))
            e.tensor_copy(big_eye[:, :], big_eye_f).then_inc(*setup_dve.tick("be"))
            e.tensor_copy(take[:, :], take_f[:, :]).then_inc(*setup_dve.tick("take"))
            e.tensor_copy(causal[:, :], causal_f).then_inc(*setup_dve.tick("ca"))
            e.wait_ge(*pos_in.at("rbp", 3))
            e.tensor_copy(pos_f[:, :], pos_i[:, :]).then_inc(*setup_dve.tick("pos"))
            e.tensor_tensor(step_f[:, :], step_f[:, :], prev_f[:, :], ALU.subtract).then_inc(*setup_dve.tick("steps"))
            e.wait_ge(*setup_dve.at("steps"))
            for qq in range(4):
                r = slice(32 * qq, 32 * qq + 32)
                e.tensor_scalar(edge[r, :], pos_f[r, qq:S:4], thr[r, :], None, ALU.subtract).then_inc(*setup_dve.tick("edge", qq))
            hi_rows = slice(64, P)

            def angles(e):
                e.tensor_scalar(ang[hi_rows, :], pos_f[hi_rows, :], inv_freq[hi_rows, :], None, ALU.mult).then_inc(*setup_dve.tick("a0"))
                e.wait_ge(*setup_dve.at("a0"))
                tau = 2.0 * math.pi
                c1 = 6.28125
                c2 = float(np.float32(np.round((tau - c1) * 2 ** 21) / 2 ** 21))
                c3 = tau - c1 - c2
                e.tensor_scalar(stat[hi_rows, 58:59], phase[hi_rows, :], 1.0 / tau, None, ALU.mult).then_inc(*setup_dve.tick("ph"))
                e.wait_ge(*setup_dve.at("ph"))
                magic = 1.5 * 2.0 ** 23
                e.tensor_scalar(turns[hi_rows, :], ang[hi_rows, :], 1.0 / tau, stat[hi_rows, 58:59], ALU.mult, ALU.add).then_inc(*setup_dve.tick("t0"))
                e.wait_ge(*setup_dve.at("t0"))
                e.tensor_scalar(turns[hi_rows, :], turns[hi_rows, :], magic, None, ALU.add).then_inc(*setup_dve.tick("t1"))
                e.wait_ge(*setup_dve.at("t1"))
                e.tensor_scalar(turns[hi_rows, :], turns[hi_rows, :], magic, None, ALU.subtract).then_inc(*setup_dve.tick("t2"))
                e.wait_ge(*setup_dve.at("t2"))
                for i, c in enumerate((c1, c2, c3)):
                    e.scalar_tensor_tensor(ang[hi_rows, :], turns[hi_rows, :], -c, ang[hi_rows, :], ALU.mult, ALU.add
                                           ).then_inc(*setup_dve.tick("r", i))
                    e.wait_ge(*setup_dve.at("r", i))
                e.tensor_scalar(ang[hi_rows, :], ang[hi_rows, :], phase[hi_rows, :], 3.1415925, ALU.add, ALU.min).then_inc(*setup_dve.tick("r3"))
                e.wait_ge(*setup_dve.at("r3"))
                e.tensor_scalar(turns[hi_rows, :], ang[hi_rows, :], -3.1415925, None, ALU.max).then_inc(*setup_dve.tick("angle"))

            e.wait_ge(*setup_dve.at("edge", 3))
            for g in range(S // 4):
                if g == S // 8:
                    for s in SEQ:
                        next_start(e, s, setup_stat, setup_dve)
                    angles(e)
                if not on_pool(g):
                    reach_of(e, g, reach_ready)
            e.wait_ge(*cos_done.at("sin"))
            e.tensor_scalar(cos_sin[hi_rows, :], ang[hi_rows, :], sign[hi_rows, :], None, ALU.mult).then_inc(*setup_dve.tick("cs"))
            e.wait_ge(*gains_in.at("b", DEPTH - 1, 2))
            e.wait_ge(*x_in.at("x", ST - 1))

            meet(e, 1)
            with e.Fori(0, DEPTH) as l:
                e.tensor_copy(gain[:, :], gains[:, l, :]).then_inc(*dve_stat.tick("gain"))

                def h_lo_of(i):
                    s, j = i % ST, i // ST
                    e.wait_ge(*h_hi_done.at(i))
                    cols = (slice(None), slice(4 * j, 4 * j + 4), slice(s * P, (s + 1) * P))
                    e.tensor_tensor(h_lo[cols], bank[i][:, :].rearrange("p (k q) -> p k q", k=4),
                                    h_hi[cols].bitcast(F32), ALU.subtract).then_inc(*h_lo_done.tick(i))

                for i in range(2 * ST):
                    h_lo_of(i)
                e.wait_ge(*dense.at("k_pe"))
                both, low = slice(0, 2 * IDX_DIM), slice(IDX_DIM, 2 * IDX_DIM)
                e.tensor_copy(ix_k_low[both, :], dbank("k_pe")[both, :]).then_inc(*dve_evac.tick("ix_k hi"))
                e.wait_ge(*dve_evac.at("ix_k hi"))
                e.tensor_tensor(ix_k_low[low, :], dbank("k_pe")[low, :], ix_k_low[low, :].bitcast(F32), ALU.subtract
                                ).then_inc(*dve_evac.tick("ix_k"))
                e.wait_ge(*act_evac.at("k_pe"))
                b = dbank("k_pe")
                e.scalar_tensor_tensor(k_rope[64:96, :], b[64:96, :], gain[64:96, 4:5], cos_sin[64:96, :],
                                       ALU.mult, ALU.mult).then_inc(*dve_evac.tick("kr0"))
                e.scalar_tensor_tensor(norm_out[64:96, :], b[96:P, :], gain[96:P, 4:5], cos_sin[96:P, :],
                                       ALU.mult, ALU.mult).then_inc(*dve_evac.tick("k_pe"))
                e.wait_ge(*dve_evac.at("k_pe"))
                e.tensor_tensor(k_rope[96:P, :], k_rope[64:96, :], norm_out[64:96, :], ALU.add).then_inc(*dve_evac.tick("kr1"))
                e.tensor_tensor(k_rope[64:96, :], k_rope[64:96, :], norm_out[64:96, :], ALU.add).then_inc(*dve_evac.tick("kr"))
                for s in range(ST):
                    b = dbank(f"nat{s}")
                    e.wait_ge(*dense.at(f"nat{s}"))
                    e.tensor_copy(ds_v[:, s, :], b[:, 0:HD]).then_inc(*dve_evac.tick("dv", s))
                    e.tensor_scalar(ix_w[:, s, :], b[:, HD:HD + HEADS], HEADS ** -0.5, None, ALU.mult
                                    ).then_inc(*dve_evac.tick(f"nat{s}"))
                e.wait_ge(*ix_taken.at("key"))
                e.tensor_copy(ix_k[:, :], bank[5][:, :]).then_inc(*dve_evac.tick("ix_k parts"))
                for j in range(2):
                    e.wait_ge(*dense.at(f"ix_q{j}"))
                    e.tensor_copy(ix_q_hi[:, j, :], dbank(f"ix_q{j}")[:, :]).then_inc(*dve_evac.tick(f"ix_q{j}hi"))
                    e.wait_ge(*dve_evac.at(f"ix_q{j}hi"))
                    e.tensor_tensor(ix_q_lo[:, j, :], dbank(f"ix_q{j}")[:, :], ix_q_hi[:, j, :].bitcast(F32), ALU.subtract
                                    ).then_inc(*dve_evac.tick(f"ix_q{j}"))
                copy_parts(e, 1)
                copy_parts(e, 3)
                for u, (h, t) in enumerate(INDEX_UNITS):
                    if u in (8, 12):
                        copy_parts(e, 5 if u == 8 else 7)
                    w = P * (t + 1)
                    dst, src, wt = score[:, OFF[t]:OFF[t] + w], ix_relu[:, u % 3, 0:w], ix_w[:, t, h:h + 1]
                    e.wait_ge(*ix_relu_done.at(u))
                    if h == 0:
                        e.tensor_scalar(dst, src, wt, None, ALU.mult).then_inc(*score_sum.tick(u))
                    else:
                        e.wait_ge(*score_sum.at(u - 3))
                        e.scalar_tensor_tensor(dst, src, wt, dst, ALU.mult, ALU.add).then_inc(*score_sum.tick(u))
                def topk_step(n):
                    rnd, t = n // (2 * (ST - 1)), 1 + n % (ST - 1)
                    if rnd >= TOPK // 8:
                        return
                    row, best = score[:, OFF[t]:OFF[t] + P * (t + 1)], stat[:, 32 + 8 * (t - 1):40 + 8 * (t - 1)]
                    if n // (ST - 1) % 2 == 0:
                        if rnd == 0:
                            e.wait_ge(*score_masked.at(t))
                        else:
                            e.wait_ge(*topk.at("replace", rnd - 1, t))
                        e.max(best, row).then_inc(*topk.tick("max", rnd, t))
                    else:
                        e.wait_ge(*topk.at("max", rnd, t))
                        e.match_replace(row, best, row, TAKEN).then_inc(*topk.tick("replace", rnd, t))

                units = [(h, kt) for h in range(HEADS) for kt in reversed(range(ST))]
                gain_of = {"c_kv": 0, "ds_k": 6, "c_q0": 1, "c_q1": 2}

                def normed(tile, dst, rs):
                    g = gain_of.get(tile, 5)
                    e.scalar_tensor_tensor(dst, dbank(tile)[:, :], gain[:, g:g + 1], rs, ALU.mult, ALU.mult
                                           ).then_inc(*dve_evac.tick(tile))

                def head_q(h):
                    e.wait_ge(*act_evac.at(f"qh{h}rs"))
                    if h >= 2:
                        e.wait_ge(*logits.at(4 * (h - 2) + 3))
                    e.scalar_tensor_tensor(q_head[:, h % 2, :], dbank(f"qh{h}")[:, :], gain[:, 3:4], q_rs[:, :],
                                           ALU.mult, ALU.mult).then_inc(*dve_evac.tick(f"qh{h}"))
                    e.wait_ge(*dve_evac.at(f"qh{h}"))
                    qr = q_head[64:P, h % 2, :]
                    e.tensor_tensor(qr, qr, cos_sin[64:P, :], ALU.mult).then_inc(*dve_evac.tick(f"qh{h}rope"))

                def head_k(h):
                    e.wait_ge(*act_evac.at(f"kh{h}rs"))
                    if h >= 2:
                        e.wait_ge(*logits.at(4 * (h - 2) + 3))
                    e.scalar_tensor_tensor(k_head[0:NOPE, h % 2, :], dbank(f"kh{h}")[0:NOPE, :], gain[0:NOPE, 4:5],
                                           k_rs[0:NOPE, :], ALU.mult, ALU.mult).then_inc(*dve_evac.tick(f"kh{h}"))

                for i in range(len(units) + 5):
                    if i >= 4 and (i - 4) % 8 == 7:
                        pair = (i - 4) // 8
                        e.wait_ge(*pv_done.at("stick", 8 * pair + 7))
                        e.tensor_copy(y[:, pair, :], bank[Y][:, :]).then_inc(*y_out["stick"].tick(pair))
                    if 0 <= i - 1 < len(units):
                        u = i - 1
                        h, kt = units[u]
                        w = S - kt * P
                        e.wait_ge(*stick_exp.at("ln", u))
                        if h >= 2:
                            e.wait_ge(*stick_sum.at(4 * (h - 2) + 3))
                        e.scalar_tensor_tensor(sp[:, h % 2, SOFF[kt]:SOFF[kt] + w], bank[2 + u % 4][:, 0:w], STICK_SCALE,
                                               soft[:, u % 3, 0:w], ALU.mult, ALU.max).then_inc(*stick_sp.tick(u))
                    if i < len(units):
                        w = S - units[i][1] * P
                        e.wait_ge(*stick_z.at(i))
                        if i >= 3:
                            e.wait_ge(*stick_sp.at(i - 3))
                        e.tensor_scalar(soft[:, i % 3, 0:w], bank[2 + i % 4][:, 0:w], STICK_SCALE, CLIP, ALU.mult, ALU.min
                                        ).then_inc(*stick_clip.tick(i))
                    if i == CQ_SPLIT:
                        for c in range(2):
                            e.wait_ge(*act_evac.at(f"cq_hi{c}"))
                            e.tensor_tensor(cq_lo[:, c, :], cq_out[c][:, :], cq_hi[:, c, :].bitcast(F32), ALU.subtract
                                            ).then_inc(*dve_evac.tick(f"c_q{c}lo"))
                    for name, at in FILL_SPLIT.items():
                        if i - at in (2, 3):
                            split_lo(e, name, i - at - 2)
                    if i == 33:
                        head_q(0)
                    if i == 34:
                        head_k(0)
                    topk_step(2 * i)
                    topk_step(2 * i + 1)
                    tile = FILL.get(i - 3)
                    if tile in NORMED and tile != "c_q0":
                        e.wait_ge(*act_evac.at(tile + "rs"))
                        if tile == "c_kv":
                            normed(tile, norm_out[:, :], norm_rs[:, :])
                        elif tile == "ds_k":
                            normed(tile, ds_k[:, :], norm_rs[:, :])
                        elif tile == "c_q1":
                            normed("c_q0", cq_out[0][:, :], norm_rs[:, :])
                            normed("c_q1", cq_out[1][:, :], norm_rs[:, :])
                        else:
                            normed(tile, ds_q[:, int(tile[-1]), :], norm_rs[:, :])

                def inverse(u):
                    e.wait_ge(*probs_exp.at(u))
                    if u >= 4:
                        e.wait_ge(*probs_normed.at(u - 4))
                    e.reciprocal(stat[:, 24 + u % 4:25 + u % 4], stat[:, 20 + u % 4:21 + u % 4]).then_inc(*row_inv.tick(u))

                for i in range(N_SOFT + T_LAG):
                    if i < N_SOFT:
                        br, h, t = soft_units[i]
                        w = P * (t + 1)
                        negated = stat[:, 16 + i % 4:17 + i % 4]
                        e.wait_ge(*logits.at(i))
                        if i >= 4:
                            e.wait_ge(*probs_exp.at(i - 4))
                        if br == "mla":
                            e.tensor_reduce(negated, s_bank(i)[:, 0:w], AX_X, ALU.max, negate=True
                                            ).then_inc(*row_max.tick(i))
                        else:
                            if t == 0:
                                e.wait_ge(*bias_in[h % 2].at(h))
                            e.wait_ge(*probs_turned.at(i - PR))
                            top = stat[:, 12 + i % 4:13 + i % 4]
                            e.tensor_tensor_reduce(out=probs[:, i % PR, 0:w], in0=s_bank(i)[:, 0:w],
                                                   in1=bias[:, h % 2, OFF[t]:OFF[t] + w], scale=1.0, scalar=TAKEN,
                                                   op0=ALU.add, op1=ALU.max, accum_out=top).then_inc(*row_max.tick("max", i))
                            e.wait_ge(*row_max.at("max", i))
                            e.tensor_scalar(negated, top, -1.0, None, ALU.mult).then_inc(*row_max.tick(i))
                    if 0 <= i - 1 < N_SOFT:
                        inverse(i - 1)
                    if i < N_SOFT // 2 - ST:
                        topk_step(2 * (N_STICK + 5) + i)
                    elif i < N_SOFT // 2 - 1:
                        t = i - (N_SOFT // 2 - ST) + 1
                        r = slice(OFF[t], OFF[t] + P * (t + 1))
                        e.wait_ge(*topk.at("replace", TOPK // 8 - 1, t))
                        e.tensor_scalar(chosen[:, r], score[:, r], TAKEN, 1.0, ALU.is_equal, ALU.subtract
                                        ).then_inc(*topk.tick("chosen", t))
                    u = i - T_LAG
                    if 0 <= u < N_SOFT and soft_units[u][0] == "mla":
                        w = P * (soft_units[u][2] + 1)
                        e.wait_ge(*probs_turned.at(u))
                        if u >= PTR:
                            e.wait_ge(*pv_done.at("soft", u - PTR))
                        e.tensor_copy(probs_t[:, u % PTR, 0:w], t_bank(u)[:, 0:w]).then_inc(*probs_t_ready["mla"].tick(u))
                    if i - 1 in SPLIT_Z:
                        split_lo(e, *SPLIT_Z[i - 1])
                    if i < N_SOFT and br == "mla" and h + 1 < HEADS:
                        if t == (0 if h else 1):
                            head_q(h + 1)
                        if t == 2:
                            head_k(h + 1)
                ups = 0
                for n in range(3):
                    for m in range(4):
                        tile = f"z{n}_{m}"
                        e.wait_ge(*gate_sig.at("z", n, m))
                        zs = z_sig[:, m % 2, :]
                        yt = (y[:, 4 * n + m, :] if n < 2 else y_dsa[:, m, :])
                        e.tensor_tensor(zs, zs, dbank(tile)[:, :], ALU.mult).then_inc(*branch.tick(tile + "z"))
                        e.wait_ge(*branch.at(tile + "z"))
                        if n == 0 and m == 0:
                            e.wait_ge(*y_out["mla"].at(3))
                        if n == 2 and m == 0:
                            e.wait_ge(*y_out["dsa"].at(3))
                        e.tensor_tensor(yt, yt, zs, ALU.mult).then_inc(*branch.tick(tile + "y"))
                        e.wait_ge(*merged_hi.at("br", n, m))
                        e.tensor_tensor(br_lo[:, m, :], yt, br_hi[:, m, :].bitcast(F32), ALU.subtract
                                        ).then_inc(*branch.tick(tile + "lo"))
                    for half in range(2):
                        for m in range(4 * half, 4 * half + 4):
                            e.wait_ge(*up_done.at(ups))
                            e.wait_ge(*gate_sig.at(f"g{n}_{m}"))
                            b = bank[2 + ups % 2]
                            if n == 0:
                                e.tensor_tensor(merged[:, m, :], gate[:, m % 4, :], b[:, :], ALU.mult).then_inc(*merge.tick("sum", ups))
                            else:
                                g = gate[:, m % 4, :]
                                e.tensor_tensor(g, g, b[:, :], ALU.mult).then_inc(*up_gated.tick(ups))
                                e.wait_ge(*up_gated.at(ups))
                                e.tensor_tensor(merged[:, m, :], merged[:, m, :], g, ALU.add).then_inc(*merge.tick("sum", ups))
                            ups += 1
                        if n == 2:
                            for m in range(4 * half, 4 * half + 4):
                                e.wait_ge(*merged_hi.at(m))
                                e.tensor_tensor(m_lo[:, m, :], merged[:, m, :], m_hi[:, m, :].bitcast(F32), ALU.subtract
                                                ).then_inc(*merge.tick("lo", m))
                for c in range(2):
                    for s in SEQ:
                        e.wait_ge(*out_mm.at(c, 1, s))
                        xs = x_sb[:, s, c * S:(c + 1) * S]
                        e.tensor_tensor(xs, xs, bank[2 + s][:, :], ALU.add).then_inc(*x_new.tick(c, s))
                        if c == 1 and s != SEQ[0]:
                            next_start(e, SEQ[SEQ.index(s) - 1], x_stat, dve_stat)
                next_start(e, SEQ[-1], x_stat, dve_stat)
                meet(e, l + 2)

        @block.gpsimd
        def _(e):
            def first_lo(e, stats):
                n = slab_size(SLABS[0])
                e.wait_ge(*stats.at("first_hi"))
                e.tensor_tensor(w_lo[:, 0, 0:n], raw[:, 0, 0:n], w_hi[:, 0, 0:n].bitcast(F32), ALU.subtract)

            e.wait_ge(*setup_dve.at("edge", 3))
            for g in range(S // 4):
                if g == S // 8:
                    first_lo(e, setup_stat)
                if on_pool(g):
                    reach_of(e, g, reach_pool)
            meet(e, 1)
            with e.Fori(0, DEPTH) as l:
                def lo(s):
                    split_lo(e, SLABS[s])

                for s in range(1, 5):
                    lo(s)
                n_ix = 3 * HEADS
                for t in range(1, ST):
                    e.wait_ge(*score_sum.at(n_ix - 4 + t))
                    d = score[:, OFF[t] + P * t:OFF[t] + P * (t + 1)]
                    e.affine_select(out=d, in_=d, pattern=[[-1, P]], compare_op=ALU.is_ge, fill=MASKED, base=0,
                                    channel_multiplier=1).then_inc(*score_masked.tick(t))
                for s in range(5, 8):
                    lo(s)
                units = [(h, kt) for h in range(HEADS) for kt in reversed(range(ST))]
                for i in range(len(units) + 4):
                    if 0 <= i - 1 < len(units):
                        u = i - 1
                        h, kt = units[u]
                        d = sp[:, h % 2, SOFF[kt]:SOFF[kt] + P]
                        e.wait_ge(*stick_sp.at(u))
                        e.affine_select(out=d, in_=d, pattern=[[1, P]], compare_op=ALU.is_gt, fill=0.0, base=0,
                                        channel_multiplier=-1).then_inc(*sp_masked.tick(u))
                    if 0 <= i - 1 < len(units) and 0 < kt < ST - 1:
                        e.wait_ge(*sp_masked.at(u))
                        if h:
                            e.wait_ge(*stick_sum.at(4 * h - 1 - (kt == ST - 2)))
                        own = sp[:, h % 2, SOFF[kt]:SOFF[kt] + S - kt * P]
                        after = sp[:, h % 2, SOFF[kt + 1]:SOFF[kt + 1] + P]
                        if kt == ST - 2:
                            e.tensor_tensor(later[:, 0:P], own[:, P:2 * P], after, ALU.add).then_inc(*later_ready.tick(u + 1))
                        else:
                            e.tensor_tensor(later[:, P:2 * P], own[:, P:2 * P], after, ALU.add)
                            e.wait_ge(*later_ready.at(u))
                            e.tensor_tensor(later[:, 2 * P:3 * P], own[:, 2 * P:3 * P], later[:, 0:P], ALU.add
                                            ).then_inc(*later_ready.tick(u + 1))
                    if 0 <= i - 2 < len(units):
                        u = i - 2
                        d = stick_a[:, u % 2, 0:P]
                        e.wait_ge(*stick_prob.at(u))
                        e.affine_select(out=d, in_=d, pattern=[[1, P]], compare_op=ALU.is_gt, fill=0.0, base=0,
                                        channel_multiplier=-1).then_inc(*prob_masked.tick(u))
                    if i == 5:
                        e.wait_ge(*act_evac.at("ckv_hi"))
                        e.tensor_tensor(ckv_lo[:, :], norm_out[:, :], ckv_hi[:, :].bitcast(F32), ALU.subtract
                                        ).then_inc(*pool_work.tick("ckv_lo"))

                def rope_k(h):
                    e.wait_ge(*act_evac.at(f"kh{h}rs"))
                    if h >= 2:
                        e.wait_ge(*logits.at(4 * (h - 2) + 3))
                    e.tensor_tensor(k_head[64:P, h % 2, :], k_rope[64:P, :], k_rs[64:P, :], ALU.mult
                                    ).then_inc(*pool_work.tick(f"kh{h}rope"))

                e.wait_ge(*prob_masked.at(N_STICK - 1))
                rope_k(0)
                e.wait_ge(*pool_work.at("kh0rope"))
                for i in range(N_SOFT + 1):
                    if i:
                        u = i - 1
                        w = P * (soft_units[u][2] + 1)
                        e.wait_ge(*row_inv.at(u))
                        e.tensor_scalar(probs[:, u % PR, 0:w], probs[:, u % PR, 0:w], stat[:, 24 + u % 4:25 + u % 4], 1.0,
                                        ALU.mult, ALU.mult).then_inc(*probs_normed.tick(u))
                    if i < N_SOFT:
                        br, h, t = soft_units[i]
                        if br == "mla" and h + 1 < HEADS and t == 2:
                            e.wait_ge(*probs_normed.at(i - 1))
                            rope_k(h + 1)
                            e.wait_ge(*pool_work.at(f"kh{h + 1}rope"))
                for s in range(SLAB_NO["z0_1"] + 1, NS):
                    lo(s)
                first_lo(e, x_stat)
                meet(e, l + 2)
    return {n: s.events for n, s in signals.items()}


_INS = ["x", "positions", "norm_g", "w_in", "mla_q_norm_g", "mla_kv_norm_g", "mla_w_uq", "mla_w_ukv",
        "mla_q_g", "mla_k_g", "dsa_q_g", "dsa_k_g", "rel_bias", "gate_b", "w_branch", "w_out"]


def program(nc, arrays, known):
    args = [nc.dram_tensor(n, a.shape, mybir.dt.from_np(a.dtype), kind="ExternalInput").ap() for n, a in arrays.items()]
    out = nc.dram_tensor("out_dram", (1, S, D), F32, kind="ExternalOutput").ap()
    bias_dram = nc.dram_tensor("bias_dram", (HEADS, S, S), F32).ap()
    return build(nc, *args, out, bias_dram, known)


def kernel(**inputs):
    import concourse.bacc as bacc
    from concourse.bass_utils import run_bass_kernel_spmd

    arrays = {f"in_{n}": np.ascontiguousarray(inputs[n]) for n in _INS}
    arrays["in_consts"] = constants()
    known = program(bacc.Bacc("TRN2", target_bir_lowering=False, num_devices=1), arrays, {})
    nc = bacc.Bacc("TRN2", target_bir_lowering=False, num_devices=1)
    program(nc, arrays, known)
    r = run_bass_kernel_spmd(nc, [arrays], core_ids=[0])
    return r.results[0]["out_dram"]
```
